# Optimizing a Trainium2 kernel written in Bass

```python
import math
import jax, jax.numpy as jnp
from jax import lax
import numpy as np

D_MODEL = 1024
BATCH = 1
SEQ = 512
DEPTH = 2

N_MIXERS = 2
EPS = 1e-6

M_HEADS = 8
M_QK_DIM = D_MODEL // (2 * M_HEADS)
M_V_DIM = D_MODEL // M_HEADS
M_CHUNK = 64
GATE_CAP = 15.0
M_IN = 2 * M_HEADS * M_QK_DIM + M_HEADS * M_V_DIM + D_MODEL + 2 * M_HEADS

A_HEAD_DIM = 64
A_Q_HEADS = D_MODEL // A_HEAD_DIM
A_KV_HEADS = 2
A_GROUP = A_Q_HEADS // A_KV_HEADS
WINDOW = 128
A_BLOCK = 128
A_IN = (A_Q_HEADS + 2 * A_KV_HEADS) * A_HEAD_DIM

D_FF = int(math.ceil(8 * D_MODEL / 3 / 128)) * 128
CONV_W = 3

N_MLSTM_LAYERS = (DEPTH + 1) // 2
N_ATTN_LAYERS = DEPTH // 2

kernel_name = "hybrid_mlstm_swa_sink_convffn"

def rmsnorm(x, g):
    xf = x.astype(jnp.float32)
    y = xf * lax.rsqrt(jnp.mean(xf * xf, axis=-1, keepdims=True) + EPS)
    return (y * g.astype(jnp.float32)).astype(x.dtype)

def softcap(z, cap):
    return cap * jnp.tanh(z / cap)

def mlstm_mixer(h, w_in, gate_bias, head_norm, w_out):
    B, S, _ = h.shape
    H, dk, dv, L = M_HEADS, M_QK_DIM, M_V_DIM, M_CHUNK
    NC = S // L
    proj = h @ w_in
    splits = np.cumsum([H * dk, H * dk, H * dv, D_MODEL, H])
    q, k, v, o, ig_raw, fg_raw = jnp.split(proj, splits.tolist(), axis=-1)
    ig = softcap(ig_raw.astype(jnp.float32) + gate_bias[0].astype(jnp.float32), GATE_CAP)
    lf = jax.nn.log_sigmoid(softcap(fg_raw.astype(jnp.float32) + gate_bias[1].astype(jnp.float32), GATE_CAP))

    def to_chunks(t, d):
        return t.astype(jnp.float32).reshape(B, NC, L, H, d).transpose(1, 0, 3, 2, 4)

    def gate_chunks(t):
        return t.reshape(B, NC, L, H).transpose(1, 0, 3, 2)

    qc = to_chunks(q, dk) * (dk ** -0.5)
    kc = to_chunks(k, dk)
    vc = to_chunks(v, dv)
    igc, lfc = gate_chunks(ig), gate_chunks(lf)
    causal = jnp.tril(jnp.ones((L, L), dtype=bool))

    def body(carry, xs):
        C, n, m = carry
        qb, kb, vb, igb, lfb = xs
        b = jnp.cumsum(lfb, axis=-1)
        inter = b + m[..., None]
        dlog = b[..., :, None] - b[..., None, :] + igb[..., None, :]
        dlog = jnp.where(causal, dlog, -jnp.inf)
        m_t = jnp.maximum(inter, jnp.max(dlog, axis=-1))
        w = jnp.einsum('bhtd,bhsd->bhts', qb, kb) * jnp.exp(dlog - m_t[..., None])
        s_inter = jnp.exp(inter - m_t)
        num = jnp.einsum('bhts,bhsv->bhtv', w, vb) + s_inter[..., None] * jnp.einsum('bhtd,bhdv->bhtv', qb, C)
        den = jnp.sum(w, axis=-1) + s_inter * jnp.einsum('bhtd,bhd->bht', qb, n)
        hout = num / jnp.maximum(jnp.abs(den), jnp.exp(-m_t))[..., None]
        bL = b[..., -1]
        tail = bL[..., None] - b + igb
        m_new = jnp.maximum(bL + m, jnp.max(tail, axis=-1))
        ws = jnp.exp(tail - m_new[..., None])
        decay = jnp.exp(bL + m - m_new)
        C_new = decay[..., None, None] * C + jnp.einsum('bhs,bhsd,bhsv->bhdv', ws, kb, vb)
        n_new = decay[..., None] * n + jnp.einsum('bhs,bhsd->bhd', ws, kb)
        return (C_new, n_new, m_new), hout

    init = (jnp.zeros((B, H, dk, dv), jnp.float32),
            jnp.zeros((B, H, dk), jnp.float32),
            jnp.zeros((B, H), jnp.float32))
    _, hs = lax.scan(body, init, (qc, kc, vc, igc, lfc))
    hs = hs.transpose(1, 0, 3, 2, 4).reshape(B, S, H, dv)
    hs = hs * lax.rsqrt(jnp.mean(hs * hs, axis=-1, keepdims=True) + EPS)
    hs = hs * head_norm.astype(jnp.float32).reshape(H, dv)
    gated = jax.nn.sigmoid(o.astype(jnp.float32)) * hs.reshape(B, S, H * dv)
    return gated.astype(h.dtype) @ w_out

def swa_sink_mixer(h, w_in, b_in, sinks, w_out, b_out):
    B, S, _ = h.shape
    Hq, Hkv, G, dh, BLK = A_Q_HEADS, A_KV_HEADS, A_GROUP, A_HEAD_DIM, A_BLOCK
    NB = S // BLK
    proj = h @ w_in + b_in
    q, k, v = jnp.split(proj, [Hq * dh, (Hq + Hkv) * dh], axis=-1)
    q = q.reshape(B, NB, BLK, Hkv, G, dh) * (dh ** -0.5)
    k = k.reshape(B, NB, BLK, Hkv, dh)
    v = v.reshape(B, NB, BLK, Hkv, dh)

    def with_prev(t):
        prev = jnp.pad(t, ((0, 0), (1, 0), (0, 0), (0, 0), (0, 0)))[:, :-1]
        return jnp.concatenate([prev, t], axis=2)

    kc, vc = with_prev(k), with_prev(v)
    s = jnp.einsum('bnqhgd,bnkhd->bnhgqk', q, kc).astype(jnp.float32)
    qi = jnp.arange(BLK)[:, None]
    ku = jnp.arange(2 * BLK)[None, :]
    diff = qi - (ku - BLK)
    band = (diff >= 0) & (diff < WINDOW)
    kpos = jnp.arange(NB)[:, None, None] * BLK + ku[None] - BLK
    mask = band[None] & (kpos >= 0)
    s = jnp.where(mask[None, :, None, None], s, -jnp.inf)
    sink = sinks.astype(jnp.float32).reshape(1, 1, Hkv, G, 1, 1)
    mx = jnp.maximum(jnp.max(s, axis=-1, keepdims=True), sink)
    p = jnp.exp(s - mx)
    p = p / (jnp.sum(p, axis=-1, keepdims=True) + jnp.exp(sink - mx))
    o = jnp.einsum('bnhgqk,bnkhd->bnqhgd', p.astype(vc.dtype), vc).reshape(B, S, Hq * dh)
    return o @ w_out + b_out

def conv_ffn(h, w_up, conv_w, conv_b, w_down):
    S = h.shape[1]
    u = h @ w_up
    gate, val = jnp.split(u, 2, axis=-1)
    gp = jnp.pad(gate, ((0, 0), (CONV_W - 1, 0), (0, 0)))
    gate_c = conv_b + sum(conv_w[j] * gp[:, j:j + S] for j in range(CONV_W))
    return (jax.nn.silu(gate_c) * val) @ w_down

def setup_inputs(seed: int = 0) -> dict:
    key = jax.random.key(seed)
    ks = jax.random.split(key, 24)
    nrm = lambda k, shape, s: jax.random.normal(k, shape, jnp.float32) * s
    LM, LA = N_MLSTM_LAYERS, N_ATTN_LAYERS
    f_bias = jnp.broadcast_to(jnp.linspace(3.0, 6.0, M_HEADS), (LM, M_HEADS)) + nrm(ks[2], (LM, M_HEADS), 0.1)
    i_bias = nrm(ks[3], (LM, M_HEADS), 0.1)
    gain = lambda k: 1.0 + nrm(k, (DEPTH, D_MODEL), 0.02)
    return {
        "x": nrm(ks[0], (BATCH, SEQ, D_MODEL), 1.0),
        "m_w_in": nrm(ks[1], (LM, D_MODEL, M_IN), D_MODEL ** -0.5),
        "m_gate_bias": jnp.stack([i_bias, f_bias], axis=1),
        "m_head_norm": 1.0 + nrm(ks[4], (LM, M_HEADS * M_V_DIM), 0.02),
        "m_w_out": nrm(ks[5], (LM, M_HEADS * M_V_DIM, D_MODEL), (M_HEADS * M_V_DIM) ** -0.5),
        "a_w_in": nrm(ks[6], (LA, D_MODEL, A_IN), D_MODEL ** -0.5),
        "a_b_in": nrm(ks[7], (LA, A_IN), 0.02),
        "a_sinks": nrm(ks[8], (LA, A_Q_HEADS), 0.5),
        "a_w_out": nrm(ks[9], (LA, A_Q_HEADS * A_HEAD_DIM, D_MODEL), (A_Q_HEADS * A_HEAD_DIM) ** -0.5),
        "a_b_out": nrm(ks[10], (LA, D_MODEL), 0.02),
        "norm_mix_pre": gain(ks[11]),
        "norm_mix_post": gain(ks[12]),
        "norm_ffn_pre": gain(ks[13]),
        "norm_ffn_post": gain(ks[14]),
        "f_w_up": nrm(ks[15], (DEPTH, D_MODEL, 2 * D_FF), D_MODEL ** -0.5),
        "f_conv_w": nrm(ks[16], (DEPTH, CONV_W, D_FF), CONV_W ** -0.5),
        "f_conv_b": nrm(ks[17], (DEPTH, D_FF), 0.02),
        "f_w_down": nrm(ks[18], (DEPTH, D_FF, D_MODEL), D_FF ** -0.5),
    }

def reference(x, m_w_in, m_gate_bias, m_head_norm, m_w_out,
              a_w_in, a_b_in, a_sinks, a_w_out, a_b_out,
              norm_mix_pre, norm_mix_post, norm_ffn_pre, norm_ffn_post,
              f_w_up, f_conv_w, f_conv_b, f_w_down):
    h = x
    for i in range(DEPTH):
        z = rmsnorm(h, norm_mix_pre[i])
        if i % N_MIXERS == 0:
            j = i // N_MIXERS
            z = mlstm_mixer(z, m_w_in[j], m_gate_bias[j], m_head_norm[j], m_w_out[j])
        else:
            j = i // N_MIXERS
            z = swa_sink_mixer(z, a_w_in[j], a_b_in[j], a_sinks[j], a_w_out[j], a_b_out[j])
        h = h + rmsnorm(z, norm_mix_post[i])
        z = conv_ffn(rmsnorm(h, norm_ffn_pre[i]), f_w_up[i], f_conv_w[i], f_conv_b[i], f_w_down[i])
        h = h + rmsnorm(z, norm_ffn_post[i])
    return h


_drawn_inputs = setup_inputs


def setup_inputs(seed=0):
    import zlib

    import numpy as np

    out = dict(_drawn_inputs(seed))
    spreads = {}
    factors = {'m_head_norm': 2.68, 'a_sinks': 7.666, 'norm_ffn_post': 3.2, 'f_conv_b': 3.316}
    for name, (base, spread) in spreads.items():
        noise = np.random.default_rng([zlib.crc32(name.encode()), seed]).standard_normal(out[name].shape)
        drawn = base * np.exp(spread * noise) if base else spread * noise
        out[name] = __import__('jax').numpy.asarray(drawn.astype(out[name].dtype))
    for name, factor in factors.items():
        out[name] = (out[name] * factor).astype(out[name].dtype)
    return out
```

```python
from contextlib import ExitStack

import concourse.bass as bass
from concourse import mybir

F32 = mybir.dt.float32
F32R = mybir.dt.float32r
BF16 = mybir.dt.bfloat16
ALU = mybir.AluOpType
ACT = mybir.ActivationFunctionType
AX = mybir.AxisListType

P = 128
EPS = 1e-6
GATE_CAP = 15.0
MASKED = -1.0e30
LN_EXP_SET = "natural_log_exp_and_others"
EXP_TANH_SET = "exp_and_others"
CREDIT = 4


def trunk(nc, x, m_w_in, m_gate_bias, m_head_norm, m_w_out, a_w_in, a_b_in, a_sinks, a_w_out,
          a_b_out, norm_mix_pre, norm_mix_post, norm_ffn_pre, norm_ffn_post, f_w_up, f_conv_w,
          f_conv_b, f_w_down, out):
    S, D = x.shape[1], x.shape[2]
    NB = S // P
    KT = D // P
    FF = f_w_down.shape[1]
    FT = FF // P
    MH = m_gate_bias.shape[2]
    DK, DV = D // (2 * MH), D // MH
    DH = 64
    QH = a_sinks.shape[1]
    KVH = (a_w_in.shape[2] // DH - QH) // 2
    HALF = 512
    ROWS = 2 * MH
    NS = 2 * NB
    HG = MH // 2
    AG = 4
    ASTEPS = QH // AG
    assert NB == 4 and KT == 8 and FT == 22 and MH == 8 and DV == P and DK == 64 and KVH == 2

    QK_UNITS, V_UNITS, O_UNITS = 2 * MH * DK // P, MH * DV * D // (P * D), D // P
    TAIL = 4
    G_GATE = 0
    G_QK = 1
    G_V = G_QK + QK_UNITS
    G_O = G_V + V_UNITS
    G_MOUT = G_O + O_UNITS
    G_UP = [G_MOUT + KT, 0]
    G_DOWN = [G_UP[0] + 2 * FT, 0]
    G_AIN = G_DOWN[0] + FT
    A_UNITS = (QH + 2 * KVH) * DH // P
    G_AOUT = G_AIN + A_UNITS
    G_UP[1] = G_AOUT + KT
    G_DOWN[1] = G_UP[1] + 2 * FT
    SLOT = [7] + [n % 4 for n in range(QK_UNITS + V_UNITS + O_UNITS)]
    SLOT += [(k + 4) % 8 for k in range(KT)] + [n % 4 for n in range(2 * FT)]
    SLOT += [4 + n % 2 for n in range(FT - TAIL)] + list(range(TAIL))
    SLOT += [n % 4 for n in range(A_UNITS)]
    SLOT += [(k + 4) % 8 for k in range(KT)] + [n % 4 for n in range(2 * FT)]
    SLOT += [4 + n % 2 for n in range(FT - TAIL)] + list(range(TAIL))

    DMAS = [2 if q == G_GATE or G_AIN <= q < G_AIN + KT else 1 for q in range(len(SLOT))]

    def landed(g):
        return 16 * sum(DMAS[q] for q in range(g + 1) if SLOT[q] % 4 == SLOT[g] % 4)

    def counted(g):
        return g + 1 + CREDIT

    with ExitStack() as ctx:
        def sb(name, shape, dt=F32):
            return ctx.enter_context(nc.sbuf_tensor(name, shape, dt))

        def sem(name):
            return ctx.enter_context(nc.semaphore(name))

        ps = ctx.enter_context(nc.psum_tensor("ps", [P, 8, HALF], F32))

        raw = sb("raw", [P, 4, D])
        w_hi = sb("w_hi", [P, 8, D], F32R)
        w_lo = sb("w_lo", [P, 8, D], F32R)
        act_hi = sb("act_hi", [P, KT, S], F32R)
        act_lo = sb("act_lo", [P, KT, S], F32R)
        h = sb("h", [P, NB, D])
        g_post = sb("g_post", [P, D])
        g_pre = sb("g_pre", [P, D])
        arena = sb("arena", [P, 64 * 256 + 16])
        KB = 256

        ident = sb("ident", [P, P])
        causal = sb("causal", [P, P])
        ones = sb("ones", [P, 1])
        band = sb("band", [P, 2 * P])
        u_rows = sb("u_rows", [MH, S])
        junk = sb("junk", [P, HG, P], BF16)
        stat = sb("stat", [P, 8])
        VECS = 2 * 4 * FT + MH + A_UNITS
        vecs = sb("vecs", [P, VECS])
        taps = [vecs[:, l * 4 * FT:(l + 1) * 4 * FT].rearrange("p (j f) -> p j f", j=4) for l in range(2)]
        head_norm = vecs[:, 8 * FT:8 * FT + MH]
        a_bias = vecs[:, 8 * FT + MH:VECS]
        gate_b = sb("gate_b", [P, 2])
        hn_half = sb("hn_half", [P, MH])
        gt = sb("gt", [P, NB, 4, MH])
        dm = sb("dm", [P, NB, MH])
        s2 = sb("s2", [P, NB, MH])
        fac = sb("fac", [P, 3, NB * MH])
        dtmp = sb("dtmp", [P, 3, HG])
        decay_all = sb("decay_all", [P, MH, NB])
        decay = sb("decay", [MH, 3, NB])
        dsel = sb("dsel", [MH, MH, NB])
        sink = sb("sink", [P, QH])
        asm = sb("asm", [P, 2, 6, AG])

        v_tok = arena[:, 0:16 * KB].rearrange("p (c f) -> p c f", c=NB)
        o_sig = arena[:, 16 * KB:32 * KB].rearrange("p (k t) -> p k t", k=KT)
        rows = arena[0:MH, 16 * KB:32 * KB].rearrange("p (r t) -> p r t", r=8)
        qk_t = arena[:, 32 * KB:48 * KB].rearrange("p (k t) -> p k t", k=QK_UNITS)
        kw = arena[:, 48 * KB:56 * KB].rearrange("p (c f) -> p c f", c=NB)
        ew = arena[:, 56 * KB:60 * KB].rearrange("p (b t q) -> p b t q", b=2, t=HG)
        itmp = arena[:, 60 * KB:62 * KB].rearrange("p (t q) -> p t q", t=HG)
        zrow = arena[0:MH, 60 * KB:62 * KB]
        vec_rows = arena[:, 60 * KB:60 * KB + 3 * P].rearrange("p (r f) -> p r f", r=3)
        C = arena[:, 62 * KB:62 * KB + HG * (DV + 1)].rearrange("p (t q) -> p t q", t=HG)
        gated = arena[:, 32 * KB:36 * KB].rearrange("p (k t) -> p k t", k=KT)
        q_t = arena[:, 0:16 * KB].rearrange("p (k t) -> p k t", k=KT)
        k_t = arena[:, 16 * KB:18 * KB]
        v_t = arena[:, 18 * KB:20 * KB]
        va = arena[:, 20 * KB:22 * KB].rearrange("p (c f) -> p c f", c=NB)
        sc = arena[:, 22 * KB:30 * KB].rearrange("p (b j k) -> p b j k", b=2, j=AG)
        p_t = arena[:, 30 * KB:38 * KB].rearrange("p (b j k) -> p b j k", b=2, j=AG)
        o_tok = arena[:, 38 * KB:46 * KB].rearrange("p (b f) -> p b f", b=2)
        b_out = arena[:, 60 * KB:64 * KB]
        hid = arena[:, 0:44 * KB].rearrange("p (f t) -> p f t", f=FT)
        cv = arena[:, 44 * KB:48 * KB].rearrange("p (b t) -> p b t", b=2)
        tmp = arena[:, 48 * KB:52 * KB]
        zn = arena[:, 52 * KB:60 * KB].rearrange("p (b f) -> p b f", b=2)

        raw_in = [sem(f"raw_in{i}") for i in range(4)]
        w_hi_done, w_lo_done, w_used = sem("w_hi_done"), sem("w_lo_done"), sem("w_used")
        x_in = [sem(f"x_in{i}") for i in range(NB)]
        gain_in = sem("gain_in")
        vec_in, const_in, bout_in = sem("vec_in"), sem("const_in"), sem("bout_in")
        vec_mm, vec_done = sem("vec_mm"), sem("vec_done")
        out_done = sem("out_done")
        pool_done = sem("pool_done")
        act_chain, dve_chain = sem("act_chain"), sem("dve_chain")
        y_done, rs_post, rs_pre = sem("y_done"), sem("rs_post"), sem("rs_pre")
        yb_done, h_done = sem("yb_done"), sem("h_done")
        zn_done, zt_done, z_hi, z_lo = sem("zn_done"), sem("zt_done"), sem("z_hi"), sem("z_lo")
        cv0, cv1, cv2 = (sem(n) for n in ("cv0", "cv1", "cv2"))
        silu_done, hid_done = sem("silu_done"), sem("hid_done")
        hid_hi, hid_lo = sem("hid_hi"), sem("hid_lo")
        pj_used = sem("pj_used")
        tr_mm, gt_done, dsel_done, dec_mm, kt_mm, kw_done = (
            sem(n) for n in ("tr_mm", "gt_done", "dsel_done", "dec_mm", "kt_mm", "kw_done"))
        v_mm, v_done = sem("v_mm"), sem("v_done")
        row_ready = sem("row_ready")
        row_act = sem("row_act")
        u_mm, e_raw, e_exp, st_mm, w_done, n_mm, num_done, c_done, sq_done = (
            sem(n) for n in ("u_mm", "e_raw", "e_exp", "st_mm", "w_done", "n_mm", "num_done",
                             "c_done", "sq_done"))
        o_tanh, o_done = sem("o_tanh"), sem("o_done")
        fac_dve, fac_act = sem("fac_dve"), sem("fac_act")
        hs_done, ht_mm, gated_done, op_hi, op_lo = (
            sem(n) for n in ("hs_done", "ht_mm", "gated_done", "op_hi", "op_lo"))
        va_mm, va_done, s_mm, s_mask, mx_done, p_done, pt_mm, pt_done, o_mm2, o_tok_done = (
            sem(n) for n in ("va_mm", "va_done", "s_mm", "s_mask", "mx_done", "p_done", "pt_mm",
                             "pt_done", "o_mm2", "o_tok_done"))
        sink_e, den_done = sem("sink_e"), sem("den_done")

        def values(half, b):
            return (w_used, counted(G_V + 4 * half + 3)) if b == NB - 1 else (v_mm, 3 * half + b + 1)

        def products(n):
            last = [G_MOUT + KT, G_DOWN[0] + FT, G_AOUT + KT, G_DOWN[1] + FT][n // NB] - 1
            return (w_used, counted(last)) if n % NB == NB - 1 else (y_done, n - n // NB + 1)

        w_up = [f_w_up[l].rearrange("(k p) (u c) -> u p k c", p=P, c=P) for l in range(2)]
        w_down = [f_w_down[l].rearrange("(u p) n -> u p n", p=P) for l in range(2)]

        def unit(slot):
            return (w_hi[:, slot].rearrange("p (k c) -> p k c", k=KT),
                    w_lo[:, slot].rearrange("p (k c) -> p k c", k=KT))

        block = ctx.enter_context(nc.Block())

        @block.sync
        def _(sp):
            def load(g, src, dst=None):
                s = SLOT[g] % 4
                dst = raw[:, s] if dst is None else dst
                nc.sync.dma_start(dst, src).then_inc(raw_in[s], 16)

            def load_free(g):
                last = [q for q in range(g) if SLOT[q] % 4 == SLOT[g] % 4]
                if last:
                    sp.wait_ge(w_lo_done, counted(last[-1]))

            def gains(post, pre):
                if post is not None:
                    nc.sync.dma_start(g_post[:], post.partition_broadcast(P)).then_inc(gain_in, 16)
                if pre is not None:
                    nc.sync.dma_start(g_pre[:], pre.partition_broadcast(P)).then_inc(gain_in, 16)

            for b in range(NB):
                nc.sync.dma_start(h[:, b], x[0, b * P:(b + 1) * P]).then_inc(x_in[b], 16)
                if b == 0:
                    gains(None, norm_mix_pre[0])
                    w_k = m_w_in[0].rearrange("(k p) n -> p k n", p=P)
                    wg = raw[:, 3].rearrange("p (k c) -> p k c", k=KT)
                    GC = m_w_in.shape[2] - ROWS
                    sp.wait_ge(pool_done, 1)
                    nc.sync.dma_start(wg[:, :, 0:MH], w_k[:, :, GC:GC + MH]).then_inc(raw_in[3], 16)
                    nc.sync.dma_start(wg[:, :, 32:32 + MH],
                                      w_k[:, :, GC + MH:GC + ROWS]).then_inc(raw_in[3], 16)
                if b == 1:
                    for l in range(2):
                        nc.sync.dma_start(vec_rows[0:3 * FT, l],
                                          f_conv_w[l].rearrange("j (f p) -> (j f) p", p=P))\
                            .then_inc(vec_in, 16)
                        nc.sync.dma_start(vec_rows[3 * FT:4 * FT, l],
                                          f_conv_b[l].rearrange("(f p) -> f p", p=P)).then_inc(vec_in, 16)
                    nc.sync.dma_start(vec_rows[0:MH, 2], m_head_norm[0].rearrange("(h p) -> h p", p=P))\
                        .then_inc(vec_in, 16)
                    for j in range(KVH):
                        nc.sync.dma_start(
                            vec_rows[MH:MH + KT, 2, j * DH:(j + 1) * DH],
                            a_b_in[0, j * D // 2:(j + 1) * D // 2].rearrange("(t d) -> t d", d=DH))\
                            .then_inc(vec_in, 16)
                    nc.sync.dma_start(vec_rows[MH + KT:MH + A_UNITS, 2],
                                      a_b_in[0, QH * DH:].rearrange("(c p) -> c p", p=P))\
                        .then_inc(vec_in, 16)
                    for j in range(2):
                        nc.sync.dma_start(gate_b[32 * j:32 * j + MH, 0:1],
                                          m_gate_bias[0, j:j + 1].rearrange("a h -> h a"),
                                          allow_slow_non_contiguous=True).then_inc(const_in, 16)
                    nc.sync.dma_start(sink[:], a_sinks[0].partition_broadcast(P)).then_inc(const_in, 16)
            w_in = m_w_in[0]
            for n in range(QK_UNITS):
                load_free(G_QK + n)
                load(G_QK + n, w_k[:, :, n * P:(n + 1) * P],
                     raw[:, SLOT[G_QK + n] % 4].rearrange("p (k c) -> p k c", k=KT))
            VC = 2 * MH * DK
            for n in range(V_UNITS):
                half, kp = n // 4, n % 4
                load_free(G_V + n)
                load(G_V + n, w_k[:, 2 * kp:2 * kp + 2, VC + half * HALF:VC + (half + 1) * HALF],
                     raw[:, SLOT[G_V + n] % 4].rearrange("p (k c) -> p k c", k=2))
            OC = VC + MH * DV
            for n in range(O_UNITS):
                load_free(G_O + n)
                load(G_O + n, w_k[:, :, OC + n * P:OC + (n + 1) * P],
                     raw[:, SLOT[G_O + n] % 4].rearrange("p (k c) -> p k c", k=KT))
            sp.wait_ge(zn_done, NB)
            gains(norm_mix_post[0], norm_ffn_pre[0])
            for k in range(KT):
                load_free(G_MOUT + k)
                load(G_MOUT + k, m_w_out[0, k * P:(k + 1) * P])

            def ffn_loads(l):
                up, down = G_UP[l], G_DOWN[l]
                with sp.Fori(0, FT // 2) as i:
                    for j in range(4):
                        s = SLOT[up + j] % 4
                        sp.wait_ge(w_lo_done, i * 4 + counted(up + j - 4))
                        tile = i * 2 + (FT * (j % 2) + j // 2)
                        src = f_w_up[l].rearrange("(k p) n -> p k n", p=P)[:, :, bass.ds(tile * P, P)]
                        nc.sync.dma_start(raw[:, s].rearrange("p (k c) -> p k c", k=KT), src)\
                            .then_inc(raw_in[s], 16)
                with sp.Fori(0, (FT - TAIL) // 2) as i:
                    for j in range(2):
                        sp.wait_ge(w_lo_done, i * 2 + counted(down + j - 2))
                        nc.sync.dma_start(raw[:, j], f_w_down[l, bass.ds(i * (2 * P) + j * P, P)])\
                            .then_inc(raw_in[j], 16)
                for n in range(FT - TAIL, FT):
                    load_free(down + n)
                    load(down + n, f_w_down[l, n * P:(n + 1) * P])

            ffn_loads(0)
            sp.wait_ge(zn_done, 2 * NB)
            gains(norm_ffn_post[0], norm_mix_pre[1])
            wa = a_w_in[0].rearrange("(k p) n -> p k n", p=P)
            for n in range(A_UNITS):
                load_free(G_AIN + n)
                dst = raw[:, SLOT[G_AIN + n] % 4].rearrange("p (k c) -> p k c", k=KT)
                if n < KT:
                    s = SLOT[G_AIN + n] % 4
                    for j in range(KVH):
                        c0 = (n + 8 * j) * DH
                        nc.sync.dma_start(dst[:, :, j * DH:(j + 1) * DH], wa[:, :, c0:c0 + DH])\
                            .then_inc(raw_in[s], 16)
                else:
                    load(G_AIN + n, wa[:, :, n * P:(n + 1) * P], dst)
            sp.wait_ge(zn_done, 3 * NB)
            gains(norm_mix_post[1], norm_ffn_pre[1])
            nc.sync.dma_start(b_out, a_b_out[0].partition_broadcast(P)).then_inc(bout_in, 16)
            for k in range(KT):
                load_free(G_AOUT + k)
                load(G_AOUT + k, a_w_out[0, k * P:(k + 1) * P])
            ffn_loads(1)
            sp.wait_ge(zn_done, 4 * NB)
            gains(norm_ffn_post[1], None)
            for b in range(NB):
                sp.wait_ge(h_done, 3 * NB + b + 1)
                nc.sync.dma_start(out[0, b * P:(b + 1) * P], h[:, b]).then_inc(out_done, 16)
            sp.wait_ge(out_done, 16 * NB)

        @block.gpsimd
        def _(pool):
            nc.gpsimd.memset(raw[:, 3], 0.0).then_inc(pool_done, 1)
            nc.gpsimd.memset(ident[:], 1.0).then_inc(pool_done, 1)
            nc.gpsimd.memset(causal[:], 0.0).then_inc(pool_done, 1)
            nc.gpsimd.memset(band[:], 0.0).then_inc(pool_done, 1)
            nc.gpsimd.memset(ones[:], 1.0).then_inc(w_used, CREDIT)
            pool.wait_ge(pool_done, 4)
            nc.gpsimd.affine_select(out=ident[:], in_=ident[:], compare_op=ALU.is_equal, fill=0.0,
                                    base=0, pattern=[[-1, P]], channel_multiplier=1).then_inc(pool_done, 1)
            nc.gpsimd.affine_select(out=causal[:], in_=causal[:], compare_op=ALU.is_ge, fill=MASKED,
                                    base=0, pattern=[[1, P]], channel_multiplier=-1).then_inc(pool_done, 1)
            nc.gpsimd.affine_select(out=band[:, 0:P], in_=band[:, 0:P], compare_op=ALU.is_gt,
                                    fill=MASKED, base=0, pattern=[[1, P]],
                                    channel_multiplier=-1).then_inc(pool_done, 1)
            nc.gpsimd.affine_select(out=band[:, P:], in_=band[:, P:], compare_op=ALU.is_ge,
                                    fill=MASKED, base=0, pattern=[[-1, P]],
                                    channel_multiplier=1).then_inc(pool_done, 1)
            pool.wait_ge(vec_done, 1)
            nc.gpsimd.tensor_scalar(hn_half[:], head_norm, 0.5, None, ALU.mult).then_inc(pool_done, 1)
            pool.wait_ge(pool_done, 9)
            for n in range(O_UNITS):
                pool.wait_ge(o_tanh, n + 1)
                nc.gpsimd.tensor_scalar(o_sig[:, n], o_sig[:, n], hn_half[:, n:n + 1], hn_half[:, n:n + 1],
                                        ALU.mult, ALU.add).then_inc(o_done, 1)

        @block.scalar
        def _(act):
            chain = [0]

            def link(ins):
                chain[0] += 1
                ins.then_inc(act_chain, 1)
                act.wait_ge(act_chain, chain[0])

            def split_hi(g, ring):
                s = SLOT[g]
                act.wait_ge(raw_in[s % 4], landed(g))
                act.wait_ge(w_used, counted(g - ring))
                nc.scalar.copy(w_hi[:, s], raw[:, s % 4]).then_inc(w_hi_done, 1)

            def rsqrt_mean(ss, dst, n):
                link(nc.scalar.activation(stat[:, dst:dst + 1], stat[:, ss:ss + 1], ACT.Ln,
                                          scale=1.0 / n, bias=eps_col[:, 0:1]))
                return nc.scalar.activation(stat[:, dst:dst + 1], stat[:, dst:dst + 1], ACT.Exp,
                                            scale=-0.5)

            def norm_post(n, b, bank, biased=False):
                if biased:
                    act.wait_ge(yb_done, b + 1)
                    src = tmp
                else:
                    act.wait_ge(*products(n))
                    src = ps[:, bank:bank + 2].rearrange("p a f -> p (a f)")
                if n > 3 * NB:
                    act.wait_ge(h_done, n)
                link(nc.scalar.activation(zn[:, b % 2], src, ACT.Square, accum_out=stat[:, 0:1]))
                rsqrt_mean(0, 1, D).then_inc(rs_post, 1)

            def norm_pre(n, b):
                if n < NB:
                    act.wait_ge(x_in[b], 16)
                    if n > 0:
                        act.wait_ge(zn_done, n)
                else:
                    act.wait_ge(h_done, n - NB + 1)
                link(nc.scalar.activation(tmp, h[:, b], ACT.Square, accum_out=stat[:, 2:3]))
                rsqrt_mean(2, 3, D).then_inc(rs_pre, 1)

            def norm_hi(n, b, bank):
                act.wait_ge(zt_done, n + 1)
                nc.scalar.copy(act_hi[:, :, b * P:(b + 1) * P],
                               ps[:, bank:bank + 2].rearrange("p a (k t) -> p (a k) t", t=P))\
                    .then_inc(z_hi, 1)

            eps_col = stat[:, 4:5]
            nc.scalar.preload_act_table_set(LN_EXP_SET)
            act.wait_ge(dve_chain, 1)
            for b in range(NB):
                norm_pre(b, b)
                if b == 0:
                    act.wait_ge(raw_in[3], landed(G_GATE))
                    act.wait_ge(w_used, CREDIT)
                    nc.scalar.copy(w_hi[:, SLOT[0]], raw[:, 3]).then_inc(w_hi_done, 1)
                norm_hi(b, b, 2 * b)
            for n in range(4):
                split_hi(G_QK + n, 4)

            nc.scalar.preload_act_table_set(EXP_TANH_SET)
            act.wait_ge(w_used, counted(G_GATE))
            act.wait_ge(row_ready, 1)
            link(nc.scalar.activation(rows[:, 0], ps[0:MH, 0], ACT.Tanh, scale=1.0 / GATE_CAP,
                                      bias=gate_b[0:MH, 1:2]))
            link(nc.scalar.activation(rows[:, 1], ps[32:32 + MH, 0], ACT.Tanh, scale=1.0 / GATE_CAP,
                                      bias=gate_b[32:32 + MH, 1:2]))
            link(nc.scalar.activation(rows[:, 1], rows[:, 1], ACT.Exp, scale=-GATE_CAP))
            nc.scalar.preload_act_table_set(LN_EXP_SET)
            nc.scalar.activation(rows[:, 2], rows[:, 1], ACT.Ln, scale=1.0, bias=1.0)\
                .then_inc(row_act, 1)
            nc.scalar.preload_act_table_set(EXP_TANH_SET)
            for n in range(4, QK_UNITS):
                split_hi(G_QK + n, 4)
            act.wait_ge(row_ready, 2)
            for c in range(NB):
                cs = slice(c * P, (c + 1) * P)
                nc.scalar.activation(rows[:, 5, cs], rows[:, 4, cs], ACT.Exp,
                                     bias=u_rows[:, (c + 1) * P - 1:(c + 1) * P])
                nc.scalar.activation(rows[:, 6, cs], u_rows[:, cs], ACT.Exp,
                                     bias=decay[:, 0, c:c + 1])
            nc.scalar.activation(decay[:, 2], decay[:, 1], ACT.Exp)
            nc.scalar.activation(rows[:, 7], rows[:, 3], ACT.Exp, scale=-1.0).then_inc(row_act, 1)
            def squares(s):
                c, g = s // 2, s % 2
                act.wait_ge(num_done, s + 1)
                if s >= 1:
                    act.wait_ge(sq_done, s)
                for t in range(HG):
                    hd = 2 * t + g
                    ins = nc.scalar.activation(junk[:, t], v_tok[:, c, hd * DV:(hd + 1) * DV],
                                               ACT.Square, accum_out=s2[:, c, hd:hd + 1])
                ins.then_inc(sq_done, 1)

            for n in range(V_UNITS + 1):
                split_hi(G_V + n, 4)
            act.wait_ge(gt_done, 1)
            for s in range(NS):
                act.wait_ge(e_raw, s + 1)
                nc.scalar.activation(ew[:, s % 2], ew[:, s % 2], ACT.Exp).then_inc(e_exp, 1)
                if s + 1 < O_UNITS:
                    split_hi(G_O + s + 1, 4)
                act.wait_ge(w_used, counted(G_O + s))
                nc.scalar.activation(o_sig[:, s], ps[:, 6 + s % 2], ACT.Tanh, scale=0.5)\
                    .then_inc(o_tanh, 1)
                if s >= 1:
                    squares(s - 1)
            squares(NS - 1)
            nc.scalar.preload_act_table_set(LN_EXP_SET)
            act.wait_ge(fac_dve, 1)
            link(nc.scalar.activation(fac[:, 1], fac[:, 1], ACT.Ln, scale=1.0 / DV, bias=eps_col[:, 0:1]))
            nc.scalar.activation(fac[:, 1], fac[:, 1], ACT.Exp, scale=-0.5).then_inc(fac_act, 1)

            def split_out(g0):
                for k in range(KT):
                    if k < 4:
                        split_hi(g0 + k, 4)
                    else:
                        act.wait_ge(raw_in[SLOT[g0 + k] % 4], landed(g0 + k))
                        act.wait_ge(w_used, counted(g0 - 1))
                        nc.scalar.copy(w_hi[:, SLOT[g0 + k]], raw[:, SLOT[g0 + k] % 4])\
                            .then_inc(w_hi_done, 1)

            split_out(G_MOUT)
            for c in range(NB):
                act.wait_ge(gated_done, c + 1)
                nc.scalar.copy(act_hi[:, :, c * P:(c + 1) * P], gated).then_inc(op_hi, 1)
                if c >= 1:
                    norm_post(c - 1, c - 1, 4 + 2 * ((c - 1) % 2))
                    norm_pre(NB + c - 1, c - 1)
                    norm_hi(NB + c - 1, c - 1, 4 + 2 * ((c - 1) % 2))
            norm_post(NB - 1, NB - 1, 6)
            norm_pre(2 * NB - 1, NB - 1)
            norm_hi(2 * NB - 1, NB - 1, 6)

            def ffn(l):
                up, down = G_UP[l], G_DOWN[l]

                def hi_pair(i, t):
                    for q in range(2):
                        g = up + 2 * t + q
                        s = (2 * t + q) % 4
                        act.wait_ge(raw_in[s], i * 16 + landed(g))
                        act.wait_ge(w_used, i * 4 + counted(g - 4))
                        nc.scalar.copy(w_hi[:, s], raw[:, s]).then_inc(w_hi_done, 1)

                def conv(i, t):
                    f = i * 2 + t
                    act.wait_ge(w_used, i * 4 + counted(up + 2 * t))
                    nc.scalar.activation(cv[:, t], ps[:, 2 * t], ACT.Identity,
                                         scale=taps[l][:, 2, bass.ds(f, 1)],
                                         bias=taps[l][:, 3, bass.ds(f, 1)]).then_inc(cv0, 1)
                    act.wait_ge(cv2, i * 2 + (l * FT + t + 1))
                    nc.scalar.activation(cv[:, t], cv[:, t], ACT.Silu).then_inc(silu_done, 1)

                nc.scalar.preload_act_table(ACT.Silu)
                hi_pair(0, 0)
                if l == 0:
                    act.wait_ge(vec_done, 1)
                with act.Fori(0, FT // 2 - 1) as i:
                    hi_pair(i, 1)
                    conv(i, 0)
                    hi_pair(i, 2)
                    conv(i, 1)
                i = FT // 2 - 1
                hi_pair(i, 1)
                conv(i, 0)

                def hi_down(g, s, wait_w):
                    act.wait_ge(raw_in[s % 4], landed(g) if isinstance(wait_w, int) else wait_w[1])
                    act.wait_ge(w_used, wait_w if isinstance(wait_w, int) else wait_w[0])
                    nc.scalar.copy(w_hi[:, s], raw[:, s % 4]).then_inc(w_hi_done, 1)

                def hi_hid(n, s):
                    nc.scalar.copy(act_hi[:, s], hid[:, n]).then_inc(hid_hi, 1)

                for j in range(2):
                    hi_down(down + j, 4 + j, counted(down + j - 2))
                act.wait_ge(w_used, counted(down - 1))
                for j in range(2):
                    hi_hid(j, 4 + j)
                conv(i, 1)
                nc.scalar.preload_act_table_set(LN_EXP_SET)
                with act.Fori(0, (FT - TAIL) // 2 - 1) as i:
                    for j in range(2):
                        act.wait_ge(raw_in[j], i * 16 + landed(down + 2 + j))
                        act.wait_ge(w_used, i * 2 + counted(down + j))
                        nc.scalar.copy(w_hi[:, 4 + j], raw[:, j]).then_inc(w_hi_done, 1)
                        nc.scalar.copy(act_hi[:, 4 + j], hid[:, bass.ds(i * 2 + (2 + j), 1)]
                                       .rearrange("p a t -> p (a t)")).then_inc(hid_hi, 1)
                for n in range(FT - TAIL, FT):
                    hi_down(down + n, n - (FT - TAIL), counted(down - 1))
                    if n == FT - 1:
                        act.wait_ge(hid_done, (l + 1) * FT + 2)
                    hi_hid(n, n - (FT - TAIL))

            def ffn_norms(l):
                for b in range(NB):
                    norm_post((2 * l + 1) * NB + b, b, 2 * b)
                    if l == 0:
                        norm_pre(2 * NB + b, b)
                        norm_hi(2 * NB + b, b, 2 * b)

            ffn(0)
            ffn_norms(0)

            for n in range(A_UNITS):
                split_hi(G_AIN + n, 4)
            split_out(G_AOUT)

            def probs(s):
                b, blk = s % 2, s // ASTEPS
                lo = P if blk == 0 else 0
                act.wait_ge(mx_done, s + 1)
                for j in range(AG):
                    ins = nc.scalar.activation(sc[:, b, j, lo:], sc[:, b, j, lo:], ACT.Exp, scale=DH ** -0.5,
                                               bias=asm[:, b, 1, j:j + 1],
                                               accum_out=asm[:, b, 2, j:j + 1])
                nc.scalar.activation(asm[:, b, 3], asm[:, b, 3], ACT.Exp).then_inc(p_done, 1)

            def turned(s):
                b, blk = s % 2, s // ASTEPS
                act.wait_ge(pt_mm, s + 1)
                lo = P if blk == 0 else 0
                nc.scalar.copy(p_t[:, b, :, lo:], ps[:, 2:4].rearrange("p a (j k) -> p (a j) k", k=2 * P)
                               [:, :, lo:]).then_inc(pt_done, 1)

            def attn_norm(b):
                norm_post(2 * NB + b, b, 6, biased=True)
                norm_pre(3 * NB + b, b)
                norm_hi(3 * NB + b, b, 6)

            TOT = NB * ASTEPS
            for s in range(TOT + 1):
                if s < TOT:
                    probs(s)
                if s >= 1:
                    turned(s - 1)
                if s >= 1 and s % ASTEPS == 0:
                    c = s // ASTEPS - 1
                    act.wait_ge(ht_mm, NB + c + 1)
                    nc.scalar.copy(act_hi[:, :, c * P:(c + 1) * P],
                                   ps[:, 6:8].rearrange("p a (k t) -> p (a k) t", t=P)).then_inc(op_hi, 1)
                    if c >= 1:
                        pass
                if s >= ASTEPS + 2 and (s - 2) % ASTEPS == 0:
                    attn_norm((s - 2) // ASTEPS - 1)
            attn_norm(NB - 1)

            ffn(1)
            ffn_norms(1)

        @block.vector
        def _(dve):
            chain = [0]

            def link(ins):
                chain[0] += 1
                ins.then_inc(dve_chain, 1)
                dve.wait_ge(dve_chain, chain[0])

            def split_lo(g):
                s = SLOT[g]
                dve.wait_ge(w_hi_done, g + 1)
                nc.vector.tensor_tensor(w_lo[:, s], raw[:, s % 4], w_hi[:, s].bitcast(F32),
                                        ALU.subtract).then_inc(w_lo_done, 1)

            gains_in = [0]

            def norm_post(n, b, bank, biased=False):
                y = ps[:, bank:bank + 2].rearrange("p a f -> p (a f)")
                if biased:
                    dve.wait_ge(*products(n))
                    if b == 0:
                        dve.wait_ge(bout_in, 16)
                    nc.vector.tensor_tensor(tmp, y, b_out, ALU.add).then_inc(yb_done, 1)
                    y = tmp
                dve.wait_ge(rs_post, n + 1)
                link(nc.vector.scalar_tensor_tensor(tmp, y, stat[:, 1:2], g_post[:], ALU.mult, ALU.mult))
                nc.vector.tensor_tensor(h[:, b], h[:, b], tmp, ALU.add).then_inc(h_done, 1)

            def norm_pre(n, b):
                dve.wait_ge(rs_pre, n + 1)
                if n >= 2 and n < NB:
                    dve.wait_ge(zt_done, n - 1)
                nc.vector.scalar_tensor_tensor(zn[:, b % 2], h[:, b], stat[:, 3:4], g_pre[:],
                                               ALU.mult, ALU.mult).then_inc(zn_done, 1)

            def norm_lo(n, b, bank):
                dve.wait_ge(z_hi, n + 1)
                nc.vector.tensor_tensor(act_lo[:, :, b * P:(b + 1) * P],
                                        ps[:, bank:bank + 2].rearrange("p a (k t) -> p (a k) t", t=P),
                                        act_hi[:, :, b * P:(b + 1) * P].bitcast(F32),
                                        ALU.subtract).then_inc(z_lo, 1)

            def gains(n):
                gains_in[0] += n
                dve.wait_ge(gain_in, 16 * gains_in[0])

            link(nc.vector.memset(stat[:, 4:5], EPS))
            nc.vector.memset(C[:], 0.0).then_inc(w_lo_done, CREDIT)
            link(nc.vector.memset(decay[:, 0, 0:1], 0.0))
            nc.vector.memset(junk[:, 0, 0:2], 0.0).then_inc(hid_done, 2)
            gains(1)
            for b in range(NB):
                norm_pre(b, b)
                if b == 1:
                    dve.wait_ge(vec_mm, 1)
                    link(nc.vector.tensor_copy(vecs[:], ps[:, 7, 0:VECS]))
                    nc.vector.memset(junk[:, 0, 2:4], 0.0).then_inc(vec_done, 1)
                if b == 0:
                    split_lo(G_GATE)
                norm_lo(b, b, 2 * b)
            for n in range(4):
                split_lo(G_QK + n)
            dve.wait_ge(const_in, 16 * 3)
            link(nc.vector.memset(zrow, 0.0))
            nc.vector.tensor_scalar(gate_b[0:MH, 1:2], gate_b[0:MH, 0:1], 1.0 / GATE_CAP, None, ALU.mult)
            nc.vector.tensor_scalar(gate_b[32:32 + MH, 1:2], gate_b[32:32 + MH, 0:1], 1.0 / GATE_CAP, None,
                                    ALU.mult).then_inc(row_ready, 1)

            def copy_qk(n):
                dve.wait_ge(w_used, counted(G_QK + n))
                nc.vector.tensor_copy(qk_t[:, n], ps[:, 1 + n % 2]).then_inc(pj_used, 1)

            copy_qk(0)
            dve.wait_ge(row_act, 1)
            link(nc.vector.tensor_scalar(rows[:, 0], rows[:, 0], GATE_CAP, None, ALU.mult))
            link(nc.vector.tensor_scalar(rows[:, 1], rows[:, 2], -1.0, None, ALU.mult))
            link(nc.vector.tensor_tensor_scan(rows[:, 3], rows[:, 1], rows[:, 0], 0.0, ALU.add, ALU.max))
            for c in range(NB):
                cs = slice(c * P, (c + 1) * P)
                ins = nc.vector.tensor_tensor_scan(rows[:, 2, cs], rows[:, 1, cs], zrow[:, cs], 0.0,
                                                   ALU.add, ALU.add)
            link(ins)
            nc.vector.tensor_tensor(rows[:, 4], rows[:, 0], rows[:, 2], ALU.subtract)
            link(nc.vector.tensor_tensor(u_rows[:], rows[:, 2], rows[:, 3], ALU.subtract))
            m_c = rows[:, 3].rearrange("p (c t) -> p c t", t=P)
            u_c = u_rows[:].rearrange("p (c t) -> p c t", t=P)
            link(nc.vector.tensor_copy(decay[:, 0, 1:], m_c[:, 0:NB - 1, P - 1]))
            nc.vector.tensor_tensor(decay[:, 1], u_c[:, :, P - 1], decay[:, 0], ALU.add)\
                .then_inc(row_ready, 1)
            for n in range(1, QK_UNITS):
                if n >= 4:
                    split_lo(G_QK + n)
                copy_qk(n)
            split_lo(G_V)
            dve.wait_ge(row_act, 2)
            dve.wait_ge(pool_done, 8)
            nc.vector.tensor_tensor(dsel[:], decay[:, 2].unsqueeze(1).to_broadcast([MH, MH, NB]),
                                    ident[0:MH, 0:MH].unsqueeze(2).to_broadcast([MH, MH, NB]),
                                    ALU.mult).then_inc(dsel_done, 1)
            split_lo(G_V + 1)
            dve.wait_ge(tr_mm, 1)
            link(nc.vector.tensor_copy(gt[:].rearrange("p c q h -> p (c q h)"), ps[:, 0, 0:NB * 4 * MH]))
            dve.wait_ge(dec_mm, 1)
            link(nc.vector.tensor_copy(decay_all[:].rearrange("p h c -> p (h c)"),
                                       ps[:, 3, 0:MH * NB]))
            nc.vector.tensor_scalar(gt[:, :, 2], gt[:, :, 2], DK ** -0.5, None, ALU.mult)\
                .then_inc(gt_done, 1)
            for n in range(2, V_UNITS):
                split_lo(G_V + n)
                if n % 2 == 1 or n == 4:
                    pass
                c = n - 2
                if c < NB:
                    dve.wait_ge(kt_mm, c + 1)
                    nc.vector.tensor_tensor(
                        kw[:, c].rearrange("p (h d) -> p h d", h=MH),
                        ps[:, 1 + c % 2].rearrange("p (h d) -> p h d", h=MH),
                        gt[:, c, 1].unsqueeze(2).to_broadcast([P, MH, DK]), ALU.mult)\
                        .then_inc(kw_done, 1)
                if n == 4:
                    for b in range(NB):
                        dve.wait_ge(*values(0, b))
                        nc.vector.tensor_copy(v_tok[:, b, 0:HALF], ps[:, 4 + b]).then_inc(v_done, 1)
            dve.wait_ge(gt_done, 1)
            for b in range(NB):
                dve.wait_ge(*values(1, b))
                if b == 1:
                    split_lo(G_O)
                nc.vector.tensor_copy(v_tok[:, b, HALF:], ps[:, 4 + b]).then_inc(v_done, 1)

            def weights(s):
                c, g = s // 2, s % 2
                dve.wait_ge(u_mm, s + 1)
                for t in range(HG):
                    hd = 2 * t + g
                    ins = nc.vector.scalar_tensor_tensor(
                        ew[:, s % 2, t], ps[:, 0, t * P:(t + 1) * P], gt[:, c, 0, hd:hd + 1], causal[:],
                        ALU.add, ALU.min)
                ins.then_inc(e_raw, 1)

            def weigh(s):
                dve.wait_ge(e_exp, s + 1)
                dve.wait_ge(st_mm, s + 1)
                nc.vector.scalar_tensor_tensor(
                    ew[:, s % 2].rearrange("p t q -> p (t q)"), ps[:, 1], DK ** -0.5,
                    ew[:, s % 2].rearrange("p t q -> p (t q)"), ALU.mult, ALU.mult).then_inc(w_done, 1)

            def state(s):
                c, g = s // 2, s % 2
                if c == NB - 1:
                    return
                pr = slice(g * DK, (g + 1) * DK)
                dve.wait_ge(n_mm, s + 1)
                new = ps[pr, 4].rearrange("p (t v) -> p t v", t=HG)
                if c == 0:
                    nc.vector.tensor_copy(C[pr, :, 0:DV], new)
                    nc.vector.tensor_copy(C[pr, :, DV], ps[pr, 5, 8:8 + HG]).then_inc(c_done, 1)
                    return
                dec = decay_all[pr, g::2, c].unsqueeze(2).to_broadcast([DK, HG, DV + 1])
                link(nc.vector.tensor_tensor(C[pr], C[pr], dec, ALU.mult))
                nc.vector.tensor_tensor(C[pr, :, 0:DV], C[pr, :, 0:DV], new, ALU.add)
                nc.vector.tensor_tensor(C[pr, :, DV], C[pr, :, DV], ps[pr, 5, 8:8 + HG], ALU.add)\
                    .then_inc(c_done, 1)

            def outputs(s):
                c, g = s // 2, s % 2
                dve.wait_ge(n_mm, s + 1)
                num = v_tok[:, c].rearrange("p (t two v) -> p t two v", two=2, v=DV)[:, :, g]
                intra = ps[:, 2].rearrange("p (t v) -> p t v", t=HG)
                if c == 0:
                    link(nc.vector.tensor_copy(dtmp[:, 0], ps[:, 5, 0:HG]))
                    src = intra
                else:
                    s_inter = gt[:, c, 2, g::2]
                    nc.vector.tensor_tensor(itmp[:], ps[:, 3].rearrange("p (t v) -> p t v", t=HG),
                                            s_inter.unsqueeze(2).to_broadcast([P, HG, DV]), ALU.mult)
                    link(nc.vector.tensor_tensor(dtmp[:, 1], ps[:, 5, 4:4 + HG], s_inter, ALU.mult))
                    link(nc.vector.tensor_tensor(dtmp[:, 0], ps[:, 5, 0:HG], dtmp[:, 1], ALU.add))
                link(nc.vector.scalar_tensor_tensor(dtmp[:, 2], dtmp[:, 0], -1.0, dtmp[:, 0],
                                                    ALU.mult, ALU.max))
                nc.vector.tensor_tensor(dm[:, c, g::2], dtmp[:, 2], gt[:, c, 3, g::2], ALU.max)
                if c == 0:
                    ins = nc.vector.tensor_copy(num, intra)
                else:
                    ins = nc.vector.tensor_tensor(num, intra, itmp[:], ALU.add)
                ins.then_inc(num_done, 1)
                dve.wait_ge(num_done, s + 1)

            for s in range(NS):
                weights(s)
                if s >= 1:
                    state(s - 1)
                weigh(s)
                if s >= 1:
                    outputs(s - 1)
                if s + 1 < NS:
                    split_lo(G_O + s + 1)
            outputs(NS - 1)

            flat = fac
            dve.wait_ge(sq_done, NS)
            link(nc.vector.reciprocal(fac[:, 0], dm[:].rearrange("p c h -> p (c h)")))
            link(nc.vector.tensor_tensor(fac[:, 2], fac[:, 0], fac[:, 0], ALU.mult))
            nc.vector.tensor_tensor(fac[:, 1], fac[:, 2], s2[:].rearrange("p c h -> p (c h)"),
                                    ALU.mult).then_inc(fac_dve, 1)
            dve.wait_ge(fac_act, 1)
            link(nc.vector.tensor_tensor(fac[:, 0], fac[:, 0], fac[:, 1], ALU.mult))
            for k in range(KT):
                if k == 0:
                    def scale_heads(c):
                        hv = v_tok[:, c].rearrange("p (h v) -> p h v", h=MH)
                        f = fac[:, 0, c * MH:(c + 1) * MH].unsqueeze(2).to_broadcast([P, MH, DV])
                        nc.vector.tensor_tensor(hv, hv, f, ALU.mult).then_inc(hs_done, 1)
                    scale_heads(0)
                split_lo(G_MOUT + k)
            dve.wait_ge(o_done, O_UNITS)
            for c in range(NB):
                dve.wait_ge(ht_mm, c + 1)
                if c >= 1:
                    dve.wait_ge(op_lo, c)
                    dve.wait_ge(op_hi, c)
                nc.vector.tensor_tensor(gated, ps[:, 2 * (c % 2):2 * (c % 2) + 2]
                                        .rearrange("p a (k t) -> p (a k) t", t=P),
                                        o_sig[:, :, c * P:(c + 1) * P], ALU.mult).then_inc(gated_done, 1)
                if c + 1 < NB:
                    scale_heads(c + 1)
                dve.wait_ge(gated_done, c + 1)
                dve.wait_ge(op_hi, c + 1)
                nc.vector.tensor_tensor(act_lo[:, :, c * P:(c + 1) * P], gated,
                                        act_hi[:, :, c * P:(c + 1) * P].bitcast(F32), ALU.subtract)\
                    .then_inc(op_lo, 1)
                if c == 0:
                    gains(2)
                else:
                    norm_post(c - 1, c - 1, 4 + 2 * ((c - 1) % 2))
                    norm_pre(NB + c - 1, c - 1)
                    norm_lo(NB + c - 1, c - 1, 4 + 2 * ((c - 1) % 2))
            norm_post(NB - 1, NB - 1, 6)
            norm_pre(2 * NB - 1, NB - 1)
            norm_lo(2 * NB - 1, NB - 1, 6)

            def ffn(l):
                up, down = G_UP[l], G_DOWN[l]

                def lo_pair(i, t):
                    for q in range(2):
                        s = (2 * t + q) % 4
                        dve.wait_ge(w_hi_done, i * 4 + (up + 2 * t + q + 1))
                        nc.vector.tensor_tensor(w_lo[:, s], raw[:, s], w_hi[:, s].bitcast(F32),
                                                ALU.subtract).then_inc(w_lo_done, 1)

                def conv(i, t):
                    f = i * 2 + t
                    n = l * FT + t + 1
                    dve.wait_ge(cv0, i * 2 + n)
                    nc.vector.scalar_tensor_tensor(cv[:, t, 1:], ps[:, 2 * t, 0:S - 1],
                                                   taps[l][:, 1, bass.ds(f, 1)], cv[:, t, 1:],
                                                   ALU.mult, ALU.add).then_inc(cv1, 1)
                    dve.wait_ge(cv1, i * 2 + n)
                    nc.vector.scalar_tensor_tensor(cv[:, t, 2:], ps[:, 2 * t, 0:S - 2],
                                                   taps[l][:, 0, bass.ds(f, 1)], cv[:, t, 2:],
                                                   ALU.mult, ALU.add).then_inc(cv2, 1)
                    dve.wait_ge(silu_done, i * 2 + n)
                    dve.wait_ge(w_used, i * 4 + counted(up + 2 * t + 1))
                    nc.vector.tensor_tensor(hid[:, bass.ds(f, 1)].rearrange("p a t -> p (a t)"),
                                            ps[:, 2 * t + 1], cv[:, t], ALU.mult).then_inc(hid_done, 1)

                lo_pair(0, 0)
                with dve.Fori(0, FT // 2 - 1) as i:
                    lo_pair(i, 1)
                    conv(i, 0)
                    lo_pair(i, 2)
                    conv(i, 1)
                i = FT // 2 - 1
                lo_pair(i, 1)
                conv(i, 0)

                def lo_hid(n, s):
                    dve.wait_ge(hid_hi, l * FT + n + 1)
                    nc.vector.tensor_tensor(act_lo[:, s], hid[:, n], act_hi[:, s].bitcast(F32),
                                            ALU.subtract).then_inc(hid_lo, 1)

                for j in range(2):
                    split_lo(down + j)
                for j in range(2):
                    lo_hid(j, 4 + j)
                conv(i, 1)
                with dve.Fori(0, (FT - TAIL) // 2 - 1) as i:
                    for j in range(2):
                        dve.wait_ge(w_hi_done, i * 2 + (down + 2 + j + 1))
                        nc.vector.tensor_tensor(w_lo[:, 4 + j], raw[:, j], w_hi[:, 4 + j].bitcast(F32),
                                                ALU.subtract).then_inc(w_lo_done, 1)
                        dve.wait_ge(hid_hi, i * 2 + (l * FT + 2 + j + 1))
                        nc.vector.tensor_tensor(act_lo[:, 4 + j], hid[:, bass.ds(i * 2 + (2 + j), 1)]
                                                .rearrange("p a t -> p (a t)"),
                                                act_hi[:, 4 + j].bitcast(F32),
                                                ALU.subtract).then_inc(hid_lo, 1)
                for n in range(FT - TAIL, FT):
                    split_lo(down + n)
                    lo_hid(n, n - (FT - TAIL))

            def ffn_norms(l):
                gains(2 if l == 0 else 1)
                for b in range(NB):
                    norm_post((2 * l + 1) * NB + b, b, 2 * b)
                    if l == 0:
                        norm_pre(2 * NB + b, b)
                        norm_lo(2 * NB + b, b, 2 * b)

            ffn(0)
            ffn_norms(0)

            for n in range(A_UNITS):
                split_lo(G_AIN + n)
                if n >= 1:
                    m = n - 1
                    dve.wait_ge(w_used, counted(G_AIN + m))
                    nc.vector.tensor_scalar(q_t[:, m] if m < KT else k_t, ps[:, m % 2],
                                            a_bias[:, m:m + 1], None, ALU.add).then_inc(pj_used, 1)
            m = A_UNITS - 1
            dve.wait_ge(w_used, counted(G_AIN + m))
            nc.vector.tensor_scalar(v_t, ps[:, m % 2], a_bias[:, m:m + 1], None, ALU.add)\
                .then_inc(pj_used, 1)
            dve.wait_ge(va_mm, 1)
            nc.vector.tensor_copy(va[:].rearrange("p c f -> p (c f)"), ps[:, 2]).then_inc(va_done, 1)
            for k in range(KT):
                split_lo(G_AOUT + k)
            gains(2)

            def sink_cols(s):
                n = s % ASTEPS
                return sink[:, n * AG:(n + 1) * AG]

            def masked_max(s):
                b, blk = s % 2, s // ASTEPS
                lo = P if blk == 0 else 0
                dve.wait_ge(s_mm, s + 1)
                if s >= 2:
                    dve.wait_ge(pt_mm, s - 1)
                link(nc.vector.tensor_tensor(
                    sc[:, b, :, lo:], ps[:, 0:2].rearrange("p a (j k) -> p (a j) k", k=2 * P)[:, :, lo:],
                    band[:, lo:].unsqueeze(1).to_broadcast([P, AG, 2 * P - lo]), ALU.add))
                link(nc.vector.tensor_reduce(asm[:, b, 0], sc[:, b, :, lo:], AX.X, ALU.max))
                link(nc.vector.scalar_tensor_tensor(asm[:, b, 0], asm[:, b, 0], DH ** -0.5, sink_cols(s),
                                                    ALU.mult, ALU.max))
                nc.vector.tensor_tensor(asm[:, b, 3], sink_cols(s), asm[:, b, 0], ALU.subtract)
                nc.vector.tensor_scalar(asm[:, b, 1], asm[:, b, 0], -1.0, None, ALU.mult)\
                    .then_inc(mx_done, 1)

            def normalised(s):
                b, blk = s % 2, s // ASTEPS
                n = s % ASTEPS
                dve.wait_ge(p_done, s + 1)
                link(nc.vector.tensor_tensor(asm[:, b, 4], asm[:, b, 2], asm[:, b, 3], ALU.add))
                link(nc.vector.reciprocal(asm[:, b, 5], asm[:, b, 4]))
                dve.wait_ge(o_mm2, s + 1)
                if s % ASTEPS == 0 and blk >= 2:
                    dve.wait_ge(ht_mm, NB + blk - 1)
                o = o_tok[:, blk % 2].rearrange("p (h d) -> p h d", d=DH)[:, n * AG:(n + 1) * AG]
                ins = nc.vector.tensor_tensor(
                    o, ps[:, 4 + s % 2, 0:AG * DH].rearrange("p (j d) -> p j d", j=AG),
                    asm[:, b, 5].unsqueeze(2).to_broadcast([P, AG, DH]), ALU.mult)
                ins.then_inc(o_tok_done, 1)

            def attn_norm(b):
                norm_post(2 * NB + b, b, 6, biased=True)
                norm_pre(3 * NB + b, b)
                norm_lo(3 * NB + b, b, 6)

            TOT = NB * ASTEPS
            for s in range(TOT + 1):
                if s < TOT:
                    masked_max(s)
                if s >= 1:
                    normalised(s - 1)
                if s >= 1 and s % ASTEPS == 0:
                    c = s // ASTEPS - 1
                    dve.wait_ge(op_hi, NB + c + 1)
                    nc.vector.tensor_tensor(act_lo[:, :, c * P:(c + 1) * P],
                                            ps[:, 6:8].rearrange("p a (k t) -> p (a k) t", t=P),
                                            act_hi[:, :, c * P:(c + 1) * P].bitcast(F32), ALU.subtract)\
                        .then_inc(op_lo, 1)
                if s >= ASTEPS + 2 and (s - 2) % ASTEPS == 0:
                    attn_norm((s - 2) // ASTEPS - 1)
            attn_norm(NB - 1)

            ffn(1)
            ffn_norms(1)

        @block.tensor
        def _(pe):
            def three(dst, pairs):
                n = len(pairs)
                for i, (lh, ll, rh, rl) in enumerate(pairs):
                    nc.tensor.matmul(dst, lh, rh, start=(i == 0), stop=False)
                    nc.tensor.matmul(dst, lh, rl, start=False, stop=False)
                    last = nc.tensor.matmul(dst, ll, rh, start=False, stop=(i == n - 1))
                return last

            def project(slot, dst):
                uh, ul = unit(slot)
                return three(dst, [(uh[:, k], ul[:, k], act_hi[:, k], act_lo[:, k]) for k in range(KT)])

            def turn_norm(n, b, bank):
                pe.wait_ge(zn_done, n + 1)
                for k in range(KT):
                    ins = nc.tensor.transpose(ps[:, bank + k // 4, (k % 4) * P:(k % 4 + 1) * P],
                                              zn[:, b % 2, k * P:(k + 1) * P], ident[:])
                ins.then_inc(zt_done, 1)

            pe.wait_ge(pool_done, 8)
            for b in range(NB):
                turn_norm(b, b, 2 * b)
                if b == 0:
                    pe.wait_ge(vec_in, 16 * (6 + KVH))
                    for r, n in enumerate((4 * FT, 4 * FT, MH + A_UNITS)):
                        ins = nc.tensor.transpose(ps[:, 7, r * 4 * FT:r * 4 * FT + n], vec_rows[0:n, r],
                                                  ident[0:n, 0:n])
                    ins.then_inc(vec_mm, 1)
                if b == 2:
                    pe.wait_ge(vec_done, 1)

            pe.wait_ge(z_lo, NB)
            pe.wait_ge(w_lo_done, counted(G_GATE))
            project(SLOT[0], ps[:, 0]).then_inc(w_used, 1)

            for n in range(QK_UNITS):
                g = G_QK + n
                pe.wait_ge(w_lo_done, counted(g))
                if n >= 2:
                    pe.wait_ge(pj_used, n - 1)
                project(SLOT[g], ps[:, 1 + n % 2]).then_inc(w_used, 1)

            def v_unit(n):
                g, half, kp = G_V + n, n // 4, n % 4
                s = SLOT[g]
                pe.wait_ge(w_lo_done, counted(g))
                for b in range(NB):
                    if half == 1 and kp == 0:
                        pe.wait_ge(v_done, b + 1)
                    bs = slice(b * P, (b + 1) * P)
                    for j in range(2):
                        k = 2 * kp + j
                        wh = w_hi[:, s, j * HALF:(j + 1) * HALF]
                        wl = w_lo[:, s, j * HALF:(j + 1) * HALF]
                        nc.tensor.matmul(ps[:, 4 + b], act_hi[:, k, bs], wh, start=(k == 0), stop=False)
                        nc.tensor.matmul(ps[:, 4 + b], act_hi[:, k, bs], wl, start=False, stop=False)
                        ins = nc.tensor.matmul(ps[:, 4 + b], act_lo[:, k, bs], wh, start=False,
                                               stop=(k == KT - 1))
                    if kp == 3 and b < NB - 1:
                        ins.then_inc(v_mm, 1)
                ins.then_inc(w_used, 1)

            v_unit(0)
            pe.wait_ge(row_act, 2)
            for c in range(NB):
                for q in range(4):
                    o0 = (c * 4 + q) * MH
                    ins = nc.tensor.transpose(ps[:, 0, o0:o0 + MH], rows[:, 4 + q, c * P:(c + 1) * P],
                                              ident[0:MH, 0:MH])
            ins.then_inc(tr_mm, 1)
            pe.wait_ge(dsel_done, 1)
            nc.tensor.matmul(ps[:, 3, 0:MH * NB], ones[0:MH, 0:1].to_broadcast([MH, P]), dsel[:].rearrange("p h c -> p (h c)"),
                             start=True, stop=True).then_inc(dec_mm, 1)
            v_unit(1)
            for n in range(2, V_UNITS):
                c = n - 2
                if c < NB:
                    if c >= 2:
                        pe.wait_ge(kw_done, c - 1)
                    else:
                        pe.wait_ge(pj_used, QK_UNITS)
                    for t in range(HG):
                        ins = nc.tensor.transpose(ps[:, 1 + c % 2, t * P:(t + 1) * P],
                                                  qk_t[:, HG + t, c * P:(c + 1) * P], ident[:])
                    ins.then_inc(kt_mm, 1)
                v_unit(n)

            def decays(s):
                c, g = s // 2, s % 2
                cs = slice(c * P, (c + 1) * P)
                if s >= 1:
                    pe.wait_ge(w_done, s)
                for t in range(HG):
                    hd = 2 * t + g
                    ins = nc.tensor.matmul(ps[:, 0, t * P:(t + 1) * P],
                                           ident[0:MH, hd:hd + 1].to_broadcast([MH, P]),
                                           u_rows[:, cs], start=True, stop=True)
                ins.then_inc(u_mm, 1)
                pr = slice(g * DK, (g + 1) * DK)
                for t in range(HG):
                    ins = nc.tensor.matmul(ps[:, 1, t * P:(t + 1) * P], qk_t[pr, HG + t, cs],
                                           qk_t[pr, t, cs], start=True, stop=True)
                ins.then_inc(st_mm, 1)

            def combine(s):
                c, g = s // 2, s % 2
                cs = slice(c * P, (c + 1) * P)
                pr = slice(g * DK, (g + 1) * DK)
                if s >= 1:
                    pe.wait_ge(num_done, s)
                    k = min(s, NS - 2)
                    pe.wait_ge(c_done, k)
                if c > 0:
                    for t in range(HG):
                        nc.tensor.matmul(ps[:, 3, t * P:(t + 1) * P], qk_t[pr, t, cs], C[pr, t, 0:DV],
                                         start=True, stop=True)
                        nc.tensor.matmul(ps[:, 5, 4 + t:5 + t], qk_t[pr, t, cs], C[pr, t, DV:DV + 1],
                                         start=True, stop=True)
                if c < NB - 1:
                    for t in range(HG):
                        hd = 2 * t + g
                        kws = kw[:, c, hd * DK:(hd + 1) * DK]
                        nc.tensor.matmul(ps[pr, 4, t * P:(t + 1) * P], kws,
                                         v_tok[:, c, hd * DV:(hd + 1) * DV], start=True, stop=True)
                        nc.tensor.matmul(ps[pr, 5, 8 + t:9 + t], kws, ones[:, 0:1], start=True, stop=True)
                pe.wait_ge(w_done, s + 1)
                for t in range(HG):
                    hd = 2 * t + g
                    nc.tensor.matmul(ps[:, 2, t * P:(t + 1) * P], ew[:, s % 2, t],
                                     v_tok[:, c, hd * DV:(hd + 1) * DV], start=True, stop=True)
                    ins = nc.tensor.matmul(ps[:, 5, t:t + 1], ew[:, s % 2, t], ones[:, 0:1], start=True,
                                           stop=True)
                ins.then_inc(n_mm, 1)

            pe.wait_ge(kw_done, NB)
            pe.wait_ge(gt_done, 1)
            pe.wait_ge(v_done, 2 * NB)
            decays(0)
            for s in range(NS):
                g = G_O + s
                pe.wait_ge(w_lo_done, counted(g))
                if s >= 2:
                    pe.wait_ge(o_tanh, s - 1)
                project(SLOT[g], ps[:, 6 + s % 2]).then_inc(w_used, 1)
                combine(s)
                if s + 1 < NS:
                    decays(s + 1)

            def out_block(c, bank, g0, last):
                cs = slice(c * P, (c + 1) * P)
                pe.wait_ge(op_lo, (0 if g0 == G_MOUT else NB) + c + 1)
                pe.wait_ge(w_lo_done, counted(g0 + KT - 1))
                for i, k in enumerate([4, 5, 6, 7, 0, 1, 2, 3]):
                    s = SLOT[g0 + k]
                    for half in range(2):
                        hs = slice(half * HALF, (half + 1) * HALF)
                        dst = ps[:, bank + half]
                        nc.tensor.matmul(dst, act_hi[:, k, cs], w_hi[:, s, hs], start=(i == 0), stop=False)
                        nc.tensor.matmul(dst, act_hi[:, k, cs], w_lo[:, s, hs], start=False, stop=False)
                        ins = nc.tensor.matmul(dst, act_lo[:, k, cs], w_hi[:, s, hs], start=False,
                                               stop=(i == KT - 1))
                    if last:
                        ins.then_inc(w_used, 1)
                if not last:
                    ins.then_inc(y_done, 1)

            for c in range(NB):
                bank = 2 * (c % 2)
                pe.wait_ge(hs_done, c + 1)
                if c >= 2:
                    pe.wait_ge(gated_done, c - 1)
                for k in range(KT):
                    ins = nc.tensor.transpose(ps[:, bank + k // 4, (k % 4) * P:(k % 4 + 1) * P],
                                              v_tok[:, c, k * P:(k + 1) * P], ident[:])
                ins.then_inc(ht_mm, 1)
                if c >= 2:
                    pe.wait_ge(z_lo, NB + c - 1)
                out_block(c, 4 + 2 * (c % 2), G_MOUT, c == NB - 1)
                if c >= 1:
                    turn_norm(NB + c - 1, c - 1, 4 + 2 * ((c - 1) % 2))
            turn_norm(2 * NB - 1, NB - 1, 6)

            def ffn(l):
                up, down = G_UP[l], G_DOWN[l]
                pe.wait_ge(z_lo, (2 + 2 * l) * NB)
                with pe.Fori(0, FT // 2) as i:
                    for t in range(2):
                        pe.wait_ge(hid_done, i * 2 + (l * FT + t + 1))
                        pe.wait_ge(w_lo_done, i * 4 + counted(up + 2 * t))
                        project(2 * t, ps[:, 2 * t]).then_inc(w_used, 1)
                        pe.wait_ge(w_lo_done, i * 4 + counted(up + 2 * t + 1))
                        project(2 * t + 1, ps[:, 2 * t + 1]).then_inc(w_used, 1)

                def down_part(s, b, half, start, stop):
                    bs = slice(b * P, (b + 1) * P)
                    hs = slice(half * HALF, (half + 1) * HALF)
                    dst = ps[:, 2 * b + half]
                    nc.tensor.matmul(dst, act_hi[:, s, bs], w_hi[:, s, hs], start=start, stop=False)
                    nc.tensor.matmul(dst, act_hi[:, s, bs], w_lo[:, s, hs], start=False, stop=False)
                    return nc.tensor.matmul(dst, act_lo[:, s, bs], w_hi[:, s, hs], start=False, stop=stop)

                for j in range(2):
                    pe.wait_ge(w_lo_done, counted(down + j))
                    pe.wait_ge(hid_lo, l * FT + j + 1)
                    for b in (2, 3, 0, 1):
                        if j == 0 and b < 2:
                            pe.wait_ge(hid_done, (l + 1) * FT + 1 + b)
                        for half in range(2):
                            ins = down_part(4 + j, b, half, j == 0, False)
                    ins.then_inc(w_used, 1)
                with pe.Fori(0, (FT - TAIL) // 2 - 1) as i:
                    for j in range(2):
                        pe.wait_ge(w_lo_done, i * 2 + counted(down + 2 + j))
                        pe.wait_ge(hid_lo, i * 2 + (l * FT + 2 + j + 1))
                        for b in range(NB):
                            for half in range(2):
                                ins = down_part(4 + j, b, half, False, False)
                        ins.then_inc(w_used, 1)
                pe.wait_ge(w_lo_done, counted(down + FT - 1))
                pe.wait_ge(hid_lo, (l + 1) * FT)
                for b in range(NB):
                    for s in range(TAIL):
                        for half in range(2):
                            ins = down_part(s, b, half, False, s == TAIL - 1)
                        if b == NB - 1:
                            ins.then_inc(w_used, 1)
                    if b < NB - 1:
                        ins.then_inc(y_done, 1)
                    if b >= 1 and l == 0:
                        turn_norm(2 * NB + b - 1, b - 1, 2 * (b - 1))
                if l == 0:
                    turn_norm(3 * NB - 1, NB - 1, 2 * (NB - 1))

            ffn(0)

            pe.wait_ge(z_lo, 3 * NB)
            for n in range(A_UNITS):
                g = G_AIN + n
                pe.wait_ge(w_lo_done, counted(g))
                if n >= 2:
                    pe.wait_ge(pj_used, QK_UNITS + n - 1)
                project(SLOT[g], ps[:, n % 2]).then_inc(w_used, 1)
            pe.wait_ge(pj_used, QK_UNITS + A_UNITS)
            for c in range(NB):
                ins = nc.tensor.transpose(ps[:, 2, c * P:(c + 1) * P], v_t[:, c * P:(c + 1) * P], ident[:])
            ins.then_inc(va_mm, 1)

            def scores(s):
                blk, n = s // ASTEPS, s % ASTEPS
                g = n * AG // KT
                pr = slice(g * DH, (g + 1) * DH)
                if s >= 1:
                    pe.wait_ge(mx_done, s)
                lo = P if blk == 0 else 0
                for j in range(AG):
                    t = (n * AG + j) % KT
                    dst = ps[:, j // 2, (j % 2) * 2 * P + lo:(j % 2 + 1) * 2 * P]
                    ins = nc.tensor.matmul(dst, q_t[pr, t, blk * P:(blk + 1) * P],
                                           k_t[pr, (blk - 1) * P + lo:(blk + 1) * P], start=True, stop=True)
                ins.then_inc(s_mm, 1)

            def turn_probs(s):
                b, blk = s % 2, s // ASTEPS
                pe.wait_ge(p_done, s + 1)
                if s >= 1:
                    pe.wait_ge(pt_done, s)
                for j in range(AG):
                    for kb in range(1 if blk == 0 else 0, 2):
                        ins = nc.tensor.transpose(ps[:, 2 + j // 2, ((j % 2) * 2 + kb) * P:
                                                     ((j % 2) * 2 + kb + 1) * P],
                                                  sc[:, b, j, kb * P:(kb + 1) * P], ident[:])
                ins.then_inc(pt_mm, 1)

            def mix(s):
                b, blk, n = s % 2, s // ASTEPS, s % ASTEPS
                g = n * AG // KT
                pe.wait_ge(pt_done, s + 1)
                if s >= 2:
                    pe.wait_ge(o_tok_done, s - 1)
                for j in range(AG):
                    for kb in range(1 if blk == 0 else 0, 2):
                        ins = nc.tensor.matmul(ps[:, 4 + s % 2, j * DH:(j + 1) * DH],
                                               p_t[:, b, j, kb * P:(kb + 1) * P],
                                               va[:, blk - 1 + kb, g * DH:(g + 1) * DH],
                                               start=(kb == 0 or blk == 0), stop=(kb == 1))
                ins.then_inc(o_mm2, 1)

            pe.wait_ge(va_done, 1)
            TOT = NB * ASTEPS

            def turn_out(c):
                pe.wait_ge(o_tok_done, (c + 1) * ASTEPS)
                if c >= 1:
                    pe.wait_ge(z_lo, 3 * NB + c)
                for k in range(KT):
                    ins = nc.tensor.transpose(ps[:, 6 + k // 4, (k % 4) * P:(k % 4 + 1) * P],
                                              o_tok[:, c % 2, k * P:(k + 1) * P], ident[:])
                ins.then_inc(ht_mm, 1)

            scores(0)
            for s in range(TOT + 1):
                if s + 1 < TOT:
                    scores(s + 1)
                if s < TOT:
                    turn_probs(s)
                if s >= 1:
                    mix(s - 1)
                if s >= 1 and s % ASTEPS == 0:
                    turn_out(s // ASTEPS - 1)
                if s >= ASTEPS + 1 and (s - 1) % ASTEPS == 0:
                    out_block((s - 1) // ASTEPS - 1, 6, G_AOUT, False)
                if s >= ASTEPS + 2 and (s - 2) % ASTEPS == 0:
                    c = (s - 2) // ASTEPS - 1
                    turn_norm(3 * NB + c, c, 6)
            out_block(NB - 1, 6, G_AOUT, True)
            turn_norm(4 * NB - 1, NB - 1, 6)

            ffn(1)


_INS = ["x", "m_w_in", "m_gate_bias", "m_head_norm", "m_w_out", "a_w_in", "a_b_in", "a_sinks",
        "a_w_out", "a_b_out", "norm_mix_pre", "norm_mix_post", "norm_ffn_pre", "norm_ffn_post",
        "f_w_up", "f_conv_w", "f_conv_b", "f_w_down"]


def kernel(**inputs):
    import numpy as np
    import concourse.bacc as bacc
    from concourse.bass_utils import run_bass_kernel_spmd

    nc = bacc.Bacc("TRN2", target_bir_lowering=False, num_devices=1)
    arrays, args = {}, []
    for name in _INS:
        a = np.ascontiguousarray(inputs[name])
        arrays[f"in_{name}"] = a
        args.append(nc.dram_tensor(f"in_{name}", a.shape, mybir.dt.from_np(a.dtype),
                                   kind="ExternalInput").ap())
    shape = inputs["x"].shape
    out = nc.dram_tensor("out", shape, F32, kind="ExternalOutput").ap()
    trunk(nc, *args, out)
    r = run_bass_kernel_spmd(nc, [arrays], core_ids=[0])
    return r.results[0]["out"]
```

```python
from contextlib import ExitStack

import concourse.bass as bass
from concourse import mybir

F32 = mybir.dt.float32
F32R = mybir.dt.float32r
BF16 = mybir.dt.bfloat16
ALU = mybir.AluOpType
ACT = mybir.ActivationFunctionType
AX = mybir.AxisListType

P = 128
EPS = 1e-6
GATE_CAP = 15.0
MASKED = -1.0e30
LN_EXP_SET = "natural_log_exp_and_others"
EXP_TANH_SET = "exp_and_others"
CREDIT = 4


def trunk(nc, x, m_w_in, m_gate_bias, m_head_norm, m_w_out, a_w_in, a_b_in, a_sinks, a_w_out,
          a_b_out, norm_mix_pre, norm_mix_post, norm_ffn_pre, norm_ffn_post, f_w_up, f_conv_w,
          f_conv_b, f_w_down, out):
    S, D = x.shape[1], x.shape[2]
    NB = S // P
    KT = D // P
    FF = f_w_down.shape[1]
    FT = FF // P
    MH = m_gate_bias.shape[2]
    DK, DV = D // (2 * MH), D // MH
    DH = 64
    QH = a_sinks.shape[1]
    KVH = (a_w_in.shape[2] // DH - QH) // 2
    HALF = 512
    ROWS = 2 * MH
    NS = 2 * NB
    HG = MH // 2
    AG = 4
    ASTEPS = QH // AG
    assert NB == 4 and KT == 8 and FT == 22 and MH == 8 and DV == P and DK == 64 and KVH == 2

    QK_UNITS, V_UNITS, O_UNITS = 2 * MH * DK // P, MH * DV * D // (P * D), D // P
    TAIL = 4
    G_GATE = 0
    G_QK = 1
    G_V = G_QK + QK_UNITS
    G_O = G_V + V_UNITS
    G_MOUT = G_O + O_UNITS
    G_UP = [G_MOUT + KT, 0]
    G_DOWN = [G_UP[0] + 2 * FT, 0]
    G_AIN = G_DOWN[0] + FT
    A_UNITS = (QH + 2 * KVH) * DH // P
    G_AOUT = G_AIN + A_UNITS
    G_UP[1] = G_AOUT + KT
    G_DOWN[1] = G_UP[1] + 2 * FT
    SLOT = [7] + [n % 4 for n in range(QK_UNITS + V_UNITS + O_UNITS)]
    FFN_SLOTS = [4 + n % 4 for n in range(2 * FT)] + [n % 2 for n in range(FT - TAIL)]
    FFN_SLOTS += list(range(4, 4 + TAIL))
    SLOT += [(k + 4) % 8 for k in range(KT)] + FFN_SLOTS
    SLOT += [n % 4 for n in range(A_UNITS)] + [4, 5, 6, 7, 2, 3, 0, 1] + FFN_SLOTS

    DMAS = [2 if q == G_GATE or G_AIN <= q < G_AIN + KT else 1 for q in range(len(SLOT))]

    def landed(g):
        return 16 * sum(DMAS[q] for q in range(g + 1) if SLOT[q] % 4 == SLOT[g] % 4)

    def freed(g):
        return counted(max([q for q in range(g) if SLOT[q] == SLOT[g]], default=-1))

    def counted(g):
        return g + 1 + CREDIT

    with ExitStack() as ctx:
        def sb(name, shape, dt=F32):
            return ctx.enter_context(nc.sbuf_tensor(name, shape, dt))

        def sem(name):
            return ctx.enter_context(nc.semaphore(name))

        ps = ctx.enter_context(nc.psum_tensor("ps", [P, 8, HALF], F32))

        raw = sb("raw", [P, 4, D])
        w_hi = sb("w_hi", [P, 8, D], F32R)
        w_lo = sb("w_lo", [P, 8, D], F32R)
        act_hi = sb("act_hi", [P, KT, S], F32R)
        act_lo = sb("act_lo", [P, KT, S], F32R)
        h = sb("h", [P, NB, D])
        g_post = sb("g_post", [P, D])
        g_pre = sb("g_pre", [P, D])
        arena = sb("arena", [P, 64 * 256 + 16])
        KB = 256

        ident = sb("ident", [P, P])
        causal = sb("causal", [P, P])
        ones = sb("ones", [P, 1])
        band = sb("band", [P, 2 * P])
        u_rows = sb("u_rows", [MH, S])
        junk = sb("junk", [P, HG, P], BF16)
        stat = sb("stat", [P, 2, 4])
        eps_col = sb("eps_col", [P, 1])
        VECS = 2 * 4 * FT + MH + A_UNITS
        vecs = sb("vecs", [P, VECS])
        taps = [vecs[:, l * 4 * FT:(l + 1) * 4 * FT].rearrange("p (j f) -> p j f", j=4) for l in range(2)]
        head_norm = vecs[:, 8 * FT:8 * FT + MH]
        a_bias = vecs[:, 8 * FT + MH:VECS]
        gate_b = sb("gate_b", [P, 2])
        hn_half = sb("hn_half", [P, MH])
        gt = sb("gt", [P, NB, 4, MH])
        dm = sb("dm", [P, NB, MH])
        s2 = sb("s2", [P, NB, MH])
        fac = sb("fac", [P, 3, NB * MH])
        dtmp = sb("dtmp", [P, 3, HG])
        decay_all = sb("decay_all", [P, MH, NB])
        decay = sb("decay", [MH, 3, NB])
        dsel = sb("dsel", [MH, MH, NB])
        sink = sb("sink", [P, QH])
        asm = sb("asm", [P, 2, 6, AG])

        v_tok = arena[:, 0:16 * KB].rearrange("p (c f) -> p c f", c=NB)
        o_sig = arena[:, 16 * KB:32 * KB].rearrange("p (k t) -> p k t", k=KT)
        rows = arena[0:MH, 16 * KB:32 * KB].rearrange("p (r t) -> p r t", r=8)
        qk_t = arena[:, 32 * KB:48 * KB].rearrange("p (k t) -> p k t", k=QK_UNITS)
        kw = arena[:, 48 * KB:56 * KB].rearrange("p (c f) -> p c f", c=NB)
        ew = arena[:, 56 * KB:60 * KB].rearrange("p (b t q) -> p b t q", b=2, t=HG)
        itmp = arena[:, 60 * KB:62 * KB].rearrange("p (t q) -> p t q", t=HG)
        zrow = rows[:, 5]
        vec_rows = arena[:, 60 * KB:60 * KB + 3 * P].rearrange("p (r f) -> p r f", r=3)
        C = arena[:, 62 * KB:62 * KB + HG * (DV + 1)].rearrange("p (t q) -> p t q", t=HG)
        gated = arena[:, 32 * KB:36 * KB].rearrange("p (k t) -> p k t", k=KT)
        q_t = arena[:, 0:16 * KB].rearrange("p (k t) -> p k t", k=KT)
        k_t = arena[:, 16 * KB:18 * KB]
        v_t = arena[:, 18 * KB:20 * KB]
        va = arena[:, 20 * KB:22 * KB].rearrange("p (c f) -> p c f", c=NB)
        sc = arena[:, 22 * KB:30 * KB].rearrange("p (b j k) -> p b j k", b=2, j=AG)
        p_t = arena[:, 30 * KB:38 * KB].rearrange("p (b j k) -> p b j k", b=2, j=AG)
        o_tok = arena[:, 38 * KB:46 * KB].rearrange("p (b f) -> p b f", b=2)
        b_out = arena[:, 60 * KB:64 * KB]
        hid = arena[:, 0:44 * KB].rearrange("p (f t) -> p f t", f=FT)
        cv = arena[:, 44 * KB:48 * KB].rearrange("p (b t) -> p b t", b=2)
        tmp = arena[:, 48 * KB:52 * KB]
        zn = arena[:, 52 * KB:60 * KB].rearrange("p (b f) -> p b f", b=2)
        hid_pair = [[w[:, 2, j * HALF:(j + 1) * HALF] for w in (w_hi, w_lo)] for j in range(2)]

        raw_in = [sem(f"raw_in{i}") for i in range(4)]
        w_hi_done, w_lo_done, w_used = sem("w_hi_done"), sem("w_lo_done"), sem("w_used")
        x_in = [sem(f"x_in{i}") for i in range(NB)]
        gain_in = sem("gain_in")
        vec_in, const_in, bout_in = sem("vec_in"), sem("const_in"), sem("bout_in")
        vec_mm, vec_done = sem("vec_mm"), sem("vec_done")
        out_done = sem("out_done")
        pool_done = sem("pool_done")
        act_chain, dve_chain = sem("act_chain"), sem("dve_chain")
        y_done, rs_post, rs_pre = sem("y_done"), sem("rs_post"), sem("rs_pre")
        yb_done, h_done = sem("yb_done"), sem("h_done")
        zn_done, zt_done, z_hi, z_lo = sem("zn_done"), sem("zt_done"), sem("z_hi"), sem("z_lo")
        cv0, cv1, cv2 = (sem(n) for n in ("cv0", "cv1", "cv2"))
        silu_done, hid_done = sem("silu_done"), sem("hid_done")
        hid_hi, hid_lo = sem("hid_hi"), sem("hid_lo")
        pj_used = sem("pj_used")
        tr_mm, gt_done, dsel_done, dec_mm, kt_mm, kw_done = (
            sem(n) for n in ("tr_mm", "gt_done", "dsel_done", "dec_mm", "kt_mm", "kw_done"))
        v_mm, v_done = sem("v_mm"), sem("v_done")
        row_ready = sem("row_ready")
        row_act = sem("row_act")
        u_mm, e_raw, e_exp, st_mm, w_done, n_mm, num_done, c_done, sq_done = (
            sem(n) for n in ("u_mm", "e_raw", "e_exp", "st_mm", "w_done", "n_mm", "num_done",
                             "c_done", "sq_done"))
        o_tanh, o_done = sem("o_tanh"), sem("o_done")
        fac_dve, fac_act = sem("fac_dve"), sem("fac_act")
        hs_done, ht_mm, gated_done, op_hi, op_lo = (
            sem(n) for n in ("hs_done", "ht_mm", "gated_done", "op_hi", "op_lo"))
        va_mm, va_done, s_mm, mx_done, p_done, pt_mm, pt_done, pv_mm, o_tok_done = (
            sem(n) for n in ("va_mm", "va_done", "s_mm", "mx_done", "p_done", "pt_mm", "pt_done",
                             "pv_mm", "o_tok_done"))
        t_mm, t_hi, t_lo, inv_done = sem("t_mm"), sem("t_hi"), sem("t_lo"), sem("inv_done")

        def values(half, b):
            return (w_used, counted(G_V + 4 * half + 3)) if b == NB - 1 else (v_mm, 3 * half + b + 1)

        def products(n):
            last = [G_MOUT + KT, G_DOWN[0] + FT, G_AOUT + KT, G_DOWN[1] + FT][n // NB] - 1
            return (w_used, counted(last)) if n % NB == NB - 1 else (y_done, n - n // NB + 1)

        def block_work(s):
            c, i = s // ASTEPS, s % ASTEPS
            if c < NB:
                return {0: [("out", c - 2, 3), ("y", c - 2), ("turn", "out", c - 1, 0)],
                        1: [("out", c - 1, 0), ("post", c - 2), ("turn", "out", c - 1, 1)],
                        2: [("out", c - 1, 1), ("pre", c - 2), ("turn", "norm", c - 2, 0)],
                        3: [("out", c - 1, 2), ("turn", "norm", c - 2, 1)]}[i]
            if i == 0:
                return [("out", NB - 2, 3), ("y", NB - 2), ("turn", "out", NB - 1, 0),
                        ("turn", "out", NB - 1, 1)]
            return [("out", NB - 1, 0), ("out", NB - 1, 1), ("post", NB - 2), ("out", NB - 1, 2),
                    ("pre", NB - 2), ("turn", "norm", NB - 2, 0), ("turn", "norm", NB - 2, 1),
                    ("out", NB - 1, 3), ("y", NB - 1), ("post", NB - 1), ("pre", NB - 1),
                    ("turn", "norm", NB - 1, 0), ("turn", "norm", NB - 1, 1)]

        AT_STEPS = NB * ASTEPS
        WORK = [[w for w in block_work(s) if w[2 if w[0] == "turn" else 1] >= 0]
                for s in range(AT_STEPS + 2)]
        TURNS = [w for ws in WORK for w in ws if w[0] == "turn"]

        def turn_of(what, b, half):
            return TURNS.index(("turn", what, b, half))

        def turn_bank(n):
            return 5 if n < len(TURNS) - 6 else n - (len(TURNS) - 6)

        def a_bank(n):
            return n % 3 if n < A_UNITS - 1 else 5

        OUT_SPLITS = {0: [2, 3], 1: [4], 2: [5], 3: [6, 7]}
        LAST = TURNS[-2:]

        def unit(slot):
            return (w_hi[:, slot].rearrange("p (k c) -> p k c", k=KT),
                    w_lo[:, slot].rearrange("p (k c) -> p k c", k=KT))

        block = ctx.enter_context(nc.Block())

        @block.sync
        def _(sp):
            def load(g, src, dst=None):
                s = SLOT[g] % 4
                dst = raw[:, s] if dst is None else dst
                nc.sync.dma_start(dst, src).then_inc(raw_in[s], 16)

            def load_free(g):
                last = [q for q in range(g) if SLOT[q] % 4 == SLOT[g] % 4]
                if last:
                    sp.wait_ge(w_lo_done, counted(last[-1]))

            def gains(post, pre):
                if post is not None:
                    nc.sync.dma_start(g_post[:], post.partition_broadcast(P)).then_inc(gain_in, 16)
                if pre is not None:
                    nc.sync.dma_start(g_pre[:], pre.partition_broadcast(P)).then_inc(gain_in, 16)

            for b in range(NB):
                nc.sync.dma_start(h[:, b], x[0, b * P:(b + 1) * P]).then_inc(x_in[b], 16)
                if b == 0:
                    gains(None, norm_mix_pre[0])
                if b == 1:
                    w_k = m_w_in[0].rearrange("(k p) n -> p k n", p=P)
                    wg = raw[:, 3].rearrange("p (k c) -> p k c", k=KT)
                    GC = m_w_in.shape[2] - ROWS
                    sp.wait_ge(pool_done, 1)
                    nc.sync.dma_start(wg[:, :, 0:MH], w_k[:, :, GC:GC + MH]).then_inc(raw_in[3], 16)
                    nc.sync.dma_start(wg[:, :, 32:32 + MH],
                                      w_k[:, :, GC + MH:GC + ROWS]).then_inc(raw_in[3], 16)
            w_in = m_w_in[0]

            def load_qk(n):
                load_free(G_QK + n)
                load(G_QK + n, w_k[:, :, n * P:(n + 1) * P],
                     raw[:, SLOT[G_QK + n] % 4].rearrange("p (k c) -> p k c", k=KT))

            for n in range(2):
                load_qk(n)
            for l in range(2):
                nc.sync.dma_start(vec_rows[0:3 * FT, l],
                                  f_conv_w[l].rearrange("j (f p) -> (j f) p", p=P))\
                    .then_inc(vec_in, 16)
                nc.sync.dma_start(vec_rows[3 * FT:4 * FT, l],
                                  f_conv_b[l].rearrange("(f p) -> f p", p=P)).then_inc(vec_in, 16)
            nc.sync.dma_start(vec_rows[0:MH, 2], m_head_norm[0].rearrange("(h p) -> h p", p=P))\
                .then_inc(vec_in, 16)
            for j in range(KVH):
                nc.sync.dma_start(
                    vec_rows[MH:MH + KT, 2, j * DH:(j + 1) * DH],
                    a_b_in[0, j * D // 2:(j + 1) * D // 2].rearrange("(t d) -> t d", d=DH))\
                    .then_inc(vec_in, 16)
            nc.sync.dma_start(vec_rows[MH + KT:MH + A_UNITS, 2],
                              a_b_in[0, QH * DH:].rearrange("(c p) -> c p", p=P))\
                .then_inc(vec_in, 16)
            for j in range(2):
                nc.sync.dma_start(gate_b[32 * j:32 * j + MH, 0:1],
                                  m_gate_bias[0, j:j + 1].rearrange("a h -> h a"),
                                  allow_slow_non_contiguous=True).then_inc(const_in, 16)
            nc.sync.dma_start(sink[:], a_sinks[0].partition_broadcast(P)).then_inc(const_in, 16)
            for n in range(2, QK_UNITS):
                load_qk(n)
            VC = 2 * MH * DK
            for n in range(V_UNITS):
                half, kp = n // 4, n % 4
                load_free(G_V + n)
                load(G_V + n, w_k[:, 2 * kp:2 * kp + 2, VC + half * HALF:VC + (half + 1) * HALF],
                     raw[:, SLOT[G_V + n] % 4].rearrange("p (k c) -> p k c", k=2))
            OC = VC + MH * DV
            for n in range(O_UNITS):
                load_free(G_O + n)
                load(G_O + n, w_k[:, :, OC + n * P:OC + (n + 1) * P],
                     raw[:, SLOT[G_O + n] % 4].rearrange("p (k c) -> p k c", k=KT))
            sp.wait_ge(zn_done, NB)
            gains(norm_mix_post[0], norm_ffn_pre[0])
            for k in range(KT):
                load_free(G_MOUT + k)
                load(G_MOUT + k, m_w_out[0, k * P:(k + 1) * P])

            def ffn_loads(l):
                up, down = G_UP[l], G_DOWN[l]
                w_up = f_w_up[l].rearrange("(k p) n -> p k n", p=P)
                for j in range(4):
                    load_free(up + j)
                    tile = FT * (j % 2) + j // 2
                    load(up + j, w_up[:, :, tile * P:(tile + 1) * P],
                         raw[:, j].rearrange("p (k c) -> p k c", k=KT))
                with sp.Fori(1, FT // 2) as i:
                    for j in range(4):
                        sp.wait_ge(w_lo_done, i * 4 + counted(up + j - 4))
                        tile = i * 2 + (FT * (j % 2) + j // 2)
                        nc.sync.dma_start(raw[:, j].rearrange("p (k c) -> p k c", k=KT),
                                          w_up[:, :, bass.ds(tile * P, P)]).then_inc(raw_in[j], 16)
                for j in range(2):
                    load_free(down + j)
                    load(down + j, f_w_down[l, j * P:(j + 1) * P])
                with sp.Fori(1, (FT - TAIL) // 2) as i:
                    for j in range(2):
                        sp.wait_ge(w_lo_done, i * 2 + counted(down + j - 2))
                        nc.sync.dma_start(raw[:, j], f_w_down[l, bass.ds(i * (2 * P) + j * P, P)])\
                            .then_inc(raw_in[j], 16)
                for n in range(FT - TAIL, FT):
                    load_free(down + n)
                    load(down + n, f_w_down[l, n * P:(n + 1) * P])

            ffn_loads(0)
            sp.wait_ge(zn_done, 2 * NB)
            gains(norm_ffn_post[0], norm_mix_pre[1])
            wa = a_w_in[0].rearrange("(k p) n -> p k n", p=P)
            for n in range(A_UNITS):
                load_free(G_AIN + n)
                dst = raw[:, SLOT[G_AIN + n] % 4].rearrange("p (k c) -> p k c", k=KT)
                if n < KT:
                    s = SLOT[G_AIN + n] % 4
                    for j in range(KVH):
                        c0 = (n + 8 * j) * DH
                        nc.sync.dma_start(dst[:, :, j * DH:(j + 1) * DH], wa[:, :, c0:c0 + DH])\
                            .then_inc(raw_in[s], 16)
                else:
                    load(G_AIN + n, wa[:, :, n * P:(n + 1) * P], dst)
            sp.wait_ge(zn_done, 3 * NB)
            gains(norm_mix_post[1], norm_ffn_pre[1])
            nc.sync.dma_start(b_out, a_b_out[0].partition_broadcast(P)).then_inc(bout_in, 16)
            for k in range(KT):
                load_free(G_AOUT + k)
                load(G_AOUT + k, a_w_out[0, k * P:(k + 1) * P])
            ffn_loads(1)
            sp.wait_ge(zn_done, 4 * NB)
            gains(norm_ffn_post[1], None)
            for b in range(NB):
                sp.wait_ge(h_done, 3 * NB + b + 1)
                nc.sync.dma_start(out[0, b * P:(b + 1) * P], h[:, b]).then_inc(out_done, 16)
            sp.wait_ge(out_done, 16 * NB)

        @block.gpsimd
        def _(pool):
            nc.gpsimd.memset(raw[:, 3], 0.0).then_inc(pool_done, 1)
            nc.gpsimd.memset(ident[:], 1.0).then_inc(pool_done, 1)
            nc.gpsimd.memset(causal[:], 0.0).then_inc(pool_done, 1)
            nc.gpsimd.memset(band[:], 0.0).then_inc(pool_done, 1)
            nc.gpsimd.memset(ones[:], 1.0).then_inc(w_used, CREDIT)
            pool.wait_ge(pool_done, 4)
            nc.gpsimd.affine_select(out=ident[:], in_=ident[:], compare_op=ALU.is_equal, fill=0.0,
                                    base=0, pattern=[[-1, P]], channel_multiplier=1).then_inc(pool_done, 1)
            nc.gpsimd.affine_select(out=causal[:], in_=causal[:], compare_op=ALU.is_ge, fill=MASKED,
                                    base=0, pattern=[[1, P]], channel_multiplier=-1).then_inc(pool_done, 1)
            nc.gpsimd.affine_select(out=band[:, 0:P], in_=band[:, 0:P], compare_op=ALU.is_gt,
                                    fill=MASKED, base=0, pattern=[[1, P]],
                                    channel_multiplier=-1).then_inc(pool_done, 1)
            nc.gpsimd.affine_select(out=band[:, P:], in_=band[:, P:], compare_op=ALU.is_ge,
                                    fill=MASKED, base=0, pattern=[[-1, P]],
                                    channel_multiplier=1).then_inc(pool_done, 1)
            pool.wait_ge(vec_done, 1)
            nc.gpsimd.tensor_scalar(hn_half[:], head_norm, 0.5, None, ALU.mult).then_inc(pool_done, 1)
            pool.wait_ge(pool_done, 9)
            for n in range(O_UNITS):
                pool.wait_ge(o_tanh, n + 1)
                nc.gpsimd.tensor_scalar(o_sig[:, n], o_sig[:, n], hn_half[:, n:n + 1], hn_half[:, n:n + 1],
                                        ALU.mult, ALU.add).then_inc(o_done, 1)

        @block.scalar
        def _(act):
            chain = [0]

            def link(ins):
                chain[0] += 1
                ins.then_inc(act_chain, 1)
                act.wait_ge(act_chain, chain[0])

            def split_hi(g):
                s = SLOT[g]
                act.wait_ge(raw_in[s % 4], landed(g))
                act.wait_ge(w_used, freed(g))
                nc.scalar.copy(w_hi[:, s], raw[:, s % 4]).then_inc(w_hi_done, 1)

            def rsqrt_mean(b, ss):
                dst = stat[:, b % 2, ss + 1:ss + 2]
                link(nc.scalar.activation(dst, stat[:, b % 2, ss:ss + 1], ACT.Ln, scale=1.0 / D,
                                          bias=eps_col[:, 0:1]))
                return nc.scalar.activation(dst, dst, ACT.Exp, scale=-0.5)

            def norm_post(n, b, bank, biased=False):
                if biased:
                    act.wait_ge(yb_done, b + 1)
                    src = tmp
                else:
                    act.wait_ge(*products(n))
                    src = ps[:, bank:bank + 2].rearrange("p a f -> p (a f)")
                if n >= 2:
                    act.wait_ge(h_done, n - 1)
                link(nc.scalar.activation(zn[:, b % 2], src, ACT.Square,
                                          accum_out=stat[:, b % 2, 0:1]))
                rsqrt_mean(b, 0).then_inc(rs_post, 1)

            def norm_pre(n, b):
                if n < NB:
                    act.wait_ge(x_in[b], 16)
                    if n >= 2:
                        act.wait_ge(zn_done, n - 1)
                else:
                    act.wait_ge(h_done, n - NB + 1)
                link(nc.scalar.activation(tmp, h[:, b], ACT.Square, accum_out=stat[:, b % 2, 2:3]))
                rsqrt_mean(b, 2).then_inc(rs_pre, 1)

            def norm_hi(n, b, bank):
                act.wait_ge(zt_done, n + 1)
                nc.scalar.copy(act_hi[:, :, b * P:(b + 1) * P],
                               ps[:, bank:bank + 2].rearrange("p a (k t) -> p (a k) t", t=P))\
                    .then_inc(z_hi, 1)

            nc.scalar.preload_act_table_set(LN_EXP_SET)
            act.wait_ge(dve_chain, 1)
            norm_pre(0, 0)
            norm_pre(1, 1)
            norm_hi(0, 0, 0)
            split_hi(G_GATE)
            norm_pre(2, 2)
            norm_hi(1, 1, 2)
            norm_pre(3, 3)
            split_hi(G_QK)
            norm_hi(2, 2, 4)
            split_hi(G_QK + 1)
            norm_hi(3, 3, 6)
            for n in range(2, 4):
                split_hi(G_QK + n)

            nc.scalar.preload_act_table_set(EXP_TANH_SET)
            act.wait_ge(w_used, counted(G_GATE))
            act.wait_ge(row_ready, 1)
            link(nc.scalar.activation(rows[:, 0], ps[0:MH, 0], ACT.Tanh, scale=1.0 / GATE_CAP,
                                      bias=gate_b[0:MH, 1:2]))
            link(nc.scalar.activation(rows[:, 1], ps[32:32 + MH, 0], ACT.Tanh, scale=1.0 / GATE_CAP,
                                      bias=gate_b[32:32 + MH, 1:2]))
            link(nc.scalar.activation(rows[:, 1], rows[:, 1], ACT.Exp, scale=-GATE_CAP))
            nc.scalar.preload_act_table_set(LN_EXP_SET)
            nc.scalar.activation(rows[:, 2], rows[:, 1], ACT.Ln, scale=1.0, bias=1.0)\
                .then_inc(row_act, 1)
            nc.scalar.preload_act_table_set(EXP_TANH_SET)
            for n in range(4, QK_UNITS):
                split_hi(G_QK + n)
            act.wait_ge(row_ready, 2)
            for c in range(NB):
                cs = slice(c * P, (c + 1) * P)
                nc.scalar.activation(rows[:, 5, cs], rows[:, 4, cs], ACT.Exp,
                                     bias=u_rows[:, (c + 1) * P - 1:(c + 1) * P])
                nc.scalar.activation(rows[:, 6, cs], u_rows[:, cs], ACT.Exp,
                                     bias=decay[:, 0, c:c + 1])
            nc.scalar.activation(decay[:, 2], decay[:, 1], ACT.Exp)
            nc.scalar.activation(rows[:, 7], rows[:, 3], ACT.Exp, scale=-1.0).then_inc(row_act, 1)
            def squares(s):
                c, g = s // 2, s % 2
                act.wait_ge(num_done, s + 1)
                if s >= 1:
                    act.wait_ge(sq_done, s)
                for t in range(HG):
                    hd = 2 * t + g
                    ins = nc.scalar.activation(junk[:, t], v_tok[:, c, hd * DV:(hd + 1) * DV],
                                               ACT.Square, accum_out=s2[:, c, hd:hd + 1])
                ins.then_inc(sq_done, 1)

            for n in range(V_UNITS + 1):
                split_hi(G_V + n)
            act.wait_ge(gt_done, 1)
            def gated_hi(c, half):
                act.wait_ge(gated_done, 2 * c + half + 1)
                ks = slice(4 * half, 4 * half + 4)
                nc.scalar.copy(act_hi[:, ks, c * P:(c + 1) * P], gated[:, ks]).then_inc(op_hi, 1)

            def rms_heads(n, cols):
                act.wait_ge(fac_dve, n)
                link(nc.scalar.activation(fac[:, 1, cols], fac[:, 1, cols], ACT.Ln, scale=1.0 / DV,
                                          bias=eps_col[:, 0:1]))
                nc.scalar.activation(fac[:, 1, cols], fac[:, 1, cols], ACT.Exp, scale=-0.5)\
                    .then_inc(fac_act, 1)

            for s in range(NS):
                act.wait_ge(e_raw, s + 1)
                nc.scalar.activation(ew[:, s % 2], ew[:, s % 2], ACT.Exp).then_inc(e_exp, 1)
                if s < NS - 1:
                    split_hi(G_O + s + 1)
                else:
                    squares(s - 1)
                    nc.scalar.preload_act_table_set(LN_EXP_SET)
                    rms_heads(1, slice(0, (NB - 1) * MH))
                    nc.scalar.preload_act_table_set(EXP_TANH_SET)
                    for k in range(4):
                        split_hi(G_MOUT + k)
                act.wait_ge(w_used, counted(G_O + s))
                nc.scalar.activation(o_sig[:, s], ps[:, 6 + s % 2], ACT.Tanh, scale=0.5)\
                    .then_inc(o_tanh, 1)
                if 1 <= s < NS - 1:
                    squares(s - 1)
            gated_hi(0, 0)
            nc.scalar.preload_act_table_set(LN_EXP_SET)
            for k in range(4, 7):
                split_hi(G_MOUT + k)
            gated_hi(0, 1)
            split_hi(G_MOUT + 7)
            squares(NS - 1)
            rms_heads(2, slice((NB - 1) * MH, NB * MH))
            for c in range(NB):
                if c >= 2:
                    norm_hi(NB + c - 2, c - 2, 4 + 2 * (c % 2))
                if c + 1 < NB:
                    gated_hi(c + 1, 0)
                    gated_hi(c + 1, 1)
                if c >= 1:
                    norm_post(c - 1, c - 1, 4 + 2 * ((c - 1) % 2))
                    if c == NB - 1:
                        split_hi(G_UP[0])
                    norm_pre(NB + c - 1, c - 1)
            for n in range(1, 4):
                split_hi(G_UP[0] + n)
            norm_hi(2 * NB - 2, NB - 2, 4)
            norm_post(NB - 1, NB - 1, 6)
            norm_pre(2 * NB - 1, NB - 1)
            norm_hi(2 * NB - 1, NB - 1, 6)

            def ffn(l):
                up, down = G_UP[l], G_DOWN[l]

                def hi_pair(i, t):
                    for q in range(2):
                        g = up + 2 * t + q
                        s = (2 * t + q) % 4
                        act.wait_ge(raw_in[s], i * 16 + landed(g))
                        act.wait_ge(w_used, i * 4 + counted(g - 4))
                        nc.scalar.copy(w_hi[:, 4 + s], raw[:, s]).then_inc(w_hi_done, 1)

                def conv(i, t):
                    f = i * 2 + t
                    act.wait_ge(w_used, i * 4 + counted(up + 2 * t))
                    nc.scalar.activation(cv[:, t], ps[:, 2 * t], ACT.Identity,
                                         scale=taps[l][:, 2, bass.ds(f, 1)],
                                         bias=taps[l][:, 3, bass.ds(f, 1)]).then_inc(cv0, 1)
                    act.wait_ge(cv2, i * 2 + (l * FT + t + 1))
                    nc.scalar.activation(cv[:, t], cv[:, t], ACT.Silu).then_inc(silu_done, 1)

                nc.scalar.preload_act_table(ACT.Silu)
                if l == 0:
                    act.wait_ge(vec_done, 1)
                with act.Fori(0, FT // 2 - 1) as i:
                    conv(i, 0)
                    hi_pair(i, 2)
                    conv(i, 1)
                    hi_pair(i, 3)
                for j in range(2):
                    split_hi(down + j)
                for j in range(2):
                    nc.scalar.copy(hid_pair[j][0], hid[:, j]).then_inc(hid_hi, 1)
                conv(FT // 2 - 1, 0)
                conv(FT // 2 - 1, 1)
                nc.scalar.preload_act_table_set(LN_EXP_SET)
                with act.Fori(0, (FT - TAIL) // 2 - 1) as i:
                    for j in range(2):
                        act.wait_ge(raw_in[j], i * 16 + landed(down + 2 + j))
                        act.wait_ge(w_used, i * 2 + counted(down + j))
                        nc.scalar.copy(w_hi[:, j], raw[:, j]).then_inc(w_hi_done, 1)
                        nc.scalar.copy(hid_pair[j][0], hid[:, bass.ds(i * 2 + (2 + j), 1)]
                                       .rearrange("p a t -> p (a t)")).then_inc(hid_hi, 1)
                for n in range(FT - TAIL, FT):
                    split_hi(down + n)
                    if n == FT - 1:
                        act.wait_ge(hid_done, (l + 1) * FT + 2)
                    nc.scalar.copy(act_hi[:, n - (FT - TAIL)], hid[:, n]).then_inc(hid_hi, 1)

            def ffn_norms(l):
                for b in range(NB):
                    norm_post((2 * l + 1) * NB + b, b, 2 * b)
                    if l == 0:
                        if b >= 1:
                            norm_hi(2 * NB + b - 1, b - 1, 2 * (b - 1))
                        norm_pre(2 * NB + b, b)
                        if b < 3:
                            split_hi(G_AIN + b)
                if l == 0:
                    norm_hi(3 * NB - 1, NB - 1, 2 * (NB - 1))

            ffn(0)
            ffn_norms(0)
            for n in range(3, A_UNITS):
                split_hi(G_AIN + n)
            for k in range(2):
                split_hi(G_AOUT + k)

            def probs(s):
                b, blk = s % 2, s // ASTEPS
                lo = P if blk == 0 else 0
                act.wait_ge(mx_done, s + 1)
                for j in range(AG):
                    nc.scalar.activation(sc[:, b, j, lo:], sc[:, b, j, lo:], ACT.Exp,
                                         bias=asm[:, b, 1, j:j + 1], accum_out=asm[:, b, 2, j:j + 1])
                nc.scalar.activation(asm[:, b, 3], asm[:, b, 3], ACT.Exp).then_inc(p_done, 1)

            def turned(s):
                b, blk = s % 2, s // ASTEPS
                act.wait_ge(pt_mm, s + 1)
                lo = P if blk == 0 else 0
                nc.scalar.copy(p_t[:, b, :, lo:], ps[:, 2:4].rearrange("p a (j k) -> p (a j) k", k=2 * P)
                               [:, :, lo:]).then_inc(pt_done, 1)

            def turn_hi(b, half):
                n = turns_hi[0]
                turns_hi[0] += 1
                act.wait_ge(t_mm, n + 1)
                nc.scalar.copy(act_hi[:, 4 * half:4 * half + 4, b * P:(b + 1) * P],
                               ps[:, turn_bank(n)].rearrange("p (k t) -> p k t", t=P)).then_inc(t_hi, 1)

            turns_hi = [0]

            def work(w):
                if w[0] == "y":
                    norm_post(2 * NB + w[1], w[1], 6, biased=True)
                elif w[0] == "post":
                    norm_pre(3 * NB + w[1], w[1])
                elif w[0] == "turn":
                    turn_hi(w[2], w[3])

            probs(0)
            for s in range(AT_STEPS + 2):
                if 1 <= s <= AT_STEPS:
                    turned(s - 1)
                if s >= AT_STEPS:
                    for w in sorted(WORK[s], key=lambda w: s == AT_STEPS and w[0] == "y"):
                        work(w)
                        if w == ("post", NB - 2):
                            split_hi(G_UP[1])
                        if w == ("turn", "norm", NB - 2, 0):
                            split_hi(G_UP[1] + 1)
                        if w == ("turn", "norm", NB - 2, 1):
                            split_hi(G_UP[1] + 2)
                    continue
                if s >= 1:
                    for w in WORK[s - 1]:
                        if w[0] in ("y", "post"):
                            work(w)
                if s + 1 < AT_STEPS:
                    probs(s + 1)
                for k in OUT_SPLITS.get(s, []):
                    split_hi(G_AOUT + k)
                for w in WORK[s]:
                    if w[0] == "turn":
                        work(w)

            split_hi(G_UP[1] + 3)
            ffn(1)
            ffn_norms(1)

        @block.vector
        def _(dve):
            chain = [0]

            def link(ins):
                chain[0] += 1
                ins.then_inc(dve_chain, 1)
                dve.wait_ge(dve_chain, chain[0])

            def split_lo(g):
                s = SLOT[g]
                dve.wait_ge(w_hi_done, g + 1)
                nc.vector.tensor_tensor(w_lo[:, s], raw[:, s % 4], w_hi[:, s].bitcast(F32),
                                        ALU.subtract).then_inc(w_lo_done, 1)

            gains_in = [0]

            def norm_post(n, b, bank, biased=False):
                y = tmp if biased else ps[:, bank:bank + 2].rearrange("p a f -> p (a f)")
                if n > 3 * NB:
                    dve.wait_ge(h_done, n)
                dve.wait_ge(rs_post, n + 1)
                link(nc.vector.scalar_tensor_tensor(tmp, y, stat[:, b % 2, 1:2], g_post[:], ALU.mult, ALU.mult))
                nc.vector.tensor_tensor(h[:, b], h[:, b], tmp, ALU.add).then_inc(h_done, 1)

            def add_bias(b):
                dve.wait_ge(*products(2 * NB + b))
                if b == 0:
                    dve.wait_ge(bout_in, 16)
                nc.vector.tensor_tensor(tmp, ps[:, 6:8].rearrange("p a f -> p (a f)"), b_out, ALU.add)\
                    .then_inc(yb_done, 1)

            def norm_pre(n, b):
                dve.wait_ge(rs_pre, n + 1)
                if n >= 2 and n < NB:
                    dve.wait_ge(zt_done, n - 1)
                nc.vector.scalar_tensor_tensor(zn[:, b % 2], h[:, b], stat[:, b % 2, 3:4], g_pre[:],
                                               ALU.mult, ALU.mult).then_inc(zn_done, 1)

            def norm_lo(n, b, bank):
                dve.wait_ge(z_hi, n + 1)
                nc.vector.tensor_tensor(act_lo[:, :, b * P:(b + 1) * P],
                                        ps[:, bank:bank + 2].rearrange("p a (k t) -> p (a k) t", t=P),
                                        act_hi[:, :, b * P:(b + 1) * P].bitcast(F32),
                                        ALU.subtract).then_inc(z_lo, 1)

            def gains(n):
                gains_in[0] += n
                dve.wait_ge(gain_in, 16 * gains_in[0])

            link(nc.vector.memset(eps_col[:], EPS))
            nc.vector.memset(zrow, 0.0)
            nc.vector.memset(C[:], 0.0).then_inc(w_lo_done, CREDIT)
            link(nc.vector.memset(decay[:, 0, 0:1], 0.0))
            nc.vector.memset(junk[:, 0, 0:2], 0.0).then_inc(hid_done, 2)
            gains(1)
            norm_pre(0, 0)
            norm_pre(1, 1)
            norm_lo(0, 0, 0)
            split_lo(G_GATE)
            norm_pre(2, 2)
            norm_lo(1, 1, 2)
            norm_pre(3, 3)
            split_lo(G_QK)
            norm_lo(2, 2, 4)
            split_lo(G_QK + 1)
            norm_lo(3, 3, 6)
            for n in range(2, 4):
                split_lo(G_QK + n)
            dve.wait_ge(const_in, 16 * 3)
            nc.vector.tensor_scalar(gate_b[0:MH, 1:2], gate_b[0:MH, 0:1], 1.0 / GATE_CAP, None, ALU.mult)
            nc.vector.tensor_scalar(gate_b[32:32 + MH, 1:2], gate_b[32:32 + MH, 0:1], 1.0 / GATE_CAP, None,
                                    ALU.mult).then_inc(row_ready, 1)

            def copy_qk(n):
                dve.wait_ge(w_used, counted(G_QK + n))
                nc.vector.tensor_copy(qk_t[:, n], ps[:, 1 + n % 2]).then_inc(pj_used, 1)

            copy_qk(0)
            dve.wait_ge(row_act, 1)
            link(nc.vector.tensor_scalar(rows[:, 0], rows[:, 0], GATE_CAP, None, ALU.mult))
            link(nc.vector.tensor_scalar(rows[:, 1], rows[:, 2], -1.0, None, ALU.mult))
            link(nc.vector.tensor_tensor_scan(rows[:, 3], rows[:, 1], rows[:, 0], 0.0, ALU.add, ALU.max))
            for c in range(NB):
                cs = slice(c * P, (c + 1) * P)
                ins = nc.vector.tensor_tensor_scan(rows[:, 2, cs], rows[:, 1, cs], zrow[:, cs], 0.0,
                                                   ALU.add, ALU.add)
            link(ins)
            nc.vector.tensor_tensor(rows[:, 4], rows[:, 0], rows[:, 2], ALU.subtract)
            link(nc.vector.tensor_tensor(u_rows[:], rows[:, 2], rows[:, 3], ALU.subtract))
            m_c = rows[:, 3].rearrange("p (c t) -> p c t", t=P)
            u_c = u_rows[:].rearrange("p (c t) -> p c t", t=P)
            link(nc.vector.tensor_copy(decay[:, 0, 1:], m_c[:, 0:NB - 1, P - 1]))
            nc.vector.tensor_tensor(decay[:, 1], u_c[:, :, P - 1], decay[:, 0], ALU.add)\
                .then_inc(row_ready, 1)
            for n in range(1, QK_UNITS):
                if n >= 3:
                    split_lo(G_QK + n + 1)
                copy_qk(n)
                if n == 4:
                    dve.wait_ge(vec_mm, 1)
                    nc.vector.tensor_copy(vecs[:], ps[:, 3, 0:VECS]).then_inc(vec_done, 1)
            dve.wait_ge(row_act, 2)
            dve.wait_ge(pool_done, 8)
            nc.vector.tensor_tensor(dsel[:], decay[:, 2].unsqueeze(1).to_broadcast([MH, MH, NB]),
                                    ident[0:MH, 0:MH].unsqueeze(2).to_broadcast([MH, MH, NB]),
                                    ALU.mult).then_inc(dsel_done, 1)
            split_lo(G_V + 1)
            dve.wait_ge(tr_mm, 1)
            link(nc.vector.tensor_copy(gt[:].rearrange("p c q h -> p (c q h)"), ps[:, 0, 0:NB * 4 * MH]))
            dve.wait_ge(dec_mm, 1)
            link(nc.vector.tensor_copy(decay_all[:].rearrange("p h c -> p (h c)"),
                                       ps[:, 3, 0:MH * NB]))
            nc.vector.tensor_scalar(gt[:, :, 2], gt[:, :, 2], DK ** -0.5, None, ALU.mult)\
                .then_inc(gt_done, 1)
            for n in range(2, V_UNITS):
                split_lo(G_V + n)
                if n % 2 == 1 or n == 4:
                    pass
                c = n - 2
                if c < NB:
                    dve.wait_ge(kt_mm, c + 1)
                    nc.vector.tensor_tensor(
                        kw[:, c].rearrange("p (h d) -> p h d", h=MH),
                        ps[:, 1 + c % 2].rearrange("p (h d) -> p h d", h=MH),
                        gt[:, c, 1].unsqueeze(2).to_broadcast([P, MH, DK]), ALU.mult)\
                        .then_inc(kw_done, 1)
                if n == 4:
                    for b in range(NB):
                        dve.wait_ge(*values(0, b))
                        nc.vector.tensor_copy(v_tok[:, b, 0:HALF], ps[:, 4 + b]).then_inc(v_done, 1)
            dve.wait_ge(gt_done, 1)
            for b in range(NB):
                dve.wait_ge(*values(1, b))
                if b == 1:
                    split_lo(G_O)
                nc.vector.tensor_copy(v_tok[:, b, HALF:], ps[:, 4 + b]).then_inc(v_done, 1)

            def weights(s):
                c, g = s // 2, s % 2
                dve.wait_ge(u_mm, s + 1)
                for t in range(HG):
                    hd = 2 * t + g
                    ins = nc.vector.scalar_tensor_tensor(
                        ew[:, s % 2, t], ps[:, 0, t * P:(t + 1) * P], gt[:, c, 0, hd:hd + 1], causal[:],
                        ALU.add, ALU.min)
                ins.then_inc(e_raw, 1)

            def weigh(s):
                dve.wait_ge(e_exp, s + 1)
                dve.wait_ge(st_mm, s + 1)
                nc.vector.scalar_tensor_tensor(
                    ew[:, s % 2].rearrange("p t q -> p (t q)"), ps[:, 1], DK ** -0.5,
                    ew[:, s % 2].rearrange("p t q -> p (t q)"), ALU.mult, ALU.mult).then_inc(w_done, 1)

            def state(s):
                c, g = s // 2, s % 2
                if c == NB - 1:
                    return
                pr = slice(g * DK, (g + 1) * DK)
                dve.wait_ge(n_mm, s + 1)
                new = ps[pr, 4].rearrange("p (t v) -> p t v", t=HG)
                if c == 0:
                    nc.vector.tensor_copy(C[pr, :, 0:DV], new)
                    nc.vector.tensor_copy(C[pr, :, DV], ps[pr, 5, 8:8 + HG]).then_inc(c_done, 1)
                    return
                dec = decay_all[pr, g::2, c].unsqueeze(2).to_broadcast([DK, HG, DV + 1])
                link(nc.vector.tensor_tensor(C[pr], C[pr], dec, ALU.mult))
                nc.vector.tensor_tensor(C[pr, :, 0:DV], C[pr, :, 0:DV], new, ALU.add)
                nc.vector.tensor_tensor(C[pr, :, DV], C[pr, :, DV], ps[pr, 5, 8:8 + HG], ALU.add)\
                    .then_inc(c_done, 1)

            def outputs(s):
                c, g = s // 2, s % 2
                dve.wait_ge(n_mm, s + 1)
                num = v_tok[:, c].rearrange("p (t two v) -> p t two v", two=2, v=DV)[:, :, g]
                intra = ps[:, 2].rearrange("p (t v) -> p t v", t=HG)
                if c == 0:
                    link(nc.vector.tensor_copy(dtmp[:, 0], ps[:, 5, 0:HG]))
                    src = intra
                else:
                    s_inter = gt[:, c, 2, g::2]
                    nc.vector.tensor_tensor(itmp[:], ps[:, 3].rearrange("p (t v) -> p t v", t=HG),
                                            s_inter.unsqueeze(2).to_broadcast([P, HG, DV]), ALU.mult)
                    link(nc.vector.tensor_tensor(dtmp[:, 1], ps[:, 5, 4:4 + HG], s_inter, ALU.mult))
                    link(nc.vector.tensor_tensor(dtmp[:, 0], ps[:, 5, 0:HG], dtmp[:, 1], ALU.add))
                link(nc.vector.scalar_tensor_tensor(dtmp[:, 2], dtmp[:, 0], -1.0, dtmp[:, 0],
                                                    ALU.mult, ALU.max))
                nc.vector.tensor_tensor(dm[:, c, g::2], dtmp[:, 2], gt[:, c, 3, g::2], ALU.max)
                if c == 0:
                    ins = nc.vector.tensor_copy(num, intra)
                else:
                    ins = nc.vector.tensor_tensor(num, intra, itmp[:], ALU.add)
                ins.then_inc(num_done, 1)
                dve.wait_ge(num_done, s + 1)

            def head_factors(n, c0, c1):
                cols = slice(c0 * MH, c1 * MH)
                dve.wait_ge(sq_done, 2 * c1)
                link(nc.vector.reciprocal(fac[:, 0, cols], dm[:, c0:c1].rearrange("p c h -> p (c h)")))
                link(nc.vector.tensor_tensor(fac[:, 2, cols], fac[:, 0, cols], fac[:, 0, cols], ALU.mult))
                nc.vector.tensor_tensor(fac[:, 1, cols], fac[:, 2, cols],
                                        s2[:, c0:c1].rearrange("p c h -> p (c h)"),
                                        ALU.mult).then_inc(fac_dve, 1)
                dve.wait_ge(fac_act, n)
                link(nc.vector.tensor_tensor(fac[:, 0, cols], fac[:, 0, cols], fac[:, 1, cols], ALU.mult))

            def scale_heads(c):
                hv = v_tok[:, c].rearrange("p (h v) -> p h v", h=MH)
                f = fac[:, 0, c * MH:(c + 1) * MH].unsqueeze(2).to_broadcast([P, MH, DV])
                nc.vector.tensor_tensor(hv, hv, f, ALU.mult).then_inc(hs_done, 1)

            def gate_heads(c, half):
                dve.wait_ge(ht_mm, c + 1)
                dve.wait_ge(o_done, 4 * half + 4)
                ks = slice(4 * half, 4 * half + 4)
                if c >= 1:
                    dve.wait_ge(op_lo, 2 * c - 1 + half)
                nc.vector.tensor_tensor(gated[:, ks], ps[:, 2 * (c % 2) + half]
                                        .rearrange("p (k t) -> p k t", t=P),
                                        o_sig[:, ks, c * P:(c + 1) * P], ALU.mult).then_inc(gated_done, 1)

            def gated_lo(c, half):
                dve.wait_ge(op_hi, 2 * c + half + 1)
                ks = slice(4 * half, 4 * half + 4)
                nc.vector.tensor_tensor(act_lo[:, ks, c * P:(c + 1) * P], gated[:, ks],
                                        act_hi[:, ks, c * P:(c + 1) * P].bitcast(F32), ALU.subtract)\
                    .then_inc(op_lo, 1)

            for s in range(NS):
                if s >= 1:
                    outputs(s - 1)
                    state(s - 1)
                weights(s)
                weigh(s)
                if s + 1 < NS:
                    split_lo(G_O + s + 1)
            head_factors(1, 0, NB - 1)
            scale_heads(0)
            scale_heads(1)
            split_lo(G_MOUT)
            outputs(NS - 1)
            split_lo(G_MOUT + 1)
            gate_heads(0, 0)
            gated_lo(0, 0)
            for k in range(2, 4):
                split_lo(G_MOUT + k)
            gate_heads(0, 1)
            for k in range(4, 7):
                split_lo(G_MOUT + k)
            gated_lo(0, 1)
            split_lo(G_MOUT + 7)
            head_factors(2, NB - 1, NB)
            for c in range(NB):
                if c >= 2:
                    norm_lo(NB + c - 2, c - 2, 4 + 2 * (c % 2))
                if c + 1 < NB:
                    gate_heads(c + 1, 0)
                    gate_heads(c + 1, 1)
                    if c + 2 < NB:
                        scale_heads(c + 2)
                    gated_lo(c + 1, 0)
                    gated_lo(c + 1, 1)
                if c == 0:
                    gains(2)
                else:
                    norm_post(c - 1, c - 1, 4 + 2 * ((c - 1) % 2))
                    if c == NB - 1:
                        split_lo(G_UP[0])
                    norm_pre(NB + c - 1, c - 1)
            for n in range(1, 4):
                split_lo(G_UP[0] + n)
            norm_lo(2 * NB - 2, NB - 2, 4)
            norm_post(NB - 1, NB - 1, 6)
            norm_pre(2 * NB - 1, NB - 1)
            norm_lo(2 * NB - 1, NB - 1, 6)

            def ffn(l):
                up, down = G_UP[l], G_DOWN[l]

                def lo_pair(i, t):
                    for q in range(2):
                        s = (2 * t + q) % 4
                        dve.wait_ge(w_hi_done, i * 4 + (up + 2 * t + q + 1))
                        nc.vector.tensor_tensor(w_lo[:, 4 + s], raw[:, s], w_hi[:, 4 + s].bitcast(F32),
                                                ALU.subtract).then_inc(w_lo_done, 1)

                def conv(i, t):
                    f = i * 2 + t
                    n = l * FT + t + 1
                    dve.wait_ge(cv0, i * 2 + n)
                    nc.vector.scalar_tensor_tensor(cv[:, t, 1:], ps[:, 2 * t, 0:S - 1],
                                                   taps[l][:, 1, bass.ds(f, 1)], cv[:, t, 1:],
                                                   ALU.mult, ALU.add).then_inc(cv1, 1)
                    dve.wait_ge(cv1, i * 2 + n)
                    nc.vector.scalar_tensor_tensor(cv[:, t, 2:], ps[:, 2 * t, 0:S - 2],
                                                   taps[l][:, 0, bass.ds(f, 1)], cv[:, t, 2:],
                                                   ALU.mult, ALU.add).then_inc(cv2, 1)
                    dve.wait_ge(silu_done, i * 2 + n)
                    dve.wait_ge(w_used, i * 4 + counted(up + 2 * t + 1))
                    nc.vector.tensor_tensor(hid[:, bass.ds(f, 1)].rearrange("p a t -> p (a t)"),
                                            ps[:, 2 * t + 1], cv[:, t], ALU.mult).then_inc(hid_done, 1)

                with dve.Fori(0, FT // 2 - 1) as i:
                    conv(i, 0)
                    lo_pair(i, 2)
                    conv(i, 1)
                    lo_pair(i, 3)

                def lo_hid(n):
                    dve.wait_ge(hid_hi, l * FT + n + 1)
                    j = n - (FT - TAIL)
                    hi, lo = (act_hi[:, j], act_lo[:, j]) if j >= 0 else hid_pair[n]
                    nc.vector.tensor_tensor(lo, hid[:, n], hi.bitcast(F32),
                                            ALU.subtract).then_inc(hid_lo, 1)

                for j in range(2):
                    split_lo(down + j)
                for j in range(2):
                    lo_hid(j)
                conv(FT // 2 - 1, 0)
                conv(FT // 2 - 1, 1)
                with dve.Fori(0, (FT - TAIL) // 2 - 1) as i:
                    for j in range(2):
                        dve.wait_ge(w_hi_done, i * 2 + (down + 2 + j + 1))
                        nc.vector.tensor_tensor(w_lo[:, j], raw[:, j], w_hi[:, j].bitcast(F32),
                                                ALU.subtract).then_inc(w_lo_done, 1)
                        dve.wait_ge(hid_hi, i * 2 + (l * FT + 2 + j + 1))
                        nc.vector.tensor_tensor(hid_pair[j][1], hid[:, bass.ds(i * 2 + (2 + j), 1)]
                                                .rearrange("p a t -> p (a t)"),
                                                hid_pair[j][0].bitcast(F32),
                                                ALU.subtract).then_inc(hid_lo, 1)
                for n in range(FT - TAIL, FT):
                    split_lo(down + n)
                    lo_hid(n)

            def ffn_norms(l):
                gains(2 if l == 0 else 1)
                for b in range(NB):
                    norm_post((2 * l + 1) * NB + b, b, 2 * b)
                    if l == 0:
                        if b >= 1:
                            norm_lo(2 * NB + b - 1, b - 1, 2 * (b - 1))
                        norm_pre(2 * NB + b, b)
                        if b < 3:
                            split_lo(G_AIN + b)
                if l == 0:
                    norm_lo(3 * NB - 1, NB - 1, 2 * (NB - 1))

            ffn(0)
            ffn_norms(0)

            def add_a_bias(n):
                dve.wait_ge(w_used, counted(G_AIN + n))
                nc.vector.tensor_scalar([*[q_t[:, m] for m in range(KT)], k_t, v_t][n], ps[:, a_bank(n)],
                                        a_bias[:, n:n + 1], None, ALU.add).then_inc(pj_used, 1)

            for n in range(A_UNITS - 1):
                if n >= 2:
                    split_lo(G_AIN + n + 1)
                add_a_bias(n)

            def sink_cols(s):
                n = s % ASTEPS
                return sink[:, n * AG:(n + 1) * AG]

            def masked_max(s):
                b, blk = s % 2, s // ASTEPS
                lo = P if blk == 0 else 0
                dve.wait_ge(s_mm, s + 1)
                if s >= 2:
                    dve.wait_ge(pt_mm, s - 1)
                for j in range(AG):
                    ins = nc.vector.tensor_tensor_reduce(
                        out=sc[:, b, j, lo:], in0=ps[:, j // 2, (j % 2) * 2 * P + lo:(j % 2 + 1) * 2 * P],
                        in1=band[:, lo:], scale=DH ** -0.5, scalar=sink_cols(s)[:, j:j + 1],
                        op0=ALU.add, op1=ALU.max, accum_out=asm[:, b, 0, j:j + 1])
                link(ins)
                nc.vector.tensor_tensor(asm[:, b, 3], sink_cols(s), asm[:, b, 0], ALU.subtract)
                nc.vector.tensor_scalar(asm[:, b, 1], asm[:, b, 0], -1.0, None, ALU.mult)\
                    .then_inc(mx_done, 1)

            def inverse(s):
                b = s % 2
                dve.wait_ge(p_done, s + 1)
                link(nc.vector.tensor_tensor(asm[:, b, 4], asm[:, b, 2], asm[:, b, 3], ALU.add))
                nc.vector.reciprocal(asm[:, b, 5], asm[:, b, 4]).then_inc(inv_done, 1)

            def normalised(s):
                b, blk, n = s % 2, s // ASTEPS, s % ASTEPS
                dve.wait_ge(pv_mm, s + 1)
                dve.wait_ge(inv_done, s + 1)
                if n == 0 and blk >= 2:
                    dve.wait_ge(t_mm, turn_of("out", blk - 2, 1) + 1)
                o = o_tok[:, blk % 2].rearrange("p (h d) -> p h d", d=DH)[:, n * AG:(n + 1) * AG]
                nc.vector.tensor_tensor(
                    o, ps[:, 4, 0:AG * DH].rearrange("p (j d) -> p j d", j=AG),
                    asm[:, b, 5].unsqueeze(2).to_broadcast([P, AG, DH]), ALU.mult).then_inc(o_tok_done, 1)

            def turn_lo(b, half):
                n = turns_lo[0]
                turns_lo[0] += 1
                dve.wait_ge(t_hi, n + 1)
                at = (slice(None), slice(4 * half, 4 * half + 4), slice(b * P, (b + 1) * P))
                nc.vector.tensor_tensor(act_lo[at], ps[:, turn_bank(n)].rearrange("p (k t) -> p k t", t=P),
                                        act_hi[at].bitcast(F32), ALU.subtract).then_inc(t_lo, 1)

            turns_lo = [0]
            split_lo(G_AOUT)
            masked_max(0)
            split_lo(G_AOUT + 1)
            for s in range(AT_STEPS + 2):
                if s < AT_STEPS:
                    inverse(s)
                if s + 1 < AT_STEPS:
                    masked_max(s + 1)
                if s == 0:
                    add_a_bias(A_UNITS - 1)
                    dve.wait_ge(va_mm, 1)
                    nc.vector.tensor_copy(va[:].rearrange("p c f -> p (c f)"), ps[:, 4])\
                        .then_inc(va_done, 1)
                if 1 <= s <= AT_STEPS:
                    normalised(s - 1)
                for k in OUT_SPLITS.get(s, []):
                    split_lo(G_AOUT + k)
                if s == 1:
                    gains(2)
                for w in WORK[s]:
                    if w == ("turn", "norm", NB - 2, 0):
                        split_lo(G_UP[1])
                        split_lo(G_UP[1] + 1)
                    if w == ("post", NB - 1):
                        split_lo(G_UP[1] + 2)
                    if w[0] == "turn":
                        turn_lo(w[2], w[3])
                    elif w[0] == "y":
                        add_bias(w[1])
                    elif w[0] == "post":
                        norm_post(2 * NB + w[1], w[1], 6, biased=True)
                    elif w[0] == "pre":
                        norm_pre(3 * NB + w[1], w[1])

            split_lo(G_UP[1] + 3)
            ffn(1)
            ffn_norms(1)

        @block.tensor
        def _(pe):
            def three(dst, pairs):
                n = len(pairs)
                for i, (lh, ll, rh, rl) in enumerate(pairs):
                    nc.tensor.matmul(dst, lh, rh, start=(i == 0), stop=False)
                    nc.tensor.matmul(dst, lh, rl, start=False, stop=False)
                    last = nc.tensor.matmul(dst, ll, rh, start=False, stop=(i == n - 1))
                return last

            def project(slot, bank, lo=0, hi=S):
                uh, ul = unit(slot)
                return three(ps[:, bank, lo:hi],
                             [(uh[:, k], ul[:, k], act_hi[:, k, lo:hi], act_lo[:, k, lo:hi])
                              for k in range(KT)])

            def turn_norm(n, b, bank):
                pe.wait_ge(zn_done, n + 1)
                for k in range(KT):
                    ins = nc.tensor.transpose(ps[:, bank + k // 4, (k % 4) * P:(k % 4 + 1) * P],
                                              zn[:, b % 2, k * P:(k + 1) * P], ident[:])
                ins.then_inc(zt_done, 1)

            pe.wait_ge(pool_done, 8)
            turn_norm(0, 0, 0)
            turn_norm(1, 1, 2)

            def gate_or_qk(g, lo, hi):
                pe.wait_ge(z_lo, hi // P)
                pe.wait_ge(w_lo_done, counted(g))
                n = g - G_QK
                if n >= 2:
                    pe.wait_ge(pj_used, n - 1)
                ins = project(SLOT[g], 0 if g == G_GATE else 1 + n % 2, lo, hi)
                if hi == S:
                    ins.then_inc(w_used, 1)

            turn_norm(2, 2, 4)
            gate_or_qk(G_GATE, 0, 2 * P)
            gate_or_qk(G_QK, 0, 2 * P)
            turn_norm(3, 3, 6)
            gate_or_qk(G_GATE, 2 * P, S)
            gate_or_qk(G_QK, 2 * P, S)
            for n in range(1, QK_UNITS):
                gate_or_qk(G_QK + n, 0, S)
                if n == 4:
                    pe.wait_ge(vec_in, 16 * (6 + KVH))
                    for r, q in enumerate((4 * FT, 4 * FT, MH + A_UNITS)):
                        ins = nc.tensor.transpose(ps[:, 3, r * 4 * FT:r * 4 * FT + q], vec_rows[0:q, r],
                                                  ident[0:q, 0:q])
                    ins.then_inc(vec_mm, 1)

            def v_unit(n):
                g, half, kp = G_V + n, n // 4, n % 4
                s = SLOT[g]
                pe.wait_ge(w_lo_done, counted(g))
                for b in range(NB):
                    if half == 1 and kp == 0:
                        pe.wait_ge(v_done, b + 1)
                    bs = slice(b * P, (b + 1) * P)
                    for j in range(2):
                        k = 2 * kp + j
                        wh = w_hi[:, s, j * HALF:(j + 1) * HALF]
                        wl = w_lo[:, s, j * HALF:(j + 1) * HALF]
                        nc.tensor.matmul(ps[:, 4 + b], act_hi[:, k, bs], wh, start=(k == 0), stop=False)
                        nc.tensor.matmul(ps[:, 4 + b], act_hi[:, k, bs], wl, start=False, stop=False)
                        ins = nc.tensor.matmul(ps[:, 4 + b], act_lo[:, k, bs], wh, start=False,
                                               stop=(k == KT - 1))
                    if kp == 3 and b < NB - 1:
                        ins.then_inc(v_mm, 1)
                ins.then_inc(w_used, 1)

            v_unit(0)
            pe.wait_ge(row_act, 2)
            for c in range(NB):
                for q in range(4):
                    o0 = (c * 4 + q) * MH
                    ins = nc.tensor.transpose(ps[:, 0, o0:o0 + MH], rows[:, 4 + q, c * P:(c + 1) * P],
                                              ident[0:MH, 0:MH])
            ins.then_inc(tr_mm, 1)
            pe.wait_ge(dsel_done, 1)
            nc.tensor.matmul(ps[:, 3, 0:MH * NB], ones[0:MH, 0:1].to_broadcast([MH, P]), dsel[:].rearrange("p h c -> p (h c)"),
                             start=True, stop=True).then_inc(dec_mm, 1)
            v_unit(1)
            for n in range(2, V_UNITS):
                c = n - 2
                if c < NB:
                    if c >= 2:
                        pe.wait_ge(kw_done, c - 1)
                    else:
                        pe.wait_ge(pj_used, QK_UNITS)
                    for t in range(HG):
                        ins = nc.tensor.transpose(ps[:, 1 + c % 2, t * P:(t + 1) * P],
                                                  qk_t[:, HG + t, c * P:(c + 1) * P], ident[:])
                    ins.then_inc(kt_mm, 1)
                v_unit(n)

            def decays(s):
                c, g = s // 2, s % 2
                cs = slice(c * P, (c + 1) * P)
                if s >= 1:
                    pe.wait_ge(w_done, s)
                for t in range(HG):
                    hd = 2 * t + g
                    ins = nc.tensor.matmul(ps[:, 0, t * P:(t + 1) * P],
                                           ident[0:MH, hd:hd + 1].to_broadcast([MH, P]),
                                           u_rows[:, cs], start=True, stop=True)
                ins.then_inc(u_mm, 1)
                pr = slice(g * DK, (g + 1) * DK)
                for t in range(HG):
                    ins = nc.tensor.matmul(ps[:, 1, t * P:(t + 1) * P], qk_t[pr, HG + t, cs],
                                           qk_t[pr, t, cs], start=True, stop=True)
                ins.then_inc(st_mm, 1)

            def combine(s):
                c, g = s // 2, s % 2
                cs = slice(c * P, (c + 1) * P)
                pr = slice(g * DK, (g + 1) * DK)
                if s >= 1:
                    pe.wait_ge(num_done, s)
                    k = min(s, NS - 2)
                    pe.wait_ge(c_done, k)
                if c > 0:
                    for t in range(HG):
                        nc.tensor.matmul(ps[:, 3, t * P:(t + 1) * P], qk_t[pr, t, cs], C[pr, t, 0:DV],
                                         start=True, stop=True)
                        nc.tensor.matmul(ps[:, 5, 4 + t:5 + t], qk_t[pr, t, cs], C[pr, t, DV:DV + 1],
                                         start=True, stop=True)
                if c < NB - 1:
                    for t in range(HG):
                        hd = 2 * t + g
                        kws = kw[:, c, hd * DK:(hd + 1) * DK]
                        nc.tensor.matmul(ps[pr, 4, t * P:(t + 1) * P], kws,
                                         v_tok[:, c, hd * DV:(hd + 1) * DV], start=True, stop=True)
                        nc.tensor.matmul(ps[pr, 5, 8 + t:9 + t], kws, ones[:, 0:1], start=True, stop=True)
                pe.wait_ge(w_done, s + 1)
                for t in range(HG):
                    hd = 2 * t + g
                    nc.tensor.matmul(ps[:, 2, t * P:(t + 1) * P], ew[:, s % 2, t],
                                     v_tok[:, c, hd * DV:(hd + 1) * DV], start=True, stop=True)
                    ins = nc.tensor.matmul(ps[:, 5, t:t + 1], ew[:, s % 2, t], ones[:, 0:1], start=True,
                                           stop=True)
                ins.then_inc(n_mm, 1)

            def turn_heads(c):
                bank = 2 * (c % 2)
                pe.wait_ge(hs_done, c + 1)
                if c == 1:
                    pe.wait_ge(num_done, NS)
                if c >= 2:
                    pe.wait_ge(gated_done, 2 * (c - 1))
                for k in range(KT):
                    ins = nc.tensor.transpose(ps[:, bank + k // 4, (k % 4) * P:(k % 4 + 1) * P],
                                              v_tok[:, c, k * P:(k + 1) * P], ident[:])
                ins.then_inc(ht_mm, 1)

            pe.wait_ge(kw_done, NB)
            pe.wait_ge(gt_done, 1)
            pe.wait_ge(v_done, 2 * NB)
            decays(0)
            for s in range(NS):
                g = G_O + s
                pe.wait_ge(w_lo_done, counted(g))
                if s >= 2:
                    pe.wait_ge(o_tanh, s - 1)
                if s < NS - 1:
                    project(SLOT[g], 6 + s % 2).then_inc(w_used, 1)
                    combine(s)
                    decays(s + 1)
                else:
                    project(SLOT[g], 6 + s % 2, 0, S // 2)
                    combine(s)
                    turn_heads(0)
                    project(SLOT[g], 6 + s % 2, S // 2, S).then_inc(w_used, 1)

            def out_part(c, bank, g0, ks, last):
                cs = slice(c * P, (c + 1) * P)
                for k in ks:
                    s = SLOT[g0 + k]
                    for half in range(2):
                        hs = slice(half * HALF, (half + 1) * HALF)
                        dst = ps[:, bank + half]
                        nc.tensor.matmul(dst, act_hi[:, k, cs], w_hi[:, s, hs], start=(k == 0), stop=False)
                        nc.tensor.matmul(dst, act_hi[:, k, cs], w_lo[:, s, hs], start=False, stop=False)
                        ins = nc.tensor.matmul(dst, act_lo[:, k, cs], w_hi[:, s, hs], start=False,
                                               stop=(k == KT - 1))
                    if last:
                        ins.then_inc(w_used, 1)
                if not last and k == KT - 1:
                    ins.then_inc(y_done, 1)

            def out_block(c, bank, ks):
                for k in ks:
                    pe.wait_ge(op_lo, 2 * c + k // 4 + 1)
                    pe.wait_ge(w_lo_done, counted(G_MOUT + k))
                    out_part(c, bank, G_MOUT, [k], c == NB - 1)

            for c in range(NB):
                if c + 1 < NB:
                    turn_heads(c + 1)
                if c >= 2:
                    pe.wait_ge(z_lo, NB + c - 1)
                bank = 4 + 2 * (c % 2)
                out_block(c, bank, range(6))
                if c >= 1:
                    turn_norm(NB + c - 1, c - 1, 10 - bank)
                out_block(c, bank, range(6, KT))

            def ffn(l, blocks_done, turn_last):
                up, down = G_UP[l], G_DOWN[l]
                READY = (NB - 1) * P
                blocks_done(NB - 1)
                for n in range(3):
                    pe.wait_ge(w_lo_done, counted(up + n))
                    project(4 + n, n, 0, READY)
                    if n == 1:
                        turn_last()
                blocks_done(NB)
                for n in range(4):
                    pe.wait_ge(w_lo_done, counted(up + n))
                    project(4 + n, n, READY if n < 3 else 0, S).then_inc(w_used, 1)
                with pe.Fori(1, FT // 2) as i:
                    for t in range(2):
                        pe.wait_ge(hid_done, i * 2 + (l * FT + t + 1))
                        pe.wait_ge(w_lo_done, i * 4 + counted(up + 2 * t))
                        project(4 + 2 * t, 2 * t).then_inc(w_used, 1)
                        pe.wait_ge(w_lo_done, i * 4 + counted(up + 2 * t + 1))
                        project(5 + 2 * t, 2 * t + 1).then_inc(w_used, 1)

                def down_part(s, pair, b, half, start, stop):
                    bs = slice(b * P, (b + 1) * P)
                    hs = slice(half * HALF, (half + 1) * HALF)
                    dst = ps[:, 2 * b + half]
                    hi, lo = pair
                    nc.tensor.matmul(dst, hi[:, bs], w_hi[:, s, hs], start=start, stop=False)
                    nc.tensor.matmul(dst, hi[:, bs], w_lo[:, s, hs], start=False, stop=False)
                    return nc.tensor.matmul(dst, lo[:, bs], w_hi[:, s, hs], start=False, stop=stop)

                for j in range(2):
                    pe.wait_ge(w_lo_done, counted(down + j))
                    pe.wait_ge(hid_lo, l * FT + j + 1)
                    for b in (2, 3, 0, 1):
                        if j == 0 and b < 2:
                            pe.wait_ge(hid_done, (l + 1) * FT + 1 + b)
                        for half in range(2):
                            ins = down_part(j, hid_pair[j], b, half, j == 0, False)
                    ins.then_inc(w_used, 1)
                with pe.Fori(0, (FT - TAIL) // 2 - 1) as i:
                    for j in range(2):
                        pe.wait_ge(w_lo_done, i * 2 + counted(down + 2 + j))
                        pe.wait_ge(hid_lo, i * 2 + (l * FT + 2 + j + 1))
                        for b in range(NB):
                            for half in range(2):
                                ins = down_part(j, hid_pair[j], b, half, False, False)
                        ins.then_inc(w_used, 1)
                for b in range(NB):
                    for s in range(TAIL):
                        if b == 0:
                            n = FT - TAIL + s
                            pe.wait_ge(w_lo_done, counted(down + n))
                            pe.wait_ge(hid_lo, l * FT + n + 1)
                        for half in range(2):
                            ins = down_part(4 + s, (act_hi[:, s], act_lo[:, s]), b, half, False,
                                            s == TAIL - 1)
                        if b == NB - 1:
                            ins.then_inc(w_used, 1)
                        if s == 1 and b >= 2 and l == 0:
                            turn_norm(2 * NB + b - 2, b - 2, 2 * (b - 2))
                    if b < NB - 1:
                        ins.then_inc(y_done, 1)

            def norm_blocks(n):
                pe.wait_ge(z_lo, NB + n)

            ffn(0, norm_blocks, lambda: turn_norm(2 * NB - 1, NB - 1, 6))

            for n, lo, hi in [(0, 0, 2 * P), (1, 0, 2 * P), (2, 0, 3 * P), (0, 2 * P, S),
                              (1, 2 * P, S), (2, 3 * P, S)] + [(n, 0, S) for n in range(3, A_UNITS - 1)]:
                g = G_AIN + n
                pe.wait_ge(z_lo, 2 * NB + hi // P)
                pe.wait_ge(w_lo_done, counted(g))
                if n >= 3:
                    pe.wait_ge(pj_used, QK_UNITS + n - 2)
                ins = project(SLOT[g], a_bank(n), lo, hi)
                if hi == S:
                    ins.then_inc(w_used, 1)
                elif n < 2:
                    turn_norm(2 * NB + 2 + n, 2 + n, 4 + 2 * n)

            def turn_values():
                pe.wait_ge(pj_used, QK_UNITS + A_UNITS)
                for c in range(NB):
                    ins = nc.tensor.transpose(ps[:, 4, c * P:(c + 1) * P], v_t[:, c * P:(c + 1) * P],
                                              ident[:])
                ins.then_inc(va_mm, 1)

            def scores(s):
                blk, n = s // ASTEPS, s % ASTEPS
                g = n * AG // KT
                pr = slice(g * DH, (g + 1) * DH)
                if s >= 1:
                    pe.wait_ge(mx_done, s)
                else:
                    pe.wait_ge(pj_used, QK_UNITS + A_UNITS - 1)
                lo = P if blk == 0 else 0
                for j in range(AG):
                    t = (n * AG + j) % KT
                    dst = ps[:, j // 2, (j % 2) * 2 * P + lo:(j % 2 + 1) * 2 * P]
                    ins = nc.tensor.matmul(dst, q_t[pr, t, blk * P:(blk + 1) * P],
                                           k_t[pr, (blk - 1) * P + lo:(blk + 1) * P], start=True, stop=True)
                ins.then_inc(s_mm, 1)

            def turn_probs(s):
                b, blk = s % 2, s // ASTEPS
                pe.wait_ge(p_done, s + 1)
                if s >= 1:
                    pe.wait_ge(pt_done, s)
                for j in range(AG):
                    for kb in range(1 if blk == 0 else 0, 2):
                        ins = nc.tensor.transpose(ps[:, 2 + j // 2, ((j % 2) * 2 + kb) * P:
                                                     ((j % 2) * 2 + kb + 1) * P],
                                                  sc[:, b, j, kb * P:(kb + 1) * P], ident[:])
                ins.then_inc(pt_mm, 1)

            def mix(s):
                b, blk, n = s % 2, s // ASTEPS, s % ASTEPS
                g = n * AG // KT
                pe.wait_ge(pt_done, s + 1)
                if s >= 1:
                    pe.wait_ge(o_tok_done, s)
                else:
                    pe.wait_ge(va_done, 1)
                for j in range(AG):
                    for kb in range(1 if blk == 0 else 0, 2):
                        ins = nc.tensor.matmul(ps[:, 4, j * DH:(j + 1) * DH],
                                               p_t[:, b, j, kb * P:(kb + 1) * P],
                                               va[:, blk - 1 + kb, g * DH:(g + 1) * DH],
                                               start=(kb == 0 or blk == 0), stop=(kb == 1))
                ins.then_inc(pv_mm, 1)

            def turn(what, b, half):
                n = turn_of(what, b, half)
                if what == "out":
                    pe.wait_ge(o_tok_done, (b + 1) * ASTEPS)
                else:
                    pe.wait_ge(zn_done, 3 * NB + b + 1)
                free = [q for q in range(n) if turn_bank(q) == turn_bank(n)]
                if free:
                    pe.wait_ge(t_lo, free[-1] + 1)
                src = o_tok[:, b % 2] if what == "out" else zn[:, b % 2]
                for k in range(4):
                    ins = nc.tensor.transpose(ps[:, turn_bank(n), k * P:(k + 1) * P],
                                              src[:, (4 * half + k) * P:(4 * half + k + 1) * P], ident[:])
                ins.then_inc(t_mm, 1)

            def project_values(half):
                g = G_AIN + A_UNITS - 1
                if half == 0:
                    pe.wait_ge(w_lo_done, counted(g))
                ins = project(SLOT[g], 5, half * S // 2, (half + 1) * S // 2)
                if half == 1:
                    ins.then_inc(w_used, 1)

            scores(0)
            project_values(0)
            for s in range(AT_STEPS + 2):
                if s + 1 < AT_STEPS:
                    scores(s + 1)
                if 1 <= s <= AT_STEPS:
                    mix(s - 1)
                for w in WORK[s]:
                    if w[0] == "turn" and w not in LAST:
                        turn(*w[1:])
                    if w[0] == "out":
                        b, q = w[1], w[2]
                        pe.wait_ge(t_lo, turn_of("out", b, q // 2) + 1)
                        if q == 0:
                            if b == 0:
                                pe.wait_ge(w_lo_done, counted(G_AOUT + KT - 1))
                            else:
                                pe.wait_ge(yb_done, b)
                        out_part(b, 6, G_AOUT, range(2 * q, 2 * q + 2), b == NB - 1)
                if s == 0:
                    project_values(1)
                if s < AT_STEPS:
                    turn_probs(s)
                if s == 0:
                    turn_values()

            def turned_blocks(n):
                pe.wait_ge(t_lo, len(TURNS) - 2 * (NB - n))

            ffn(1, turned_blocks, lambda: [turn(*w[1:]) for w in LAST])


_INS = ["x", "m_w_in", "m_gate_bias", "m_head_norm", "m_w_out", "a_w_in", "a_b_in", "a_sinks",
        "a_w_out", "a_b_out", "norm_mix_pre", "norm_mix_post", "norm_ffn_pre", "norm_ffn_post",
        "f_w_up", "f_conv_w", "f_conv_b", "f_w_down"]


def kernel(**inputs):
    import numpy as np
    import concourse.bacc as bacc
    from concourse.bass_utils import run_bass_kernel_spmd

    nc = bacc.Bacc("TRN2", target_bir_lowering=False, num_devices=1)
    arrays, args = {}, []
    for name in _INS:
        a = np.ascontiguousarray(inputs[name])
        arrays[f"in_{name}"] = a
        args.append(nc.dram_tensor(f"in_{name}", a.shape, mybir.dt.from_np(a.dtype),
                                   kind="ExternalInput").ap())
    shape = inputs["x"].shape
    out = nc.dram_tensor("out", shape, F32, kind="ExternalOutput").ap()
    trunk(nc, *args, out)
    r = run_bass_kernel_spmd(nc, [arrays], core_ids=[0])
    return r.results[0]["out"]
```

```python
from contextlib import ExitStack

import concourse.bass as bass
from concourse import mybir

F32 = mybir.dt.float32
F32R = mybir.dt.float32r
BF16 = mybir.dt.bfloat16
ALU = mybir.AluOpType
ACT = mybir.ActivationFunctionType

P = 128
EPS = 1e-6
GATE_CAP = 15.0
MASKED = -1.0e30
LN_EXP_SET = "natural_log_exp_and_others"
EXP_TANH_SET = "exp_and_others"
CREDIT = 4


def trunk(nc, x, m_w_in, m_gate_bias, m_head_norm, m_w_out, a_w_in, a_b_in, a_sinks, a_w_out,
          a_b_out, norm_mix_pre, norm_mix_post, norm_ffn_pre, norm_ffn_post, f_w_up, f_conv_w,
          f_conv_b, f_w_down, out):
    S, D = x.shape[1], x.shape[2]
    NB = S // P
    KT = D // P
    FF = f_w_down.shape[1]
    FT = FF // P
    MH = m_gate_bias.shape[2]
    DK, DV = D // (2 * MH), D // MH
    DH = 64
    QH = a_sinks.shape[1]
    KVH = (a_w_in.shape[2] // DH - QH) // 2
    HALF = 512
    ROWS = 2 * MH
    NS = 2 * NB
    HG = MH // 2
    AG = 4
    ASTEPS = QH // AG
    assert NB == 4 and KT == 8 and FT == 22 and MH == 8 and DV == P and DK == 64 and KVH == 2

    QK_UNITS, V_UNITS, O_UNITS = 2 * MH * DK // P, MH * DV * D // (P * D), D // P
    TAIL = 4
    G_GATE = 0
    G_QK = 1
    G_V = G_QK + QK_UNITS
    G_O = G_V + V_UNITS
    G_MOUT = G_O + O_UNITS
    G_UP = [G_MOUT + KT, 0]
    G_DOWN = [G_UP[0] + 2 * FT, 0]
    G_AIN = G_DOWN[0] + FT
    A_UNITS = (QH + 2 * KVH) * DH // P
    A_TILE = [0, 1, 2, 3, KT, KT + 1, 4, 5, 6, 7]
    G_AOUT = G_AIN + A_UNITS
    G_UP[1] = G_AOUT + KT
    G_DOWN[1] = G_UP[1] + 2 * FT
    SLOT = [7] + [n % 4 for n in range(QK_UNITS + V_UNITS + O_UNITS)]
    FFN_SLOTS = [4 + n % 4 for n in range(2 * FT)] + [n % 2 for n in range(FT - TAIL)]
    FFN_SLOTS += list(range(4, 4 + TAIL))
    SLOT += [(k + 4) % 8 for k in range(KT)] + FFN_SLOTS
    SLOT += [n % 4 for n in range(A_UNITS)] + [4, 5, 6, 7, 2, 3, 0, 1] + FFN_SLOTS

    DMAS = [1] * len(SLOT)
    for q in [G_GATE] + [G_AIN + n for n in range(A_UNITS) if A_TILE[n] < KT]:
        DMAS[q] = 2

    def landed(g):
        return 16 * sum(DMAS[q] for q in range(g + 1) if SLOT[q] % 4 == SLOT[g] % 4)

    def freed(g):
        users = [q for q in range(g) if SLOT[q] == SLOT[g]]
        if SLOT[g] == 2 and g > G_DOWN[0]:
            users.append(G_DOWN[0] + FT - TAIL - 1)
        return counted(max(users, default=-1))

    def counted(g):
        return g + 1 + CREDIT

    with ExitStack() as ctx:
        def sb(name, shape, dt=F32):
            return ctx.enter_context(nc.sbuf_tensor(name, shape, dt))

        def sem(name):
            return ctx.enter_context(nc.semaphore(name))

        ps = ctx.enter_context(nc.psum_tensor("ps", [P, 8, HALF], F32))

        raw = sb("raw", [P, 4, D])
        w_hi = sb("w_hi", [P, 8, D], F32R)
        w_lo = sb("w_lo", [P, 8, D], F32R)
        act_hi = sb("act_hi", [P, KT, S], F32R)
        act_lo = sb("act_lo", [P, KT, S], F32R)
        h = sb("h", [P, NB, D])
        g_post = sb("g_post", [P, D])
        g_pre = sb("g_pre", [P, D])
        arena = sb("arena", [P, 64 * 256 + 40])
        KB = 256

        ident = sb("ident", [P, P])
        causal = sb("causal", [P, P])
        ones = sb("ones", [P, 1])
        band = sb("band", [P, 2 * P])
        u_rows = sb("u_rows", [MH, S])
        junk = sb("junk", [P, HG, P], BF16)
        stat = sb("stat", [P, 2, 4])
        eps_col = sb("eps_col", [P, 1])
        VECS = 2 * 4 * FT + MH + A_UNITS
        vecs = sb("vecs", [P, VECS])
        taps = [vecs[:, l * 4 * FT:(l + 1) * 4 * FT].rearrange("p (j f) -> p j f", j=4) for l in range(2)]
        head_norm = vecs[:, 8 * FT:8 * FT + MH]
        a_bias = vecs[:, 8 * FT + MH:VECS]
        gate_b = sb("gate_b", [P, 2])
        hn_half = sb("hn_half", [P, MH])
        gt = sb("gt", [P, NB, 4, MH])
        dm = sb("dm", [P, NB, MH])
        s2 = sb("s2", [P, NB, MH])
        fac = sb("fac", [P, 3, NB * MH])
        dtmp = sb("dtmp", [P, HG])
        decay_all = sb("decay_all", [P, MH, NB])
        decay = sb("decay", [MH, 3, NB])
        dsel = sb("dsel", [MH, MH, NB])
        sink = sb("sink", [P, QH])
        asm = sb("asm", [P, 2, 6, AG])

        DV1 = DV + 1
        V = NB * MH * DV1
        v_tok = arena[:, 0:V].rearrange("p (c h v) -> p c h v", c=NB, h=MH)
        o_sig = arena[:, V:V + 16 * KB].rearrange("p (k t) -> p k t", k=KT)
        rows = arena[0:MH, V:V + 16 * KB].rearrange("p (r t) -> p r t", r=8)
        zrow = rows[:, 5]
        Q = V + 16 * KB
        qk_t = arena[:, Q:Q + 16 * KB].rearrange("p (k t) -> p k t", k=QK_UNITS)
        gated = arena[:, Q:Q + 4 * KB].rearrange("p (k t) -> p k t", k=KT)
        K = Q + 16 * KB
        kw = arena[:, K:K + 8 * KB].rearrange("p (c f) -> p c f", c=NB)
        E = K + 8 * KB
        ew = arena[:, E:E + 4 * KB].rearrange("p (b t q) -> p b t q", b=2, t=HG)
        I = E + 4 * KB
        vec_rows = arena[:, I:I + 3 * P].rearrange("p (r f) -> p r f", r=3)
        itmp = arena[:, I:I + HG * DV1].rearrange("p (t q) -> p t q", t=HG)
        C = arena[:, I + HG * DV1:I + 2 * HG * DV1].rearrange("p (t q) -> p t q", t=HG)
        q_t = arena[:, 0:16 * KB].rearrange("p (k t) -> p k t", k=KT)
        k_t = arena[:, 16 * KB:18 * KB]
        v_t = arena[:, 18 * KB:20 * KB]
        va = arena[:, 20 * KB:22 * KB].rearrange("p (c f) -> p c f", c=NB)
        sc = arena[:, 22 * KB:30 * KB].rearrange("p (b j k) -> p b j k", b=2, j=AG)
        p_t = arena[:, 30 * KB:38 * KB].rearrange("p (b j k) -> p b j k", b=2, j=AG)
        o_tok = arena[:, 38 * KB:46 * KB].rearrange("p (b f) -> p b f", b=2)
        b_out = arena[:, 60 * KB:64 * KB]
        hid = arena[:, 0:44 * KB].rearrange("p (f t) -> p f t", f=FT)
        cv = arena[:, 44 * KB:48 * KB].rearrange("p (b t) -> p b t", b=2)
        tmp = arena[:, 48 * KB:52 * KB]
        zn = arena[:, 52 * KB:60 * KB].rearrange("p (b f) -> p b f", b=2)
        hid_pair = [[w[:, 2, j * HALF:(j + 1) * HALF] for w in (w_hi, w_lo)] for j in range(2)]

        raw_in = [sem(f"raw_in{i}") for i in range(4)]
        w_hi_done, w_lo_done, w_used = sem("w_hi_done"), sem("w_lo_done"), sem("w_used")
        x_in = [sem(f"x_in{i}") for i in range(NB)]
        gain_in = sem("gain_in")
        vec_in, const_in, bout_in = sem("vec_in"), sem("const_in"), sem("bout_in")
        vec_mm, vec_done = sem("vec_mm"), sem("vec_done")
        out_done = sem("out_done")
        pool_done = sem("pool_done")
        act_chain, dve_chain = sem("act_chain"), sem("dve_chain")
        y_done, rs_post, rs_pre = sem("y_done"), sem("rs_post"), sem("rs_pre")
        yb_done, h_done = sem("yb_done"), sem("h_done")
        zn_done, zt_done, z_hi, z_lo = sem("zn_done"), sem("zt_done"), sem("z_hi"), sem("z_lo")
        cv0, cv1, cv2 = (sem(n) for n in ("cv0", "cv1", "cv2"))
        silu_done, hid_done = sem("silu_done"), sem("hid_done")
        hid_hi, hid_lo = sem("hid_hi"), sem("hid_lo")
        pj_used = sem("pj_used")
        tr_mm, gt_done, dsel_done, dec_mm, kt_mm, kw_done = (
            sem(n) for n in ("tr_mm", "gt_done", "dsel_done", "dec_mm", "kt_mm", "kw_done"))
        v_mm, v_done = sem("v_mm"), sem("v_done")
        row_ready = sem("row_ready")
        row_act = sem("row_act")
        u_mm, e_raw, e_exp, st_mm, w_done, n_mm, num_done, c_done, sq_done = (
            sem(n) for n in ("u_mm", "e_raw", "e_exp", "st_mm", "w_done", "n_mm", "num_done",
                             "c_done", "sq_done"))
        o_tanh, o_done = sem("o_tanh"), sem("o_done")
        fac_dve, fac_act = sem("fac_dve"), sem("fac_act")
        hs_done, ht_mm, gated_done, op_hi, op_lo = (
            sem(n) for n in ("hs_done", "ht_mm", "gated_done", "op_hi", "op_lo"))
        va_mm, va_done, s_mm, mx_done, p_done, pt_mm, pt_done, pv_mm, o_tok_done = (
            sem(n) for n in ("va_mm", "va_done", "s_mm", "mx_done", "p_done", "pt_mm", "pt_done",
                             "pv_mm", "o_tok_done"))
        qb_mm = sem("qb_mm")
        t_mm, t_hi, t_lo, inv_done = sem("t_mm"), sem("t_hi"), sem("t_lo"), sem("inv_done")

        def values(half, b):
            return (w_used, counted(G_V + 4 * half + 3)) if b == NB - 1 else (v_mm, 3 * half + b + 1)

        def products(n):
            last = [G_MOUT + KT, G_DOWN[0] + FT, G_AOUT + KT, G_DOWN[1] + FT][n // NB] - 1
            return (w_used, counted(last)) if n % NB == NB - 1 else (y_done, n - n // NB + 1)

        def block_work(s):
            c, i = s // ASTEPS, s % ASTEPS
            if c < NB:
                return {0: [("out", c - 2, 3), ("y", c - 2), ("turn", "out", c - 1, 0)],
                        1: [("out", c - 1, 0), ("post", c - 2), ("turn", "out", c - 1, 1)],
                        2: [("out", c - 1, 1), ("pre", c - 2), ("turn", "norm", c - 2, 0)],
                        3: [("out", c - 1, 2), ("turn", "norm", c - 2, 1)]}[i]
            if i == 0:
                return [("out", NB - 2, 3), ("y", NB - 2), ("turn", "out", NB - 1, 0),
                        ("turn", "out", NB - 1, 1)]
            return [("out", NB - 1, 0), ("out", NB - 1, 1), ("post", NB - 2), ("out", NB - 1, 2),
                    ("pre", NB - 2), ("turn", "norm", NB - 2, 0), ("turn", "norm", NB - 2, 1),
                    ("out", NB - 1, 3), ("y", NB - 1), ("post", NB - 1), ("pre", NB - 1),
                    ("turn", "norm", NB - 1, 0), ("turn", "norm", NB - 1, 1)]

        AT_STEPS = NB * ASTEPS
        WORK = [[w for w in block_work(s) if w[2 if w[0] == "turn" else 1] >= 0]
                for s in range(AT_STEPS + 2)]
        TURNS = [w for ws in WORK for w in ws if w[0] == "turn"]

        def turn_of(what, b, half):
            return TURNS.index(("turn", what, b, half))

        def turn_bank(n):
            return 5 if n < len(TURNS) - 6 else n - (len(TURNS) - 6)

        def head(bank, place, t, pr=slice(None)):
            bank, t = (bank, t) if t < HG - 1 else (5, place)
            return ps[pr, bank, t * DV1:(t + 1) * DV1]

        def heads(bank, place, pr=slice(None)):
            three = ps[pr, bank, 0:(HG - 1) * DV1].rearrange("p (t v) -> p t v", v=DV1)
            last = head(bank, place, HG - 1, pr).unsqueeze(1)
            return [(slice(0, HG - 1), three), (slice(HG - 1, HG), last)]

        def a_bank(n):
            return (0, 1, 2, 3, 2, 3, 5, 6, 7, 5)[n]

        GROUPS = [0, 2, 1, 3]

        OUT_SPLITS = {0: [0, 1], 1: [2], 2: [3], 3: [4], 4: [5], 5: [6], 6: [7]}
        LAST = TURNS[-2:]

        def unit(slot):
            return (w_hi[:, slot].rearrange("p (k c) -> p k c", k=KT),
                    w_lo[:, slot].rearrange("p (k c) -> p k c", k=KT))

        block = ctx.enter_context(nc.Block())

        @block.sync
        def _(sp):
            def load(g, src, dst=None):
                s = SLOT[g] % 4
                dst = raw[:, s] if dst is None else dst
                nc.sync.dma_start(dst, src).then_inc(raw_in[s], 16)

            def load_free(g):
                last = [q for q in range(g) if SLOT[q] % 4 == SLOT[g] % 4]
                if last:
                    sp.wait_ge(w_lo_done, counted(last[-1]))

            def gains(post, pre):
                if post is not None:
                    nc.sync.dma_start(g_post[:], post.partition_broadcast(P)).then_inc(gain_in, 16)
                if pre is not None:
                    nc.sync.dma_start(g_pre[:], pre.partition_broadcast(P)).then_inc(gain_in, 16)

            for b in range(NB):
                nc.sync.dma_start(h[:, b], x[0, b * P:(b + 1) * P]).then_inc(x_in[b], 16)
                if b == 0:
                    gains(None, norm_mix_pre[0])
                if b == 1:
                    w_k = m_w_in[0].rearrange("(k p) n -> p k n", p=P)
                    wg = raw[:, 3].rearrange("p (k c) -> p k c", k=KT)
                    GC = m_w_in.shape[2] - ROWS
                    sp.wait_ge(pool_done, 1)
                    nc.sync.dma_start(wg[:, :, 0:MH], w_k[:, :, GC:GC + MH]).then_inc(raw_in[3], 16)
                    nc.sync.dma_start(wg[:, :, 32:32 + MH],
                                      w_k[:, :, GC + MH:GC + ROWS]).then_inc(raw_in[3], 16)
            w_in = m_w_in[0]

            def load_qk(n):
                load_free(G_QK + n)
                load(G_QK + n, w_k[:, :, n * P:(n + 1) * P],
                     raw[:, SLOT[G_QK + n] % 4].rearrange("p (k c) -> p k c", k=KT))

            for n in range(3):
                load_qk(n)
            for j in range(2):
                nc.sync.dma_start(gate_b[32 * j:32 * j + MH, 0:1],
                                  m_gate_bias[0, j:j + 1].rearrange("a h -> h a"),
                                  allow_slow_non_contiguous=True).then_inc(const_in, 16)
            nc.sync.dma_start(sink[:], a_sinks[0].partition_broadcast(P)).then_inc(const_in, 16)
            load_qk(3)
            for l in range(2):
                nc.sync.dma_start(vec_rows[0:3 * FT, l],
                                  f_conv_w[l].rearrange("j (f p) -> (j f) p", p=P))\
                    .then_inc(vec_in, 16)
                nc.sync.dma_start(vec_rows[3 * FT:4 * FT, l],
                                  f_conv_b[l].rearrange("(f p) -> f p", p=P)).then_inc(vec_in, 16)
            nc.sync.dma_start(vec_rows[0:MH, 2], m_head_norm[0].rearrange("(h p) -> h p", p=P))\
                .then_inc(vec_in, 16)
            for j in range(KVH):
                nc.sync.dma_start(
                    vec_rows[MH:MH + KT, 2, j * DH:(j + 1) * DH],
                    a_b_in[0, j * D // 2:(j + 1) * D // 2].rearrange("(t d) -> t d", d=DH))\
                    .then_inc(vec_in, 16)
            nc.sync.dma_start(vec_rows[MH + KT:MH + A_UNITS, 2],
                              a_b_in[0, QH * DH:].rearrange("(c p) -> c p", p=P))\
                .then_inc(vec_in, 16)
            for n in range(4, QK_UNITS):
                load_qk(n)
            VC = 2 * MH * DK
            for n in range(V_UNITS):
                half, kp = n // 4, n % 4
                load_free(G_V + n)
                load(G_V + n, w_k[:, 2 * kp:2 * kp + 2, VC + half * HALF:VC + (half + 1) * HALF],
                     raw[:, SLOT[G_V + n] % 4].rearrange("p (k c) -> p k c", k=2))
            OC = VC + MH * DV
            for n in range(O_UNITS):
                load_free(G_O + n)
                load(G_O + n, w_k[:, :, OC + n * P:OC + (n + 1) * P],
                     raw[:, SLOT[G_O + n] % 4].rearrange("p (k c) -> p k c", k=KT))
            sp.wait_ge(zn_done, NB)
            gains(norm_mix_post[0], norm_ffn_pre[0])
            for k in range(KT):
                load_free(G_MOUT + k)
                load(G_MOUT + k, m_w_out[0, k * P:(k + 1) * P])

            def ffn_loads(l):
                up, down = G_UP[l], G_DOWN[l]
                w_up = f_w_up[l].rearrange("(k p) n -> p k n", p=P)
                for j in range(4):
                    load_free(up + j)
                    tile = FT * (j % 2) + j // 2
                    load(up + j, w_up[:, :, tile * P:(tile + 1) * P],
                         raw[:, j].rearrange("p (k c) -> p k c", k=KT))
                with sp.Fori(1, FT // 2) as i:
                    for j in range(4):
                        sp.wait_ge(w_lo_done, i * 4 + counted(up + j - 4))
                        tile = i * 2 + (FT * (j % 2) + j // 2)
                        nc.sync.dma_start(raw[:, j].rearrange("p (k c) -> p k c", k=KT),
                                          w_up[:, :, bass.ds(tile * P, P)]).then_inc(raw_in[j], 16)
                for j in range(2):
                    load_free(down + j)
                    load(down + j, f_w_down[l, j * P:(j + 1) * P])
                with sp.Fori(1, (FT - TAIL) // 2) as i:
                    for j in range(2):
                        sp.wait_ge(w_lo_done, i * 2 + counted(down + j - 2))
                        nc.sync.dma_start(raw[:, j], f_w_down[l, bass.ds(i * (2 * P) + j * P, P)])\
                            .then_inc(raw_in[j], 16)
                for n in range(FT - TAIL, FT):
                    load_free(down + n)
                    load(down + n, f_w_down[l, n * P:(n + 1) * P])

            ffn_loads(0)
            sp.wait_ge(zn_done, 2 * NB)
            gains(norm_ffn_post[0], norm_mix_pre[1])
            wa = a_w_in[0].rearrange("(k p) n -> p k n", p=P)
            for n in range(A_UNITS):
                load_free(G_AIN + n)
                dst = raw[:, SLOT[G_AIN + n] % 4].rearrange("p (k c) -> p k c", k=KT)
                t = A_TILE[n]
                if t < KT:
                    s = SLOT[G_AIN + n] % 4
                    for j in range(KVH):
                        c0 = (t + 8 * j) * DH
                        nc.sync.dma_start(dst[:, :, j * DH:(j + 1) * DH], wa[:, :, c0:c0 + DH])\
                            .then_inc(raw_in[s], 16)
                else:
                    load(G_AIN + n, wa[:, :, t * P:(t + 1) * P], dst)
            sp.wait_ge(zn_done, 3 * NB)
            gains(norm_mix_post[1], norm_ffn_pre[1])
            nc.sync.dma_start(b_out, a_b_out[0].partition_broadcast(P)).then_inc(bout_in, 16)
            for k in range(KT):
                load_free(G_AOUT + k)
                load(G_AOUT + k, a_w_out[0, k * P:(k + 1) * P])
            ffn_loads(1)
            sp.wait_ge(zn_done, 4 * NB)
            gains(norm_ffn_post[1], None)
            for b in range(NB):
                for half in range(2 if b == NB - 1 else 1):
                    hs = slice(half * HALF, (half + 1) * HALF) if b == NB - 1 else slice(0, D)
                    sp.wait_ge(h_done, 3 * NB + b + half + 1)
                    nc.sync.dma_start(out[0, b * P:(b + 1) * P, hs], h[:, b, hs]).then_inc(out_done, 16)
            sp.wait_ge(out_done, 16 * (NB + 1))

        @block.gpsimd
        def _(pool):
            nc.gpsimd.memset(raw[:, 3], 0.0).then_inc(pool_done, 1)
            nc.gpsimd.memset(ident[:], 1.0).then_inc(pool_done, 1)
            nc.gpsimd.memset(causal[:], 0.0).then_inc(pool_done, 1)
            nc.gpsimd.memset(band[:], 0.0).then_inc(pool_done, 1)
            nc.gpsimd.memset(ones[:], 1.0).then_inc(w_used, CREDIT)
            pool.wait_ge(pool_done, 4)
            nc.gpsimd.affine_select(out=ident[:], in_=ident[:], compare_op=ALU.is_equal, fill=0.0,
                                    base=0, pattern=[[-1, P]], channel_multiplier=1).then_inc(pool_done, 1)
            nc.gpsimd.affine_select(out=causal[:], in_=causal[:], compare_op=ALU.is_ge, fill=MASKED,
                                    base=0, pattern=[[1, P]], channel_multiplier=-1).then_inc(pool_done, 1)
            nc.gpsimd.affine_select(out=band[:, 0:P], in_=band[:, 0:P], compare_op=ALU.is_gt,
                                    fill=MASKED, base=0, pattern=[[1, P]],
                                    channel_multiplier=-1).then_inc(pool_done, 1)
            nc.gpsimd.affine_select(out=band[:, P:], in_=band[:, P:], compare_op=ALU.is_ge,
                                    fill=MASKED, base=0, pattern=[[-1, P]],
                                    channel_multiplier=1).then_inc(pool_done, 1)
            pool.wait_ge(vec_done, 1)
            nc.gpsimd.tensor_scalar(hn_half[:], head_norm, 0.5, None, ALU.mult).then_inc(pool_done, 1)
            pool.wait_ge(pool_done, 9)
            for n in range(O_UNITS):
                pool.wait_ge(o_tanh, n + 1)
                nc.gpsimd.tensor_scalar(o_sig[:, n], o_sig[:, n], hn_half[:, n:n + 1], hn_half[:, n:n + 1],
                                        ALU.mult, ALU.add).then_inc(o_done, 1)

        @block.scalar
        def _(act):
            chain = [0]

            def link(ins):
                chain[0] += 1
                ins.then_inc(act_chain, 1)
                act.wait_ge(act_chain, chain[0])

            def split_hi(g):
                s = SLOT[g]
                act.wait_ge(raw_in[s % 4], landed(g))
                act.wait_ge(w_used, freed(g))
                nc.scalar.copy(w_hi[:, s], raw[:, s % 4]).then_inc(w_hi_done, 1)

            def rsqrt_mean(b, ss):
                dst = stat[:, b % 2, ss + 1:ss + 2]
                link(nc.scalar.activation(dst, stat[:, b % 2, ss:ss + 1], ACT.Ln, scale=1.0 / D,
                                          bias=eps_col[:, 0:1]))
                return nc.scalar.activation(dst, dst, ACT.Exp, scale=-0.5)

            def norm_post(n, b, bank, biased=False):
                if biased:
                    act.wait_ge(yb_done, b + 1)
                    src = tmp
                else:
                    act.wait_ge(*products(n))
                    src = ps[:, bank:bank + 2].rearrange("p a f -> p (a f)")
                if n >= 2:
                    act.wait_ge(h_done, n - 1)
                link(nc.scalar.activation(zn[:, b % 2], src, ACT.Square,
                                          accum_out=stat[:, b % 2, 0:1]))
                rsqrt_mean(b, 0).then_inc(rs_post, 1)

            def norm_pre(n, b):
                if n < NB:
                    act.wait_ge(x_in[b], 16)
                    if n >= 2:
                        act.wait_ge(zn_done, n - 1)
                else:
                    act.wait_ge(h_done, n - NB + 1)
                link(nc.scalar.activation(tmp, h[:, b], ACT.Square, accum_out=stat[:, b % 2, 2:3]))
                rsqrt_mean(b, 2).then_inc(rs_pre, 1)

            def norm_hi(n, b, bank):
                act.wait_ge(zt_done, n + 1)
                nc.scalar.copy(act_hi[:, :, b * P:(b + 1) * P],
                               ps[:, bank:bank + 2].rearrange("p a (k t) -> p (a k) t", t=P))\
                    .then_inc(z_hi, 1)

            nc.scalar.preload_act_table_set(LN_EXP_SET)
            act.wait_ge(dve_chain, 1)
            norm_pre(0, 0)
            norm_pre(1, 1)
            norm_hi(0, 0, 0)
            norm_pre(2, 2)
            split_hi(G_GATE)
            norm_hi(1, 1, 2)
            norm_pre(3, 3)
            split_hi(G_QK)
            norm_hi(2, 2, 4)
            split_hi(G_QK + 1)
            norm_hi(3, 3, 6)
            for n in range(2, 4):
                split_hi(G_QK + n)

            nc.scalar.preload_act_table_set(EXP_TANH_SET)
            act.wait_ge(w_used, counted(G_GATE))
            act.wait_ge(row_ready, 1)
            link(nc.scalar.activation(rows[:, 0], ps[0:MH, 0], ACT.Tanh, scale=1.0 / GATE_CAP,
                                      bias=gate_b[0:MH, 1:2]))
            link(nc.scalar.activation(rows[:, 1], ps[32:32 + MH, 0], ACT.Tanh, scale=1.0 / GATE_CAP,
                                      bias=gate_b[32:32 + MH, 1:2]))
            link(nc.scalar.activation(rows[:, 1], rows[:, 1], ACT.Exp, scale=-GATE_CAP))
            nc.scalar.preload_act_table_set(LN_EXP_SET)
            nc.scalar.activation(rows[:, 2], rows[:, 1], ACT.Ln, scale=1.0, bias=1.0)\
                .then_inc(row_act, 1)
            nc.scalar.preload_act_table_set(EXP_TANH_SET)
            for n in range(4, QK_UNITS):
                split_hi(G_QK + n)
            act.wait_ge(row_ready, 2)
            for c in range(NB):
                cs = slice(c * P, (c + 1) * P)
                nc.scalar.activation(rows[:, 5, cs], rows[:, 4, cs], ACT.Exp,
                                     bias=u_rows[:, (c + 1) * P - 1:(c + 1) * P])
                nc.scalar.activation(rows[:, 6, cs], u_rows[:, cs], ACT.Exp,
                                     bias=decay[:, 0, c:c + 1])
            nc.scalar.activation(decay[:, 2], decay[:, 1], ACT.Exp)
            nc.scalar.activation(rows[:, 7], rows[:, 3], ACT.Exp, scale=-1.0).then_inc(row_act, 1)
            def squares(s):
                c, g = s // 2, s % 2
                act.wait_ge(num_done, s + 1)
                if s >= 1:
                    act.wait_ge(sq_done, s)
                for t in range(HG):
                    hd = 2 * t + g
                    ins = nc.scalar.activation(junk[:, t], v_tok[:, c, hd, 0:DV],
                                               ACT.Square, accum_out=s2[:, c, hd:hd + 1])
                ins.then_inc(sq_done, 1)

            for n in range(V_UNITS + 1):
                split_hi(G_V + n)
            act.wait_ge(gt_done, 1)
            def gated_hi(c, half):
                act.wait_ge(gated_done, 2 * c + half + 1)
                ks = slice(4 * half, 4 * half + 4)
                nc.scalar.copy(act_hi[:, ks, c * P:(c + 1) * P], gated[:, ks]).then_inc(op_hi, 1)

            def rms_heads(n, cols):
                act.wait_ge(fac_dve, n)
                link(nc.scalar.activation(fac[:, 1, cols], fac[:, 1, cols], ACT.Ln, scale=1.0 / DV,
                                          bias=eps_col[:, 0:1]))
                nc.scalar.activation(fac[:, 1, cols], fac[:, 1, cols], ACT.Exp, scale=-0.5)\
                    .then_inc(fac_act, 1)

            for s in range(NS):
                act.wait_ge(e_raw, s + 1)
                nc.scalar.activation(ew[:, s % 2], ew[:, s % 2], ACT.Exp).then_inc(e_exp, 1)
                if s < NS - 1:
                    split_hi(G_O + s + 1)
                else:
                    for k in range(4):
                        split_hi(G_MOUT + k)
                    squares(s - 1)
                    gated_hi(0, 0)
                if s == NS - 3:
                    nc.scalar.preload_act_table_set(LN_EXP_SET)
                    rms_heads(1, slice(0, 2 * MH))
                    nc.scalar.preload_act_table_set(EXP_TANH_SET)
                act.wait_ge(w_used, counted(G_O + s))
                nc.scalar.activation(o_sig[:, s], ps[:, 6 + s % 2], ACT.Tanh, scale=0.5)\
                    .then_inc(o_tanh, 1)
                if 1 <= s < NS - 1:
                    squares(s - 1)
            nc.scalar.preload_act_table_set(LN_EXP_SET)
            split_hi(G_MOUT + 4)
            gated_hi(0, 1)
            for k in range(5, KT):
                split_hi(G_MOUT + k)
            for half in range(2):
                gated_hi(1, half)
            squares(NS - 1)
            rms_heads(2, slice(2 * MH, NB * MH))
            for c in range(NB):
                if c >= 2:
                    norm_hi(NB + c - 2, c - 2, 4 + 2 * (c % 2))
                if c >= 1:
                    norm_post(c - 1, c - 1, 4 + 2 * ((c - 1) % 2))
                    if c == NB - 1:
                        split_hi(G_UP[0])
                if c >= 1:
                    norm_pre(NB + c - 1, c - 1)
                    if c + 1 < NB:
                        gated_hi(c + 1, 0)
                        gated_hi(c + 1, 1)
            for n in range(1, 4):
                split_hi(G_UP[0] + n)
            norm_hi(2 * NB - 2, NB - 2, 4)
            norm_post(NB - 1, NB - 1, 6)
            norm_pre(2 * NB - 1, NB - 1)
            norm_hi(2 * NB - 1, NB - 1, 6)

            def ffn(l):
                up, down = G_UP[l], G_DOWN[l]

                def hi_pair(i, t):
                    for q in range(2):
                        g = up + 2 * t + q
                        s = (2 * t + q) % 4
                        act.wait_ge(raw_in[s], i * 16 + landed(g))
                        act.wait_ge(w_used, i * 4 + counted(g - 4))
                        nc.scalar.copy(w_hi[:, 4 + s], raw[:, s]).then_inc(w_hi_done, 1)

                def conv(i, t):
                    f = i * 2 + t
                    act.wait_ge(w_used, i * 4 + counted(up + 2 * t))
                    nc.scalar.activation(cv[:, t], ps[:, 2 * t], ACT.Identity,
                                         scale=taps[l][:, 2, bass.ds(f, 1)],
                                         bias=taps[l][:, 3, bass.ds(f, 1)]).then_inc(cv0, 1)
                    act.wait_ge(cv2, i * 2 + (l * FT + t + 1))
                    nc.scalar.activation(cv[:, t], cv[:, t], ACT.Silu).then_inc(silu_done, 1)

                nc.scalar.preload_act_table(ACT.Silu)
                if l == 0:
                    act.wait_ge(vec_done, 1)
                with act.Fori(0, FT // 2 - 1) as i:
                    conv(i, 0)
                    hi_pair(i, 2)
                    conv(i, 1)
                    hi_pair(i, 3)
                for j in range(2):
                    split_hi(down + j)
                for j in range(2):
                    nc.scalar.copy(hid_pair[j][0], hid[:, j]).then_inc(hid_hi, 1)
                conv(FT // 2 - 1, 0)
                conv(FT // 2 - 1, 1)
                nc.scalar.preload_act_table_set(LN_EXP_SET)
                with act.Fori(0, (FT - TAIL) // 2 - 1) as i:
                    for j in range(2):
                        act.wait_ge(raw_in[j], i * 16 + landed(down + 2 + j))
                        act.wait_ge(w_used, i * 2 + counted(down + j))
                        nc.scalar.copy(w_hi[:, j], raw[:, j]).then_inc(w_hi_done, 1)
                        nc.scalar.copy(hid_pair[j][0], hid[:, bass.ds(i * 2 + (2 + j), 1)]
                                       .rearrange("p a t -> p (a t)")).then_inc(hid_hi, 1)
                for n in range(FT - TAIL, FT):
                    split_hi(down + n)
                    if n == FT - 1:
                        act.wait_ge(hid_done, (l + 1) * FT + 2)
                    nc.scalar.copy(act_hi[:, n - (FT - TAIL)], hid[:, n]).then_inc(hid_hi, 1)

            def ffn_norms(l):
                for b in range(NB):
                    norm_post((2 * l + 1) * NB + b, b, 2 * b)
                    if l == 0:
                        if b >= 1:
                            norm_hi(2 * NB + b - 1, b - 1, 2 * (b - 1))
                        if b == 2:
                            split_hi(G_AIN + 2)
                        norm_pre(2 * NB + b, b)
                        if b != 2:
                            split_hi(G_AIN + b)
                if l == 0:
                    norm_hi(3 * NB - 1, NB - 1, 2 * (NB - 1))

            ffn(0)
            ffn_norms(0)
            for n in range(4, A_UNITS):
                split_hi(G_AIN + n)

            def probs(s):
                b, blk = s % 2, s // ASTEPS
                lo = P if blk == 0 else 0
                act.wait_ge(mx_done, s + 1)
                for j in range(AG):
                    nc.scalar.activation(sc[:, b, j, lo:], sc[:, b, j, lo:], ACT.Exp,
                                         bias=asm[:, b, 1, j:j + 1], accum_out=asm[:, b, 2, j:j + 1])
                nc.scalar.activation(asm[:, b, 3], asm[:, b, 3], ACT.Exp).then_inc(p_done, 1)

            def turned(s):
                b, blk = s % 2, s // ASTEPS
                act.wait_ge(pt_mm, s + 1)
                lo = P if blk == 0 else 0
                nc.scalar.copy(p_t[:, b, :, lo:], ps[:, 2:4].rearrange("p a (j k) -> p (a j) k", k=2 * P)
                               [:, :, lo:]).then_inc(pt_done, 1)

            def turn_hi(b, half):
                n = turns_hi[0]
                turns_hi[0] += 1
                act.wait_ge(t_mm, n + 1)
                nc.scalar.copy(act_hi[:, 4 * half:4 * half + 4, b * P:(b + 1) * P],
                               ps[:, turn_bank(n)].rearrange("p (k t) -> p k t", t=P)).then_inc(t_hi, 1)

            turns_hi = [0]

            def work(w):
                if w[0] == "y":
                    norm_post(2 * NB + w[1], w[1], 6, biased=True)
                elif w[0] == "post":
                    norm_pre(3 * NB + w[1], w[1])
                elif w[0] == "turn":
                    turn_hi(w[2], w[3])

            probs(0)
            for s in range(AT_STEPS + 2):
                if 1 <= s <= AT_STEPS and s != ASTEPS + 1:
                    turned(s - 1)
                if s >= AT_STEPS:
                    for w in sorted(WORK[s], key=lambda w: s == AT_STEPS and w[0] == "y"):
                        work(w)
                        if w == ("post", NB - 2):
                            split_hi(G_UP[1])
                            split_hi(G_UP[1] + 1)
                        if w == ("turn", "norm", NB - 2, 1):
                            split_hi(G_UP[1] + 2)
                        if w == ("post", NB - 1):
                            split_hi(G_UP[1] + 3)
                    continue
                if s >= 1:
                    for w in WORK[s - 1]:
                        if w[0] in ("y", "post"):
                            work(w)
                for k in OUT_SPLITS.get(s, []):
                    split_hi(G_AOUT + k)
                if s == ASTEPS:
                    turned(s)
                if s + 1 < AT_STEPS:
                    probs(s + 1)
                for w in WORK[s]:
                    if w[0] == "turn":
                        work(w)

            ffn(1)
            ffn_norms(1)

        @block.vector
        def _(dve):
            chain = [0]

            def link(ins):
                chain[0] += 1
                ins.then_inc(dve_chain, 1)
                dve.wait_ge(dve_chain, chain[0])

            def split_lo(g):
                s = SLOT[g]
                dve.wait_ge(w_hi_done, g + 1)
                nc.vector.tensor_tensor(w_lo[:, s], raw[:, s % 4], w_hi[:, s].bitcast(F32),
                                        ALU.subtract).then_inc(w_lo_done, 1)

            gains_in = [0]

            def norm_post(n, b, bank, biased=False):
                y = tmp if biased else ps[:, bank:bank + 2].rearrange("p a f -> p (a f)")
                if n > 3 * NB:
                    dve.wait_ge(h_done, n)
                dve.wait_ge(rs_post, n + 1)
                if n == 4 * NB - 1:
                    for half in range(2):
                        hs = slice(half * HALF, (half + 1) * HALF)
                        link(nc.vector.scalar_tensor_tensor(tmp[:, hs], y[:, hs], stat[:, b % 2, 1:2],
                                                            g_post[:, hs], ALU.mult, ALU.mult))
                        nc.vector.tensor_tensor(h[:, b, hs], h[:, b, hs], tmp[:, hs], ALU.add)\
                            .then_inc(h_done, 1)
                    return
                link(nc.vector.scalar_tensor_tensor(tmp, y, stat[:, b % 2, 1:2], g_post[:], ALU.mult, ALU.mult))
                nc.vector.tensor_tensor(h[:, b], h[:, b], tmp, ALU.add).then_inc(h_done, 1)

            def add_bias(b):
                dve.wait_ge(*products(2 * NB + b))
                if b == 0:
                    dve.wait_ge(bout_in, 16)
                nc.vector.tensor_tensor(tmp, ps[:, 6:8].rearrange("p a f -> p (a f)"), b_out, ALU.add)\
                    .then_inc(yb_done, 1)

            def norm_pre(n, b):
                dve.wait_ge(rs_pre, n + 1)
                if n >= 2 and n < NB:
                    dve.wait_ge(zt_done, n - 1)
                nc.vector.scalar_tensor_tensor(zn[:, b % 2], h[:, b], stat[:, b % 2, 3:4], g_pre[:],
                                               ALU.mult, ALU.mult).then_inc(zn_done, 1)

            def norm_lo(n, b, bank):
                dve.wait_ge(z_hi, n + 1)
                nc.vector.tensor_tensor(act_lo[:, :, b * P:(b + 1) * P],
                                        ps[:, bank:bank + 2].rearrange("p a (k t) -> p (a k) t", t=P),
                                        act_hi[:, :, b * P:(b + 1) * P].bitcast(F32),
                                        ALU.subtract).then_inc(z_lo, 1)

            def gains(n):
                gains_in[0] += n
                dve.wait_ge(gain_in, 16 * gains_in[0])

            link(nc.vector.memset(eps_col[:], EPS))
            nc.vector.memset(zrow, 0.0).then_inc(hid_done, 2)
            nc.vector.memset(v_tok[:, :, :, DV:DV1], 1.0).then_inc(w_lo_done, CREDIT)
            link(nc.vector.memset(decay[:, 0, 0:1], 0.0))
            gains(1)
            norm_pre(0, 0)
            norm_pre(1, 1)
            norm_lo(0, 0, 0)
            norm_pre(2, 2)
            split_lo(G_GATE)
            norm_lo(1, 1, 2)
            norm_pre(3, 3)
            split_lo(G_QK)
            norm_lo(2, 2, 4)
            split_lo(G_QK + 1)
            norm_lo(3, 3, 6)
            for n in range(2, 4):
                split_lo(G_QK + n)
            dve.wait_ge(const_in, 16 * 3)
            nc.vector.tensor_scalar(gate_b[0:MH, 1:2], gate_b[0:MH, 0:1], 1.0 / GATE_CAP, None, ALU.mult)
            nc.vector.tensor_scalar(gate_b[32:32 + MH, 1:2], gate_b[32:32 + MH, 0:1], 1.0 / GATE_CAP, None,
                                    ALU.mult).then_inc(row_ready, 1)

            def copy_qk(n):
                dve.wait_ge(w_used, counted(G_QK + n))
                nc.vector.tensor_copy(qk_t[:, n], ps[:, 1 + n % 2]).then_inc(pj_used, 1)

            copy_qk(0)
            dve.wait_ge(row_act, 1)
            link(nc.vector.tensor_scalar(rows[:, 0], rows[:, 0], GATE_CAP, None, ALU.mult))
            link(nc.vector.tensor_scalar(rows[:, 1], rows[:, 2], -1.0, None, ALU.mult))
            link(nc.vector.tensor_tensor_scan(rows[:, 3], rows[:, 1], rows[:, 0], 0.0, ALU.add, ALU.max))
            for c in range(NB):
                cs = slice(c * P, (c + 1) * P)
                ins = nc.vector.tensor_tensor_scan(rows[:, 2, cs], rows[:, 1, cs], zrow[:, cs], 0.0,
                                                   ALU.add, ALU.add)
            link(ins)
            nc.vector.tensor_tensor(rows[:, 4], rows[:, 0], rows[:, 2], ALU.subtract)
            link(nc.vector.tensor_tensor(u_rows[:], rows[:, 2], rows[:, 3], ALU.subtract))
            m_c = rows[:, 3].rearrange("p (c t) -> p c t", t=P)
            u_c = u_rows[:].rearrange("p (c t) -> p c t", t=P)
            link(nc.vector.tensor_copy(decay[:, 0, 1:], m_c[:, 0:NB - 1, P - 1]))
            nc.vector.tensor_tensor(decay[:, 1], u_c[:, :, P - 1], decay[:, 0], ALU.add)\
                .then_inc(row_ready, 1)
            for n in range(1, QK_UNITS):
                if n >= 3:
                    split_lo(G_QK + n + 1)
                copy_qk(n)
                if n == 4:
                    dve.wait_ge(vec_mm, 1)
                    nc.vector.tensor_copy(vecs[:], ps[:, 3, 0:VECS]).then_inc(vec_done, 1)
            dve.wait_ge(row_act, 2)
            dve.wait_ge(pool_done, 8)
            nc.vector.tensor_tensor(dsel[:], decay[:, 2].unsqueeze(1).to_broadcast([MH, MH, NB]),
                                    ident[0:MH, 0:MH].unsqueeze(2).to_broadcast([MH, MH, NB]),
                                    ALU.mult).then_inc(dsel_done, 1)
            split_lo(G_V + 1)
            dve.wait_ge(tr_mm, 1)
            link(nc.vector.tensor_copy(gt[:].rearrange("p c q h -> p (c q h)"), ps[:, 0, 0:NB * 4 * MH]))
            dve.wait_ge(dec_mm, 1)
            link(nc.vector.tensor_copy(decay_all[:].rearrange("p h c -> p (h c)"),
                                       ps[:, 3, 0:MH * NB]))
            nc.vector.tensor_scalar(gt[:, :, 2], gt[:, :, 2], DK ** -0.5, None, ALU.mult)\
                .then_inc(gt_done, 1)

            def copy_v(half, b):
                dve.wait_ge(*values(half, b))
                nc.vector.tensor_copy(v_tok[:, b, 4 * half:4 * half + 4, 0:DV],
                                      ps[:, 4 + b].rearrange("p (h v) -> p h v", v=DV)).then_inc(v_done, 1)

            for n in range(2, V_UNITS):
                split_lo(G_V + n)
                c = n - 2
                if n == 4:
                    for b in range(NB - 1):
                        copy_v(0, b)
                if c < NB:
                    dve.wait_ge(kt_mm, c + 1)
                    nc.vector.tensor_tensor(
                        kw[:, c].rearrange("p (h d) -> p h d", h=MH),
                        ps[:, 1 + c % 2].rearrange("p (h d) -> p h d", h=MH),
                        gt[:, c, 1].unsqueeze(2).to_broadcast([P, MH, DK]), ALU.mult)\
                        .then_inc(kw_done, 1)
                if n == 4:
                    copy_v(0, NB - 1)
            dve.wait_ge(gt_done, 1)
            for b in range(NB):
                if b == 1:
                    split_lo(G_O)
                copy_v(1, b)

            def weights(s):
                c, g = s // 2, s % 2
                dve.wait_ge(u_mm, s + 1)
                for t in range(HG):
                    hd = 2 * t + g
                    ins = nc.vector.scalar_tensor_tensor(
                        ew[:, s % 2, t], ps[:, 0, t * P:(t + 1) * P], gt[:, c, 0, hd:hd + 1], causal[:],
                        ALU.add, ALU.min)
                ins.then_inc(e_raw, 1)

            def weigh(s):
                dve.wait_ge(e_exp, s + 1)
                dve.wait_ge(st_mm, s + 1)
                nc.vector.scalar_tensor_tensor(
                    ew[:, s % 2].rearrange("p t q -> p (t q)"), ps[:, 1], DK ** -0.5,
                    ew[:, s % 2].rearrange("p t q -> p (t q)"), ALU.mult, ALU.mult).then_inc(w_done, 1)

            def state(s):
                c, g = s // 2, s % 2
                if c == NB - 1:
                    return
                pr = slice(g * DK, (g + 1) * DK)
                dve.wait_ge(n_mm, s + 1)
                news = heads(4, 2, pr)
                if c == 0:
                    for ts, new in news:
                        ins = nc.vector.tensor_copy(C[pr, ts], new)
                else:
                    dec = decay_all[pr, g::2, c].unsqueeze(2).to_broadcast([DK, HG, DV1])
                    link(nc.vector.tensor_tensor(C[pr], C[pr], dec, ALU.mult))
                    for ts, new in news:
                        ins = nc.vector.tensor_tensor(C[pr, ts], C[pr, ts], new, ALU.add)
                ins.then_inc(c_done, 1)

            def outputs(s):
                c, g = s // 2, s % 2
                dve.wait_ge(n_mm, s + 1)
                out = v_tok[:, c].rearrange("p (t two) v -> p t two v", two=2)[:, :, g]
                if c > 0:
                    s_inter = gt[:, c, 2, g::2]
                    for ts, inter in heads(3, 1):
                        n = ts.stop - ts.start
                        ins = nc.vector.tensor_tensor(
                            itmp[:, ts], inter, s_inter[:, ts].unsqueeze(2).to_broadcast([P, n, DV1]),
                            ALU.mult)
                    link(ins)
                for ts, intra in heads(2, 0):
                    if c > 0:
                        ins = nc.vector.tensor_tensor(out[:, ts], intra, itmp[:, ts], ALU.add)
                    else:
                        ins = nc.vector.tensor_copy(out[:, ts], intra)
                ins.then_inc(num_done, 1)
                dve.wait_ge(num_done, s + 1)
                den = out[:, :, DV]
                link(nc.vector.scalar_tensor_tensor(dtmp[:], den, -1.0, den, ALU.mult, ALU.max))
                link(nc.vector.tensor_tensor(dm[:, c, g::2], dtmp[:], gt[:, c, 3, g::2], ALU.max))

            def head_factors(c0, c1):
                cols = slice(c0 * MH, c1 * MH)
                dve.wait_ge(sq_done, 2 * c1)
                link(nc.vector.reciprocal(fac[:, 0, cols], dm[:, c0:c1].rearrange("p c h -> p (c h)")))
                link(nc.vector.tensor_tensor(fac[:, 2, cols], fac[:, 0, cols], fac[:, 0, cols], ALU.mult))
                nc.vector.tensor_tensor(fac[:, 1, cols], fac[:, 2, cols],
                                        s2[:, c0:c1].rearrange("p c h -> p (c h)"),
                                        ALU.mult).then_inc(fac_dve, 1)

            def finish_factors(n, c0, c1):
                cols = slice(c0 * MH, c1 * MH)
                dve.wait_ge(fac_act, n)
                link(nc.vector.tensor_tensor(fac[:, 0, cols], fac[:, 0, cols], fac[:, 1, cols], ALU.mult))

            def scale_heads(c):
                hv = v_tok[:, c, :, 0:DV]
                f = fac[:, 0, c * MH:(c + 1) * MH].unsqueeze(2).to_broadcast([P, MH, DV])
                nc.vector.tensor_tensor(hv, hv, f, ALU.mult).then_inc(hs_done, 1)

            def gate_heads(c, half):
                dve.wait_ge(ht_mm, c + 1)
                dve.wait_ge(o_done, 4 * half + 4)
                ks = slice(4 * half, 4 * half + 4)
                if c >= 1:
                    dve.wait_ge(op_lo, 2 * c - 1 + half)
                nc.vector.tensor_tensor(gated[:, ks], ps[:, 2 * (c % 2) + half]
                                        .rearrange("p (k t) -> p k t", t=P),
                                        o_sig[:, ks, c * P:(c + 1) * P], ALU.mult).then_inc(gated_done, 1)

            def gated_lo(c, half):
                dve.wait_ge(op_hi, 2 * c + half + 1)
                ks = slice(4 * half, 4 * half + 4)
                nc.vector.tensor_tensor(act_lo[:, ks, c * P:(c + 1) * P], gated[:, ks],
                                        act_hi[:, ks, c * P:(c + 1) * P].bitcast(F32), ALU.subtract)\
                    .then_inc(op_lo, 1)

            for s in range(NS):
                if s >= 1:
                    outputs(s - 1)
                    state(s - 1)
                weights(s)
                weigh(s)
                if s + 1 < NS:
                    split_lo(G_O + s + 1)
                if s == NS - 3:
                    head_factors(0, 2)
                if s == NS - 2:
                    finish_factors(1, 0, 2)
                    scale_heads(0)
                    scale_heads(1)
            split_lo(G_MOUT)
            outputs(NS - 1)
            gate_heads(0, 0)
            split_lo(G_MOUT + 1)
            gated_lo(0, 0)
            for k in range(2, 4):
                split_lo(G_MOUT + k)
            gate_heads(0, 1)
            split_lo(G_MOUT + 4)
            gated_lo(0, 1)
            for k in range(5, KT):
                split_lo(G_MOUT + k)
            for half in range(2):
                gate_heads(1, half)
            for half in range(2):
                gated_lo(1, half)
            head_factors(2, NB)
            finish_factors(2, 2, NB)
            for c in range(NB):
                if c >= 2:
                    norm_lo(NB + c - 2, c - 2, 4 + 2 * (c % 2))
                if c == 0:
                    gains(2)
                else:
                    norm_post(c - 1, c - 1, 4 + 2 * ((c - 1) % 2))
                    if c == NB - 1:
                        split_lo(G_UP[0])
                if 1 <= c < NB - 1:
                    gate_heads(c + 1, 0)
                    gate_heads(c + 1, 1)
                if c >= 1:
                    norm_pre(NB + c - 1, c - 1)
                if c + 2 < NB:
                    scale_heads(c + 2)
                if 1 <= c < NB - 1:
                    gated_lo(c + 1, 0)
                    gated_lo(c + 1, 1)
            for n in range(1, 4):
                split_lo(G_UP[0] + n)
            norm_lo(2 * NB - 2, NB - 2, 4)
            norm_post(NB - 1, NB - 1, 6)
            norm_pre(2 * NB - 1, NB - 1)
            norm_lo(2 * NB - 1, NB - 1, 6)

            def ffn(l):
                up, down = G_UP[l], G_DOWN[l]

                def lo_pair(i, t):
                    for q in range(2):
                        s = (2 * t + q) % 4
                        dve.wait_ge(w_hi_done, i * 4 + (up + 2 * t + q + 1))
                        nc.vector.tensor_tensor(w_lo[:, 4 + s], raw[:, s], w_hi[:, 4 + s].bitcast(F32),
                                                ALU.subtract).then_inc(w_lo_done, 1)

                def conv(i, t):
                    f = i * 2 + t
                    n = l * FT + t + 1
                    dve.wait_ge(cv0, i * 2 + n)
                    nc.vector.scalar_tensor_tensor(cv[:, t, 1:], ps[:, 2 * t, 0:S - 1],
                                                   taps[l][:, 1, bass.ds(f, 1)], cv[:, t, 1:],
                                                   ALU.mult, ALU.add).then_inc(cv1, 1)
                    dve.wait_ge(cv1, i * 2 + n)
                    nc.vector.scalar_tensor_tensor(cv[:, t, 2:], ps[:, 2 * t, 0:S - 2],
                                                   taps[l][:, 0, bass.ds(f, 1)], cv[:, t, 2:],
                                                   ALU.mult, ALU.add).then_inc(cv2, 1)
                    dve.wait_ge(silu_done, i * 2 + n)
                    dve.wait_ge(w_used, i * 4 + counted(up + 2 * t + 1))
                    nc.vector.tensor_tensor(hid[:, bass.ds(f, 1)].rearrange("p a t -> p (a t)"),
                                            ps[:, 2 * t + 1], cv[:, t], ALU.mult).then_inc(hid_done, 1)

                with dve.Fori(0, FT // 2 - 1) as i:
                    conv(i, 0)
                    lo_pair(i, 2)
                    conv(i, 1)
                    lo_pair(i, 3)

                def lo_hid(n):
                    dve.wait_ge(hid_hi, l * FT + n + 1)
                    j = n - (FT - TAIL)
                    hi, lo = (act_hi[:, j], act_lo[:, j]) if j >= 0 else hid_pair[n]
                    nc.vector.tensor_tensor(lo, hid[:, n], hi.bitcast(F32),
                                            ALU.subtract).then_inc(hid_lo, 1)

                for j in range(2):
                    split_lo(down + j)
                for j in range(2):
                    lo_hid(j)
                conv(FT // 2 - 1, 0)
                conv(FT // 2 - 1, 1)
                with dve.Fori(0, (FT - TAIL) // 2 - 1) as i:
                    for j in range(2):
                        dve.wait_ge(w_hi_done, i * 2 + (down + 2 + j + 1))
                        nc.vector.tensor_tensor(w_lo[:, j], raw[:, j], w_hi[:, j].bitcast(F32),
                                                ALU.subtract).then_inc(w_lo_done, 1)
                        dve.wait_ge(hid_hi, i * 2 + (l * FT + 2 + j + 1))
                        nc.vector.tensor_tensor(hid_pair[j][1], hid[:, bass.ds(i * 2 + (2 + j), 1)]
                                                .rearrange("p a t -> p (a t)"),
                                                hid_pair[j][0].bitcast(F32),
                                                ALU.subtract).then_inc(hid_lo, 1)
                for n in range(FT - TAIL, FT):
                    split_lo(down + n)
                    lo_hid(n)

            def ffn_norms(l):
                gains(2 if l == 0 else 1)
                for b in range(NB):
                    norm_post((2 * l + 1) * NB + b, b, 2 * b)
                    if l == 0:
                        if b == NB - 1:
                            split_lo(G_AIN + 2)
                        if b >= 1:
                            norm_lo(2 * NB + b - 1, b - 1, 2 * (b - 1))
                        norm_pre(2 * NB + b, b)
                        if b != 2:
                            split_lo(G_AIN + b)
                if l == 0:
                    norm_lo(3 * NB - 1, NB - 1, 2 * (NB - 1))

            ffn(0)
            ffn_norms(0)

            def add_a_bias(n, part=0, lo=0, hi=S):
                if n >= 6 and part == 0:
                    dve.wait_ge(qb_mm, n - 5)
                else:
                    dve.wait_ge(w_used, counted(G_AIN + n))
                t = A_TILE[n]
                dst = [*[q_t[:, m] for m in range(KT)], k_t, v_t][t]
                nc.vector.tensor_scalar(dst[:, lo:hi], ps[:, a_bank(n), lo:hi],
                                        a_bias[:, t:t + 1], None, ALU.add).then_inc(pj_used, 1)

            for n in range(6):
                if n >= 3:
                    split_lo(G_AIN + n + 1)
                add_a_bias(n)

            def sink_cols(s):
                n = GROUPS[s % ASTEPS]
                return sink[:, n * AG:(n + 1) * AG]

            def masked_max(s):
                b, blk = s % 2, s // ASTEPS
                lo = P if blk == 0 else 0
                dve.wait_ge(s_mm, s + 1)
                if s >= 2:
                    dve.wait_ge(pt_mm, s - 1)
                for j in range(AG):
                    ins = nc.vector.tensor_tensor_reduce(
                        out=sc[:, b, j, lo:], in0=ps[:, j // 2, (j % 2) * 2 * P + lo:(j % 2 + 1) * 2 * P],
                        in1=band[:, lo:], scale=DH ** -0.5, scalar=sink_cols(s)[:, j:j + 1],
                        op0=ALU.add, op1=ALU.max, accum_out=asm[:, b, 0, j:j + 1])
                link(ins)
                nc.vector.tensor_tensor(asm[:, b, 3], sink_cols(s), asm[:, b, 0], ALU.subtract)
                nc.vector.tensor_scalar(asm[:, b, 1], asm[:, b, 0], -1.0, None, ALU.mult)\
                    .then_inc(mx_done, 1)

            def inverse(s):
                b = s % 2
                dve.wait_ge(p_done, s + 1)
                link(nc.vector.tensor_tensor(asm[:, b, 4], asm[:, b, 2], asm[:, b, 3], ALU.add))
                nc.vector.reciprocal(asm[:, b, 5], asm[:, b, 4]).then_inc(inv_done, 1)

            def normalised(s):
                b, blk, n = s % 2, s // ASTEPS, GROUPS[s % ASTEPS]
                dve.wait_ge(pv_mm, s + 1)
                dve.wait_ge(inv_done, s + 1)
                if n == 0 and blk >= 2:
                    dve.wait_ge(t_mm, turn_of("out", blk - 2, 1) + 1)
                o = o_tok[:, blk % 2].rearrange("p (h d) -> p h d", d=DH)[:, n * AG:(n + 1) * AG]
                nc.vector.tensor_tensor(
                    o, ps[:, 4, 0:AG * DH].rearrange("p (j d) -> p j d", j=AG),
                    asm[:, b, 5].unsqueeze(2).to_broadcast([P, AG, DH]), ALU.mult).then_inc(o_tok_done, 1)

            def turn_lo(b, half):
                n = turns_lo[0]
                turns_lo[0] += 1
                dve.wait_ge(t_hi, n + 1)
                at = (slice(None), slice(4 * half, 4 * half + 4), slice(b * P, (b + 1) * P))
                nc.vector.tensor_tensor(act_lo[at], ps[:, turn_bank(n)].rearrange("p (k t) -> p k t", t=P),
                                        act_hi[at].bitcast(F32), ALU.subtract).then_inc(t_lo, 1)

            turns_lo = [0]
            split_lo(G_AIN + 7)
            masked_max(0)
            for n in range(6, A_UNITS):
                if n < 8:
                    split_lo(G_AIN + n + 2)
                add_a_bias(n, 0, 0, S // 2)
            dve.wait_ge(va_mm, 1)
            nc.vector.tensor_copy(va[:].rearrange("p c f -> p (c f)"), ps[:, 4]).then_inc(va_done, 1)
            for s in range(AT_STEPS + 2):
                if s < AT_STEPS:
                    inverse(s)
                if s + 1 < AT_STEPS:
                    masked_max(s + 1)
                if 1 <= s <= AT_STEPS:
                    normalised(s - 1)
                for k in OUT_SPLITS.get(s, []):
                    split_lo(G_AOUT + k)
                if s < 4:
                    add_a_bias(6 + s, 1, S // 2, S)
                if s == 1:
                    gains(2)
                for w in WORK[s]:
                    if w == ("pre", NB - 2):
                        split_lo(G_UP[1])
                    if w == ("turn", "norm", NB - 2, 0):
                        split_lo(G_UP[1] + 1)
                    if w == ("post", NB - 1):
                        split_lo(G_UP[1] + 2)
                    if w[0] == "turn":
                        turn_lo(w[2], w[3])
                    elif w[0] == "y":
                        add_bias(w[1])
                    elif w[0] == "post":
                        norm_post(2 * NB + w[1], w[1], 6, biased=True)
                    elif w[0] == "pre":
                        norm_pre(3 * NB + w[1], w[1])
                    if w == ("pre", NB - 1):
                        split_lo(G_UP[1] + 3)

            ffn(1)
            ffn_norms(1)

        @block.tensor
        def _(pe):
            def three(dst, pairs):
                n = len(pairs)
                for i, (lh, ll, rh, rl) in enumerate(pairs):
                    nc.tensor.matmul(dst, lh, rh, start=(i == 0), stop=False)
                    nc.tensor.matmul(dst, lh, rl, start=False, stop=False)
                    last = nc.tensor.matmul(dst, ll, rh, start=False, stop=(i == n - 1))
                return last

            def project(slot, bank, lo=0, hi=S):
                uh, ul = unit(slot)
                return three(ps[:, bank, lo:hi],
                             [(uh[:, k], ul[:, k], act_hi[:, k, lo:hi], act_lo[:, k, lo:hi])
                              for k in range(KT)])

            def turn_norm(n, b, bank):
                pe.wait_ge(zn_done, n + 1)
                for k in range(KT):
                    ins = nc.tensor.transpose(ps[:, bank + k // 4, (k % 4) * P:(k % 4 + 1) * P],
                                              zn[:, b % 2, k * P:(k + 1) * P], ident[:])
                ins.then_inc(zt_done, 1)

            pe.wait_ge(pool_done, 8)
            turn_norm(0, 0, 0)
            turn_norm(1, 1, 2)

            def gate_or_qk(g, lo, hi):
                pe.wait_ge(z_lo, hi // P)
                pe.wait_ge(w_lo_done, counted(g))
                n = g - G_QK
                if n >= 2:
                    pe.wait_ge(pj_used, n - 1)
                ins = project(SLOT[g], 0 if g == G_GATE else 1 + n % 2, lo, hi)
                if hi == S:
                    ins.then_inc(w_used, 1)

            turn_norm(2, 2, 4)
            gate_or_qk(G_GATE, 0, 2 * P)
            turn_norm(3, 3, 6)
            gate_or_qk(G_QK, 0, 2 * P)
            gate_or_qk(G_GATE, 2 * P, S)
            gate_or_qk(G_QK, 2 * P, S)
            for n in range(1, QK_UNITS):
                gate_or_qk(G_QK + n, 0, S)
                if n == 4:
                    pe.wait_ge(vec_in, 16 * (6 + KVH))
                    for r, q in enumerate((4 * FT, 4 * FT, MH + A_UNITS)):
                        ins = nc.tensor.transpose(ps[:, 3, r * 4 * FT:r * 4 * FT + q], vec_rows[0:q, r],
                                                  ident[0:q, 0:q])
                    ins.then_inc(vec_mm, 1)

            def v_unit(n):
                g, half, kp = G_V + n, n // 4, n % 4
                s = SLOT[g]
                pe.wait_ge(w_lo_done, counted(g))
                for b in range(NB):
                    if half == 1 and kp == 0:
                        pe.wait_ge(v_done, b + 1)
                    bs = slice(b * P, (b + 1) * P)
                    for j in range(2):
                        k = 2 * kp + j
                        wh = w_hi[:, s, j * HALF:(j + 1) * HALF]
                        wl = w_lo[:, s, j * HALF:(j + 1) * HALF]
                        nc.tensor.matmul(ps[:, 4 + b], act_hi[:, k, bs], wh, start=(k == 0), stop=False)
                        nc.tensor.matmul(ps[:, 4 + b], act_hi[:, k, bs], wl, start=False, stop=False)
                        ins = nc.tensor.matmul(ps[:, 4 + b], act_lo[:, k, bs], wh, start=False,
                                               stop=(k == KT - 1))
                    if kp == 3 and b < NB - 1:
                        ins.then_inc(v_mm, 1)
                ins.then_inc(w_used, 1)

            v_unit(0)
            pe.wait_ge(row_act, 2)
            for c in range(NB):
                for q in range(4):
                    o0 = (c * 4 + q) * MH
                    ins = nc.tensor.transpose(ps[:, 0, o0:o0 + MH], rows[:, 4 + q, c * P:(c + 1) * P],
                                              ident[0:MH, 0:MH])
            ins.then_inc(tr_mm, 1)
            pe.wait_ge(dsel_done, 1)
            nc.tensor.matmul(ps[:, 3, 0:MH * NB], ones[0:MH, 0:1].to_broadcast([MH, P]), dsel[:].rearrange("p h c -> p (h c)"),
                             start=True, stop=True).then_inc(dec_mm, 1)
            v_unit(1)
            for n in range(2, V_UNITS):
                c = n - 2
                if c < NB:
                    if c >= 2:
                        pe.wait_ge(kw_done, c - 1)
                    else:
                        pe.wait_ge(pj_used, QK_UNITS)
                    for t in range(HG):
                        ins = nc.tensor.transpose(ps[:, 1 + c % 2, t * P:(t + 1) * P],
                                                  qk_t[:, HG + t, c * P:(c + 1) * P], ident[:])
                    ins.then_inc(kt_mm, 1)
                v_unit(n)

            def decays(s):
                c, g = s // 2, s % 2
                cs = slice(c * P, (c + 1) * P)
                if s >= 1:
                    pe.wait_ge(w_done, s)
                for t in range(HG):
                    hd = 2 * t + g
                    ins = nc.tensor.matmul(ps[:, 0, t * P:(t + 1) * P],
                                           ident[0:MH, hd:hd + 1].to_broadcast([MH, P]),
                                           u_rows[:, cs], start=True, stop=True)
                ins.then_inc(u_mm, 1)
                pr = slice(g * DK, (g + 1) * DK)
                for t in range(HG):
                    ins = nc.tensor.matmul(ps[:, 1, t * P:(t + 1) * P], qk_t[pr, HG + t, cs],
                                           qk_t[pr, t, cs], start=True, stop=True)
                ins.then_inc(st_mm, 1)

            def combine(s):
                c, g = s // 2, s % 2
                cs = slice(c * P, (c + 1) * P)
                pr = slice(g * DK, (g + 1) * DK)
                if s >= 1:
                    pe.wait_ge(num_done, s)
                    k = min(s, NS - 2)
                    pe.wait_ge(c_done, k)
                if c > 0:
                    for t in range(HG):
                        nc.tensor.matmul(head(3, 1, t), qk_t[pr, t, cs], C[pr, t], start=True, stop=True)
                if c < NB - 1:
                    for t in range(HG):
                        hd = 2 * t + g
                        nc.tensor.matmul(head(4, 2, t, pr), kw[:, c, hd * DK:(hd + 1) * DK],
                                         v_tok[:, c, hd], start=True, stop=True)
                pe.wait_ge(w_done, s + 1)
                for t in range(HG):
                    ins = nc.tensor.matmul(head(2, 0, t), ew[:, s % 2, t], v_tok[:, c, 2 * t + g],
                                           start=True, stop=True)
                ins.then_inc(n_mm, 1)

            def turn_heads(c):
                bank = 2 * (c % 2)
                pe.wait_ge(hs_done, c + 1)
                if c == 1:
                    pe.wait_ge(num_done, NS)
                if c >= 2:
                    pe.wait_ge(gated_done, 2 * (c - 1))
                for k in range(KT):
                    ins = nc.tensor.transpose(ps[:, bank + k // 4, (k % 4) * P:(k % 4 + 1) * P],
                                              v_tok[:, c, k, 0:DV], ident[:])
                ins.then_inc(ht_mm, 1)

            pe.wait_ge(kw_done, NB)
            pe.wait_ge(gt_done, 1)
            decays(0)
            pe.wait_ge(v_done, 2 * NB)
            for s in range(NS):
                g = G_O + s
                pe.wait_ge(w_lo_done, counted(g))
                if s >= 2:
                    pe.wait_ge(o_tanh, s - 1)
                if s < NS - 1:
                    project(SLOT[g], 6 + s % 2).then_inc(w_used, 1)
                    combine(s)
                    decays(s + 1)
                else:
                    project(SLOT[g], 6 + s % 2, 0, S // 2)
                    combine(s)
                    turn_heads(0)
                    project(SLOT[g], 6 + s % 2, S // 2, S).then_inc(w_used, 1)

            def out_part(c, bank, g0, ks, last):
                cs = slice(c * P, (c + 1) * P)
                for k in ks:
                    s = SLOT[g0 + k]
                    for half in range(2):
                        hs = slice(half * HALF, (half + 1) * HALF)
                        dst = ps[:, bank + half]
                        nc.tensor.matmul(dst, act_hi[:, k, cs], w_hi[:, s, hs], start=(k == 0), stop=False)
                        nc.tensor.matmul(dst, act_hi[:, k, cs], w_lo[:, s, hs], start=False, stop=False)
                        ins = nc.tensor.matmul(dst, act_lo[:, k, cs], w_hi[:, s, hs], start=False,
                                               stop=(k == KT - 1))
                    if last:
                        ins.then_inc(w_used, 1)
                if not last and k == KT - 1:
                    ins.then_inc(y_done, 1)

            def out_block(c, bank, ks):
                for k in ks:
                    pe.wait_ge(op_lo, 2 * c + k // 4 + 1)
                    pe.wait_ge(w_lo_done, counted(G_MOUT + k))
                    out_part(c, bank, G_MOUT, [k], c == NB - 1)

            for c in range(NB):
                if c == 0:
                    turn_heads(1)
                if c >= 2:
                    pe.wait_ge(z_lo, NB + c - 1)
                bank = 4 + 2 * (c % 2)
                out_block(c, bank, range(3))
                if 1 <= c < NB - 1:
                    turn_heads(c + 1)
                out_block(c, bank, range(3, 6))
                if c >= 1:
                    turn_norm(NB + c - 1, c - 1, 10 - bank)
                out_block(c, bank, range(6, KT))

            def ffn(l, blocks_done, turn_last):
                up, down = G_UP[l], G_DOWN[l]
                blocks_done(NB // 2)
                for n in range(4):
                    pe.wait_ge(w_lo_done, counted(up + n))
                    project(4 + n, n, 0, S // 2)
                    if n == 2:
                        turn_last()
                blocks_done(NB)
                for n in range(4):
                    project(4 + n, n, S // 2, S).then_inc(w_used, 1)
                with pe.Fori(1, FT // 2) as i:
                    for t in range(2):
                        pe.wait_ge(hid_done, i * 2 + (l * FT + t + 1))
                        pe.wait_ge(w_lo_done, i * 4 + counted(up + 2 * t))
                        project(4 + 2 * t, 2 * t).then_inc(w_used, 1)
                        pe.wait_ge(w_lo_done, i * 4 + counted(up + 2 * t + 1))
                        project(5 + 2 * t, 2 * t + 1).then_inc(w_used, 1)

                def down_part(s, pair, b, half, start, stop):
                    bs = slice(b * P, (b + 1) * P)
                    hs = slice(half * HALF, (half + 1) * HALF)
                    dst = ps[:, 2 * b + half]
                    hi, lo = pair
                    nc.tensor.matmul(dst, hi[:, bs], w_hi[:, s, hs], start=start, stop=False)
                    nc.tensor.matmul(dst, hi[:, bs], w_lo[:, s, hs], start=False, stop=False)
                    return nc.tensor.matmul(dst, lo[:, bs], w_hi[:, s, hs], start=False, stop=stop)

                for j in range(2):
                    pe.wait_ge(w_lo_done, counted(down + j))
                    pe.wait_ge(hid_lo, l * FT + j + 1)
                    for b in (2, 3, 0, 1):
                        if j == 0 and b < 2:
                            pe.wait_ge(hid_done, (l + 1) * FT + 1 + b)
                        for half in range(2):
                            ins = down_part(j, hid_pair[j], b, half, j == 0, False)
                    ins.then_inc(w_used, 1)
                with pe.Fori(0, (FT - TAIL) // 2 - 1) as i:
                    for j in range(2):
                        pe.wait_ge(w_lo_done, i * 2 + counted(down + 2 + j))
                        pe.wait_ge(hid_lo, i * 2 + (l * FT + 2 + j + 1))
                        for b in range(NB):
                            for half in range(2):
                                ins = down_part(j, hid_pair[j], b, half, False, False)
                        ins.then_inc(w_used, 1)
                for b in range(NB):
                    for s in range(TAIL):
                        if b == 0:
                            n = FT - TAIL + s
                            pe.wait_ge(w_lo_done, counted(down + n))
                            pe.wait_ge(hid_lo, l * FT + n + 1)
                        for half in range(2):
                            ins = down_part(4 + s, (act_hi[:, s], act_lo[:, s]), b, half, False,
                                            s == TAIL - 1)
                        if b == NB - 1:
                            ins.then_inc(w_used, 1)
                        if s == 1 and b >= 2 and l == 0:
                            turn_norm(2 * NB + b - 2, b - 2, 2 * (b - 2))
                    if b < NB - 1:
                        ins.then_inc(y_done, 1)

            def norm_blocks(n):
                pe.wait_ge(z_lo, NB + n)

            ffn(0, norm_blocks, lambda: turn_norm(2 * NB - 1, NB - 1, 6))

            for n, lo, hi in [(n, 0, S // 2) for n in range(4)] + [(n, S // 2, S) for n in range(4)] \
                    + [(n, 0, S) for n in range(4, 6)]:
                g = G_AIN + n
                pe.wait_ge(z_lo, 2 * NB + hi // P)
                pe.wait_ge(w_lo_done, counted(g))
                if n >= 4:
                    pe.wait_ge(pj_used, QK_UNITS + n - 1)
                ins = project(SLOT[g], a_bank(n), lo, hi)
                if hi == S:
                    ins.then_inc(w_used, 1)
                elif n in (0, 2):
                    b = 2 + n // 2
                    turn_norm(2 * NB + b, b, 2 * b)

            def turn_values():
                pe.wait_ge(pj_used, QK_UNITS + 6)
                for c in range(NB):
                    ins = nc.tensor.transpose(ps[:, 4, c * P:(c + 1) * P], v_t[:, c * P:(c + 1) * P],
                                              ident[:])
                ins.then_inc(va_mm, 1)

            def scores(s):
                blk, n = s // ASTEPS, GROUPS[s % ASTEPS]
                g = n * AG // KT
                pr = slice(g * DH, (g + 1) * DH)
                if s >= 1:
                    pe.wait_ge(mx_done, s)
                pe.wait_ge(pj_used, QK_UNITS + (5 if s < 2 else A_UNITS if s < 6 else A_UNITS + 4))
                lo = P if blk == 0 else 0
                for j in range(AG):
                    t = (n * AG + j) % KT
                    dst = ps[:, j // 2, (j % 2) * 2 * P + lo:(j % 2 + 1) * 2 * P]
                    ins = nc.tensor.matmul(dst, q_t[pr, t, blk * P:(blk + 1) * P],
                                           k_t[pr, (blk - 1) * P + lo:(blk + 1) * P], start=True, stop=True)
                ins.then_inc(s_mm, 1)

            def turn_probs(s):
                b, blk = s % 2, s // ASTEPS
                pe.wait_ge(p_done, s + 1)
                if s >= 1:
                    pe.wait_ge(pt_done, s)
                for j in range(AG):
                    for kb in range(1 if blk == 0 else 0, 2):
                        ins = nc.tensor.transpose(ps[:, 2 + j // 2, ((j % 2) * 2 + kb) * P:
                                                     ((j % 2) * 2 + kb + 1) * P],
                                                  sc[:, b, j, kb * P:(kb + 1) * P], ident[:])
                ins.then_inc(pt_mm, 1)

            def mix(s):
                b, blk, n = s % 2, s // ASTEPS, GROUPS[s % ASTEPS]
                g = n * AG // KT
                pe.wait_ge(pt_done, s + 1)
                if s >= 1:
                    pe.wait_ge(o_tok_done, s)
                else:
                    pe.wait_ge(va_done, 1)
                for j in range(AG):
                    for kb in range(1 if blk == 0 else 0, 2):
                        ins = nc.tensor.matmul(ps[:, 4, j * DH:(j + 1) * DH],
                                               p_t[:, b, j, kb * P:(kb + 1) * P],
                                               va[:, blk - 1 + kb, g * DH:(g + 1) * DH],
                                               start=(kb == 0 or blk == 0), stop=(kb == 1))
                ins.then_inc(pv_mm, 1)

            def turn(what, b, half):
                n = turn_of(what, b, half)
                if what == "out":
                    pe.wait_ge(o_tok_done, (b + 1) * ASTEPS)
                else:
                    pe.wait_ge(zn_done, 3 * NB + b + 1)
                free = [q for q in range(n) if turn_bank(q) == turn_bank(n)]
                if free:
                    pe.wait_ge(t_lo, free[-1] + 1)
                src = o_tok[:, b % 2] if what == "out" else zn[:, b % 2]
                for k in range(4):
                    ins = nc.tensor.transpose(ps[:, turn_bank(n), k * P:(k + 1) * P],
                                              src[:, (4 * half + k) * P:(4 * half + k + 1) * P], ident[:])
                ins.then_inc(t_mm, 1)

            scores(0)
            for n in range(6, A_UNITS):
                pe.wait_ge(w_lo_done, counted(G_AIN + n))
                if n == 9:
                    pe.wait_ge(pj_used, QK_UNITS + 7)
                project(SLOT[G_AIN + n], a_bank(n), 0, S // 2).then_inc(qb_mm, 1)
            turn_values()
            for s in range(AT_STEPS + 2):
                if s + 1 < AT_STEPS:
                    scores(s + 1)
                mix_first = s < AT_STEPS - 1
                if 1 <= s and mix_first:
                    mix(s - 1)
                if s == ASTEPS:
                    turn_probs(s)
                for w in WORK[s]:
                    if w[0] == "turn" and w not in LAST:
                        turn(*w[1:])
                    if w[0] == "out":
                        b, q = w[1], w[2]
                        pe.wait_ge(t_lo, turn_of("out", b, q // 2) + 1)
                        if b == 0:
                            pe.wait_ge(w_lo_done, counted(G_AOUT + 2 * q + 1))
                        if q == 0:
                            if b == 0:
                                pe.wait_ge(pj_used, QK_UNITS + A_UNITS + 4)
                            else:
                                pe.wait_ge(yb_done, b)
                        for k in range(2 * q, 2 * q + 2):
                            out_part(b, 6, G_AOUT, [k], b == NB - 1)
                            if k == 2 * q + (s < AT_STEPS) and s <= AT_STEPS and not mix_first:
                                mix(s - 1)
                if s < 4:
                    pe.wait_ge(pj_used, QK_UNITS + A_UNITS + s // 3)
                    project(SLOT[G_AIN + 6 + s], a_bank(6 + s), S // 2, S).then_inc(w_used, 1)
                if s < AT_STEPS and s != ASTEPS:
                    turn_probs(s)

            def turned_blocks(n):
                pe.wait_ge(t_lo, len(TURNS) - 2 * (NB - n))

            ffn(1, turned_blocks, lambda: [turn(*w[1:]) for w in LAST])


_INS = ["x", "m_w_in", "m_gate_bias", "m_head_norm", "m_w_out", "a_w_in", "a_b_in", "a_sinks",
        "a_w_out", "a_b_out", "norm_mix_pre", "norm_mix_post", "norm_ffn_pre", "norm_ffn_post",
        "f_w_up", "f_conv_w", "f_conv_b", "f_w_down"]


def kernel(**inputs):
    import numpy as np
    import concourse.bacc as bacc
    from concourse.bass_utils import run_bass_kernel_spmd

    nc = bacc.Bacc("TRN2", target_bir_lowering=False, num_devices=1)
    arrays, args = {}, []
    for name in _INS:
        a = np.ascontiguousarray(inputs[name])
        arrays[f"in_{name}"] = a
        args.append(nc.dram_tensor(f"in_{name}", a.shape, mybir.dt.from_np(a.dtype),
                                   kind="ExternalInput").ap())
    shape = inputs["x"].shape
    out = nc.dram_tensor("out", shape, F32, kind="ExternalOutput").ap()
    trunk(nc, *args, out)
    r = run_bass_kernel_spmd(nc, [arrays], core_ids=[0])
    return r.results[0]["out"]
```
